# Optimizing a Trainium2 kernel written in Bass

```python
import math
import jax
import jax.numpy as jnp
from jax import lax
import numpy as np

D_MODEL = 1024
BATCH = 1
SEQ = 256
DEPTH = 1

GRID_W = 64
CTX_LEN = 256

HEAD_DIM = 64
N_Q_HEADS = 8
N_KV_HEADS = 2
Q_GROUP = N_Q_HEADS // N_KV_HEADS
ATT_Q_W = N_Q_HEADS * HEAD_DIM
ATT_KV_W = N_KV_HEADS * HEAD_DIM
Q_BLOCK = 128
ROPE_THETA = 10000.0
ROPE_AXIS_DIM = HEAD_DIM // 2

HY_W = D_MODEL // 4
HY_ORDER = 2
HY_SHORT = 3
HY_BANDS = 16
HY_EMB = 2 * HY_BANDS + 1
HY_FFN = 64
HY_DECAY_TARGET = 1e-2
HY_DECAY_SHORT_PCT = 0.3
HY_DECAY_LONG_PCT = 1.5

FN_GROUPS = 4
FN_GROUP_W = D_MODEL // 16
FN_W = FN_GROUPS * FN_GROUP_W

MIX_W = ATT_Q_W + HY_W + FN_W
N_BRANCH = 3

OFF_Q = 0
OFF_K = OFF_Q + ATT_Q_W
OFF_V = OFF_K + ATT_KV_W
OFF_HY = OFF_V + ATT_KV_W
OFF_FN = OFF_HY + (HY_ORDER + 1) * HY_W
OFF_GATE = OFF_FN + FN_W
IN_W = OFF_GATE + N_BRANCH * D_MODEL

N_EXPERTS = 16
EXPERT_FF = 2 * D_MODEL
CAPACITY_FACTOR = 2

EPS = 1e-6


def rms_norm(x, g):
    xf = x.astype(jnp.float32)
    y = xf * lax.rsqrt(jnp.mean(xf * xf, axis=-1, keepdims=True) + EPS)
    return (y * g.astype(jnp.float32)).astype(x.dtype)

def modulate(h, shift, scale):
    return h * (1.0 + scale) + shift

def axial_rope_tables(n_tokens):
    rows = n_tokens // GRID_W
    row = jnp.repeat(jnp.arange(rows, dtype=jnp.float32), GRID_W)
    col = jnp.tile(jnp.arange(GRID_W, dtype=jnp.float32), rows)
    inv = ROPE_THETA ** (-jnp.arange(0, ROPE_AXIS_DIM, 2, dtype=jnp.float32) / ROPE_AXIS_DIM)
    ang = jnp.concatenate([row[:, None] * inv, col[:, None] * inv], axis=-1)
    return jnp.cos(ang), jnp.sin(ang)

def apply_rope(u, cos, sin):
    uf = u.astype(jnp.float32).reshape(*u.shape[:-1], HEAD_DIM // 2, 2)
    u0, u1 = uf[..., 0], uf[..., 1]
    c = cos[None, :, None, :]
    s = sin[None, :, None, :]
    out = jnp.stack([u0 * c - u1 * s, u0 * s + u1 * c], axis=-1)
    return out.reshape(u.shape).astype(u.dtype)

def qk_heads(u, n_heads, gain, rope):
    b, n, _ = u.shape
    u = rms_norm(u.reshape(b, n, n_heads, HEAD_DIM), gain)
    if rope is not None:
        u = apply_rope(u, rope[0], rope[1])
    return u

def block_attention(q, k, v):
    b, n = q.shape[0], q.shape[1]
    nb = n // Q_BLOCK
    qb = q.reshape(b, nb, Q_BLOCK, N_KV_HEADS, Q_GROUP, HEAD_DIM).transpose(1, 0, 2, 3, 4, 5)
    scale = HEAD_DIM ** -0.5

    def attend(qblk):
        s = jnp.einsum('bqkgd,bskd->bkgqs', qblk, k, preferred_element_type=jnp.float32) * scale
        p = jax.nn.softmax(s, axis=-1).astype(v.dtype)
        return jnp.einsum('bkgqs,bskd->bqkgd', p, v)

    o = lax.map(attend, qb)
    return o.transpose(1, 0, 2, 3, 4, 5).reshape(b, n, ATT_Q_W)

def short_conv(u, w, b):
    n = u.shape[1]
    pad = HY_SHORT // 2
    up = jnp.pad(u, ((0, 0), (pad, pad), (0, 0)))
    out = b
    for j in range(HY_SHORT):
        out = out + up[:, j:j + n] * w[j]
    return out

def hyena_spectrum(n, w1, b1, w2, b2, w3, freq):
    f32 = jnp.float32
    w1, b1, w2, b2, w3, freq = (a.astype(f32) for a in (w1, b1, w2, b2, w3, freq))
    pos = jnp.arange(n, dtype=f32)
    t = pos / (n - 1)
    bands = jnp.linspace(1e-4, HY_BANDS - 1, HY_BANDS, dtype=f32)
    ang = (2.0 * math.pi / n) * pos[:, None] * bands[None, :]
    feats = jnp.concatenate([t[:, None], jnp.cos(ang), -jnp.sin(ang)], axis=-1)
    h = jnp.sin(freq * (feats @ w1 + b1))
    h = jnp.sin(freq * (h @ w2 + b2))
    h = (h @ w3).reshape(n, 2, HY_ORDER, HY_W)
    deltas = jnp.abs(jnp.linspace(math.log(HY_DECAY_TARGET) / HY_DECAY_LONG_PCT,
                                  math.log(HY_DECAY_TARGET) / HY_DECAY_SHORT_PCT, HY_W, dtype=f32))
    h = h * jnp.exp(-t[:, None] * deltas[None, :])[:, None, None, :]
    filt = jnp.concatenate([h[:, 0], jnp.zeros((1, HY_ORDER, HY_W), f32), h[1:, 1][::-1]], axis=0)
    filt = filt / jnp.sum(jnp.abs(filt), axis=0, keepdims=True)
    return jnp.fft.rfft(filt, axis=0)

def long_conv(z, spec, d):
    n = z.shape[1]
    zf = z.astype(jnp.float32)
    y = jnp.fft.irfft(jnp.fft.rfft(zf, n=2 * n, axis=1) * spec[None], n=2 * n, axis=1)[:, :n]
    return (y + zf * d.astype(jnp.float32)).astype(z.dtype)

def hyena_mixer(u, sw, sb, spec, bias):
    u = short_conv(u, sw, sb)
    v, g1, g2 = jnp.split(u, HY_ORDER + 1, axis=-1)
    z = g1 * long_conv(v, spec[:, 0], bias[0])
    return g2 * long_conv(z, spec[:, 1], bias[1])

def fourier_mix(u):
    b, n, _ = u.shape
    ug = u.astype(jnp.float32).reshape(b, n, FN_GROUPS, FN_GROUP_W)
    y = jnp.fft.fft2(ug, axes=(1, 3), norm='ortho').real
    return y.reshape(b, n, FN_W).astype(u.dtype)

def merge_branches(att, hy, fn, gates, w_branch, w_out):
    ga, gh, gf = jnp.split(gates, N_BRANCH, axis=-1)
    ya = att @ w_branch[:ATT_Q_W]
    yh = hy @ w_branch[ATT_Q_W:ATT_Q_W + HY_W]
    yf = fn @ w_branch[ATT_Q_W + HY_W:]
    m = jax.nn.sigmoid(ga) * ya + jax.nn.sigmoid(gh) * yh + jax.nn.sigmoid(gf) * yf
    return m @ w_out

def mixer_sublayer(h, k_ext, v_ext, rope, w_in, q_gain, k_gain, sw, sb, spec, hy_bias, w_branch, w_out):
    b, n, _ = h.shape
    p = h @ w_in
    q = qk_heads(p[..., OFF_Q:OFF_K], N_Q_HEADS, q_gain, rope)
    k = qk_heads(p[..., OFF_K:OFF_V], N_KV_HEADS, k_gain, rope)
    v = p[..., OFF_V:OFF_HY].reshape(b, n, N_KV_HEADS, HEAD_DIM)
    if k_ext is None:
        att = block_attention(q, k, v)
    else:
        att = block_attention(q, jnp.concatenate([k, k_ext], axis=1), jnp.concatenate([v, v_ext], axis=1))
    hy = hyena_mixer(p[..., OFF_HY:OFF_FN], sw, sb, spec, hy_bias)
    fn = fourier_mix(p[..., OFF_FN:OFF_GATE])
    return merge_branches(att, hy, fn, p[..., OFF_GATE:], w_branch, w_out), k, v

def expert_choice_moe(h, w_router, w_gate, w_up, w_down):
    b, n, d = h.shape
    cap = CAPACITY_FACTOR * n // N_EXPERTS
    logits = jnp.einsum('bld,de->ble', h, w_router, preferred_element_type=jnp.float32)
    aff = jax.nn.softmax(logits, axis=-1)
    top_w, top_i = lax.top_k(aff.transpose(0, 2, 1), cap)
    xg = jax.vmap(lambda hb, ib: hb[ib])(h, top_i)
    a = jnp.einsum('becd,edf->becf', xg, w_gate)
    u = jnp.einsum('becd,edf->becf', xg, w_up)
    y = jnp.einsum('becf,efd->becd', jax.nn.silu(a) * u, w_down)
    y = y * top_w[..., None].astype(y.dtype)
    return jax.vmap(lambda yb, ib: jnp.zeros((n, d), y.dtype).at[ib.reshape(-1)].add(yb.reshape(-1, d)))(y, top_i)

def first_inputs(seed: int = 0) -> dict:
    key = jax.random.key(seed)
    ks = jax.random.split(key, 27)
    f32 = jnp.float32
    D = D_MODEL

    def nrm(k, shape, scale):
        return jax.random.normal(k, shape, f32) * scale

    return {
        "x": nrm(ks[0], (BATCH, SEQ, D), 1.0),
        "c": nrm(ks[1], (BATCH, D), 1.0),
        "ctx": nrm(ks[2], (BATCH, CTX_LEN, D), 1.0),
        "c_ctx": nrm(ks[3], (D,), 1.0),
        "w_mod": nrm(ks[4], (DEPTH, D, 6 * D), 0.5 * D ** -0.5),
        "b_mod": nrm(ks[5], (DEPTH, 6 * D), 0.02),
        "norm1_g": 1.0 + nrm(ks[6], (DEPTH, D), 0.02),
        "norm2_g": 1.0 + nrm(ks[7], (DEPTH, D), 0.02),
        "w_in": nrm(ks[8], (DEPTH, D, IN_W), D ** -0.5),
        "q_gain": 1.0 + nrm(ks[9], (DEPTH, HEAD_DIM), 0.02),
        "k_gain": 1.0 + nrm(ks[10], (DEPTH, HEAD_DIM), 0.02),
        "hy_short_w": nrm(ks[11], (DEPTH, HY_SHORT, (HY_ORDER + 1) * HY_W), HY_SHORT ** -0.5),
        "hy_short_b": nrm(ks[12], (DEPTH, (HY_ORDER + 1) * HY_W), 0.02),
        "hy_f_w1": nrm(ks[13], (DEPTH, HY_EMB, HY_FFN), HY_EMB ** -0.5),
        "hy_f_b1": nrm(ks[14], (DEPTH, HY_FFN), 0.1),
        "hy_f_w2": nrm(ks[15], (DEPTH, HY_FFN, HY_FFN), HY_FFN ** -0.5),
        "hy_f_b2": nrm(ks[16], (DEPTH, HY_FFN), 0.1),
        "hy_f_w3": nrm(ks[17], (DEPTH, HY_FFN, 2 * HY_ORDER * HY_W), HY_FFN ** -0.5),
        "hy_f_freq": 1.0 + nrm(ks[18], (DEPTH, HY_FFN), 0.02),
        "hy_bias": nrm(ks[19], (DEPTH, HY_ORDER, HY_W), 1.0),
        "w_branch": nrm(ks[20], (DEPTH, MIX_W, D), (MIX_W // 4) ** -0.5),
        "w_out": nrm(ks[21], (DEPTH, D, D), D ** -0.5),
        "w_router": nrm(ks[22], (DEPTH, D, N_EXPERTS), D ** -0.5),
        "w_gate": nrm(ks[23], (DEPTH, N_EXPERTS, D, EXPERT_FF), D ** -0.5),
        "w_up": nrm(ks[24], (DEPTH, N_EXPERTS, D, EXPERT_FF), D ** -0.5),
        "w_down": nrm(ks[25], (DEPTH, N_EXPERTS, EXPERT_FF, D), EXPERT_FF ** -0.5),
        "final_g": 1.0 + nrm(ks[26], (D,), 0.02),
    }

def first_block(x, c, ctx, c_ctx, w_mod, b_mod, norm1_g, norm2_g, w_in, q_gain, k_gain,
              hy_short_w, hy_short_b, hy_f_w1, hy_f_b1, hy_f_w2, hy_f_b2, hy_f_w3, hy_f_freq,
              hy_bias, w_branch, w_out, w_router, w_gate, w_up, w_down, final_g):
    n_lat = x.shape[1]
    n_ctx = ctx.shape[1]
    rope = axial_rope_tables(n_lat)
    sc = jax.nn.silu(c)
    scc = jax.nn.silu(c_ctx)
    for l in range(DEPTH):
        last = l == DEPTH - 1
        mx = (sc @ w_mod[l] + b_mod[l])[:, None, :]
        mc = scc @ w_mod[l] + b_mod[l]
        sh1, sc1, g1, sh2, sc2, g2 = jnp.split(mx, 6, axis=-1)
        csh1, csc1, cg1, csh2, csc2, cg2 = jnp.split(mc, 6, axis=-1)

        hc = modulate(rms_norm(ctx, norm1_g[l]), csh1, csc1)
        if last:
            pkv = hc @ w_in[l][:, OFF_K:OFF_HY]
            kc = qk_heads(pkv[..., :ATT_KV_W], N_KV_HEADS, k_gain[l], None)
            vc = pkv[..., ATT_KV_W:].reshape(ctx.shape[0], n_ctx, N_KV_HEADS, HEAD_DIM)
        else:
            spec_c = hyena_spectrum(n_ctx, hy_f_w1[l], hy_f_b1[l], hy_f_w2[l], hy_f_b2[l], hy_f_w3[l], hy_f_freq[l])
            yc, kc, vc = mixer_sublayer(hc, None, None, None, w_in[l], q_gain[l], k_gain[l],
                                        hy_short_w[l], hy_short_b[l], spec_c, hy_bias[l], w_branch[l], w_out[l])

        spec_x = hyena_spectrum(n_lat, hy_f_w1[l], hy_f_b1[l], hy_f_w2[l], hy_f_b2[l], hy_f_w3[l], hy_f_freq[l])
        hx = modulate(rms_norm(x, norm1_g[l]), sh1, sc1)
        yx, _, _ = mixer_sublayer(hx, kc, vc, rope, w_in[l], q_gain[l], k_gain[l],
                                  hy_short_w[l], hy_short_b[l], spec_x, hy_bias[l], w_branch[l], w_out[l])
        x = x + g1 * yx
        h2 = modulate(rms_norm(x, norm2_g[l]), sh2, sc2)
        x = x + g2 * expert_choice_moe(h2, w_router[l], w_gate[l], w_up[l], w_down[l])

        if not last:
            ctx = ctx + cg1 * yc
            hc2 = modulate(rms_norm(ctx, norm2_g[l]), csh2, csc2)
            ctx = ctx + cg2 * expert_choice_moe(hc2, w_router[l], w_gate[l], w_up[l], w_down[l])
    return rms_norm(x, final_g)


DEPTH_2 = 2

RWKV_WIDTH = D_MODEL // 4
RWKV_HEADS = RWKV_WIDTH // HEAD_DIM
RWKV_DECAY_LORA = 64
RWKV_ICLR_LORA = 64
RWKV_GATE_LORA = 128
RWKV_COLS = 3 * RWKV_WIDTH + RWKV_GATE_LORA + 2 * RWKV_DECAY_LORA + 2 * RWKV_ICLR_LORA
MLA_V = 64
MLA_WIDTH = D_MODEL // 2
MLA_HEADS = MLA_WIDTH // MLA_V
MLA_NOPE = 64
MLA_ROPE = 32
MLA_Q_RANK = 384
MLA_KV_RANK = 256
MLA_COLS = MLA_Q_RANK + MLA_KV_RANK + MLA_ROPE
MLA_BLOCK = 128
RET_WIDTH = D_MODEL - RWKV_WIDTH - MLA_WIDTH
RET_HEADS = RET_WIDTH // HEAD_DIM
RET_COLS = 4 * RET_WIDTH
RET_CHUNK = 128

MIX_WIDTH = RWKV_WIDTH + MLA_WIDTH + RET_WIDTH
IN_COLS = RWKV_COLS + MLA_COLS + RET_COLS
D_FF = 2816
N_MOD = 9
ROPE_BASE = 10000.0
NORM_EPS = 1e-6
RWKV_LN_EPS = 64e-5
RET_LN_EPS = 1e-5


def split_cols(t, sizes):
    idx = np.cumsum(sizes)[:-1].tolist()
    return jnp.split(t, idx, axis=-1)

def rms_norm_2(t, eps=NORM_EPS):
    tf = t.astype(jnp.float32)
    return (tf * lax.rsqrt(jnp.mean(tf * tf, axis=-1, keepdims=True) + eps)).astype(t.dtype)

def head_norm(t, eps):
    tf = t.astype(jnp.float32)
    mu = jnp.mean(tf, axis=-1, keepdims=True)
    var = jnp.mean(jnp.square(tf - mu), axis=-1, keepdims=True)
    return (tf - mu) * lax.rsqrt(var + eps)

def modulate_2(t, shift, scale):
    return t * (1.0 + scale[:, None, :]) + shift[:, None, :]

def swiglu(h, w_in, w_out):
    gate, up = jnp.split(h @ w_in, 2, axis=-1)
    return (jax.nn.silu(gate) * up) @ w_out

def rotary(t, positions):
    d = t.shape[-1]
    inv = ROPE_BASE ** (-jnp.arange(0, d, 2, dtype=jnp.float32) / d)
    ang = positions.astype(jnp.float32)[..., None] * inv
    ang = ang.reshape(ang.shape[:2] + (1,) * (t.ndim - 3) + ang.shape[-1:])
    cos, sin = jnp.cos(ang).astype(t.dtype), jnp.sin(ang).astype(t.dtype)
    t1, t2 = t[..., : d // 2], t[..., d // 2:]
    return jnp.concatenate([t1 * cos - t2 * sin, t2 * cos + t1 * sin], axis=-1)

def centred_shift(t, mu):
    prev = jnp.pad(t[:, :-1], ((0, 0), (1, 0), (0, 0)))
    nxt = jnp.pad(t[:, 1:], ((0, 0), (0, 1), (0, 0)))
    return t + mu * (0.5 * (prev + nxt) - t)

def _dir_stack(t):
    t = jnp.stack([t[:, :, 0], jnp.flip(t[:, :, 1], axis=1)], axis=2)
    return jnp.transpose(t, (1, 2, 0, 3, 4))

def rwkv7_mixer(z, mu, w0, w_up, a0, a_up, g_up, k_k, k_a, r_k, ln_g, ln_b):
    B, S, _ = z.shape
    H, N = RWKV_HEADS, HEAD_DIM
    z = centred_shift(z, mu)
    r, k, v, g_lo, w_lo, a_lo = split_cols(
        z, [RWKV_WIDTH, RWKV_WIDTH, RWKV_WIDTH, RWKV_GATE_LORA, 2 * RWKV_DECAY_LORA, 2 * RWKV_ICLR_LORA])
    w_lo = w_lo.reshape(B, S, 2, RWKV_DECAY_LORA)
    a_lo = a_lo.reshape(B, S, 2, RWKV_ICLR_LORA)
    w_raw = (w0 + jnp.einsum('bsdr,drc->bsdc', jnp.tanh(w_lo), w_up)).astype(jnp.float32)
    decay = jnp.exp(-jnp.exp(-jax.nn.softplus(-w_raw) - 0.5)).reshape(B, S, 2, H, N)
    a = jax.nn.sigmoid(a0 + jnp.einsum('bsdr,drc->bsdc', a_lo, a_up))
    g = jax.nn.sigmoid(g_lo) @ g_up
    kk = (k * k_k).reshape(B, S, H, N).astype(jnp.float32)
    kk = kk / jnp.maximum(jnp.linalg.norm(kk, axis=-1, keepdims=True), 1e-12)
    kk2 = jnp.broadcast_to(kk[:, :, None], (B, S, 2, H, N))
    a5 = a.reshape(B, S, 2, H, N)
    k_mod = (k[:, :, None, :] * (1.0 + (a - 1.0) * k_a)).reshape(B, S, 2, H, N)
    rh, kh, vh = (t.reshape(B, S, H, N) for t in (r, k, v))
    r2 = jnp.broadcast_to(rh[:, :, None], (B, S, 2, H, N))
    v2 = jnp.broadcast_to(vh[:, :, None], (B, S, 2, H, N))
    xs = tuple(_dir_stack(t) for t in (decay, kk2, kk2 * a5, k_mod, v2, r2))

    def step(state, inp):
        w_t, kk_t, kka_t, k_t, v_t, r_t = inp
        sk = jnp.einsum('dbhvk,dbhk->dbhv', state, kk_t)
        new = (state * w_t[..., None, :] - sk[..., :, None] * kka_t[..., None, :]
               + v_t[..., :, None] * k_t[..., None, :])
        y_fwd = jnp.einsum('bhvk,bhk->bhv', new[0], r_t[0])
        y_bwd = jnp.einsum('bhvk,bhk->bhv', state[1], r_t[1])
        return new, jnp.stack([y_fwd, y_bwd])

    state0 = jnp.zeros((2, B, H, N, N), jnp.float32)
    _, ys = lax.scan(step, state0, xs)
    y = ys[:, 0] + jnp.flip(ys[:, 1], axis=0)
    y = jnp.transpose(y, (1, 0, 2, 3))
    y = (head_norm(y, RWKV_LN_EPS) * ln_g + ln_b).astype(z.dtype)
    bonus = jnp.sum(rh * kh * r_k, axis=-1, keepdims=True) * vh
    return (y + bonus).reshape(B, S, RWKV_WIDTH) * g

def mla_mixer(z, positions, q_norm_g, w_uq, kv_norm_g, w_ukv):
    B, S, _ = z.shape
    H = MLA_HEADS
    cq, ckv, kpe = split_cols(z, [MLA_Q_RANK, MLA_KV_RANK, MLA_ROPE])
    q = ((rms_norm_2(cq) * q_norm_g) @ w_uq).reshape(B, S, H, MLA_NOPE + MLA_ROPE)
    kv = ((rms_norm_2(ckv) * kv_norm_g) @ w_ukv).reshape(B, S, H, MLA_NOPE + MLA_V)
    q_nope, q_pe = q[..., :MLA_NOPE], rotary(q[..., MLA_NOPE:], positions)
    k_nope, v = kv[..., :MLA_NOPE], kv[..., MLA_NOPE:]
    k_pe = rotary(kpe, positions)
    scale = (MLA_NOPE + MLA_ROPE) ** -0.5
    nb = S // MLA_BLOCK
    qn_b = jnp.transpose(q_nope.reshape(B, nb, MLA_BLOCK, H, MLA_NOPE), (1, 0, 2, 3, 4))
    qp_b = jnp.transpose(q_pe.reshape(B, nb, MLA_BLOCK, H, MLA_ROPE), (1, 0, 2, 3, 4))

    def attend(blk):
        qn, qp = blk
        s = (jnp.einsum('bqhd,bkhd->bhqk', qn, k_nope)
             + jnp.einsum('bqhr,bkr->bhqk', qp, k_pe))
        p = jax.nn.softmax(s.astype(jnp.float32) * scale, axis=-1).astype(v.dtype)
        return jnp.einsum('bhqk,bkhd->bqhd', p, v)

    o = lax.map(attend, (qn_b, qp_b))
    return jnp.transpose(o, (1, 0, 2, 3, 4)).reshape(B, S, MLA_WIDTH)

def retention_dir(q, k, v, log_gamma, strict):
    B, H, S, d = q.shape
    C = RET_CHUNK
    n = S // C
    qc, kc, vc = (t.reshape(B, H, n, C, d) for t in (q, k, v))
    lg = log_gamma.astype(jnp.float32)
    pos = jnp.arange(C, dtype=jnp.float32)
    diff = pos[:, None] - pos[None, :]
    mask = diff > 0 if strict else diff >= 0
    dmat = jnp.where(mask, jnp.exp(lg[:, None, None] * jnp.maximum(diff, 0.0)), 0.0)
    scores = jnp.einsum('bhncd,bhnmd->bhncm', qc, kc) * dmat[None, :, None]
    inner = jnp.einsum('bhncm,bhnme->bhnce', scores, vc)
    k_w = kc * jnp.exp(lg[:, None] * (C - 1.0 - pos)[None, :])[None, :, None, :, None]
    kv = jnp.einsum('bhncd,bhnce->nbhde', k_w, vc)
    chunk_decay = jnp.exp(lg * C)[None, :, None, None]

    def step(R, kv_n):
        return R * chunk_decay + kv_n, R

    _, r_prev = lax.scan(step, jnp.zeros((B, H, d, d), jnp.float32), kv)
    q_w = qc * jnp.exp(lg[:, None] * (pos + 1.0)[None, :])[None, :, None, :, None]
    cross = jnp.einsum('bhncd,nbhde->bhnce', q_w, r_prev)
    return (inner + cross).reshape(B, H, S, d)

def retention_mixer(z, positions, log_rate, gn_g):
    B, S, _ = z.shape
    H, d = RET_HEADS, HEAD_DIM
    q, k, v, gate = split_cols(z, [RET_WIDTH] * 4)
    q = rotary(q.reshape(B, S, H, d), positions)
    k = rotary(k.reshape(B, S, H, d), positions) * (d ** -0.5)
    v = v.reshape(B, S, H, d)
    q, k, v = (jnp.transpose(t, (0, 2, 1, 3)) for t in (q, k, v))
    log_gamma = -jnp.exp(log_rate.astype(jnp.float32))
    y_f = retention_dir(q, k, v, log_gamma[0], False)
    y_b = jnp.flip(retention_dir(jnp.flip(q, 2), jnp.flip(k, 2), jnp.flip(v, 2), log_gamma[1], True), 2)
    y = jnp.transpose(y_f + y_b, (0, 2, 1, 3))
    y = (head_norm(y, RET_LN_EPS) * gn_g).astype(z.dtype).reshape(B, S, RET_WIDTH)
    return jax.nn.silu(gate) * y

def second_inputs(seed: int = 0) -> dict:
    key = jax.random.key(seed)
    ks = jax.random.split(key, 32)
    L, D = DEPTH_2, D_MODEL
    C = RWKV_WIDTH

    def nrm(k, shape, scale):
        return jax.random.normal(k, shape, jnp.float32) * scale

    ret_base = jnp.log(2.0 ** (-5.0 - jnp.arange(RET_HEADS, dtype=jnp.float32)))
    return {
        'x': nrm(ks[0], (BATCH, SEQ, D), 1.0),
        'c': nrm(ks[1], (BATCH, D), 1.0),
        'positions': jnp.tile(jnp.arange(SEQ, dtype=jnp.int32)[None, :], (BATCH, 1)),
        'w_ada': nrm(ks[2], (L, D, N_MOD * D), 0.5 * D ** -0.5),
        'b_ada': nrm(ks[3], (L, N_MOD * D), 0.02),
        'w_ff1_in': nrm(ks[4], (L, D, 2 * D_FF), D ** -0.5),
        'w_ff1_out': nrm(ks[5], (L, D_FF, D), D_FF ** -0.5),
        'w_ff2_in': nrm(ks[6], (L, D, 2 * D_FF), D ** -0.5),
        'w_ff2_out': nrm(ks[7], (L, D_FF, D), D_FF ** -0.5),
        'w_in': nrm(ks[8], (L, D, IN_COLS), D ** -0.5),
        'w_out': nrm(ks[9], (L, MIX_WIDTH, D), MIX_WIDTH ** -0.5),
        'rwkv_mu': jax.random.uniform(ks[10], (L, RWKV_COLS), jnp.float32),
        'rwkv_w0': jax.random.uniform(ks[11], (L, 2, C), jnp.float32, minval=-5.0, maxval=1.0),
        'rwkv_w_up': nrm(ks[12], (L, 2, RWKV_DECAY_LORA, C), 0.5 * RWKV_DECAY_LORA ** -0.5),
        'rwkv_a0': nrm(ks[13], (L, 2, C), 0.5),
        'rwkv_a_up': nrm(ks[14], (L, 2, RWKV_ICLR_LORA, C), 0.5 * RWKV_ICLR_LORA ** -0.5),
        'rwkv_g_up': nrm(ks[15], (L, RWKV_GATE_LORA, C), RWKV_GATE_LORA ** -0.5),
        'rwkv_k_k': 0.85 + nrm(ks[16], (L, C), 0.05),
        'rwkv_k_a': 1.0 + nrm(ks[17], (L, C), 0.05),
        'rwkv_r_k': nrm(ks[18], (L, RWKV_HEADS, HEAD_DIM), 0.1),
        'rwkv_ln_g': 1.0 + nrm(ks[19], (L, RWKV_HEADS, HEAD_DIM), 0.05),
        'rwkv_ln_b': nrm(ks[20], (L, RWKV_HEADS, HEAD_DIM), 0.02),
        'mla_q_norm_g': 1.0 + nrm(ks[21], (L, MLA_Q_RANK), 0.05),
        'mla_w_uq': nrm(ks[22], (L, MLA_Q_RANK, MLA_HEADS * (MLA_NOPE + MLA_ROPE)), MLA_Q_RANK ** -0.5),
        'mla_kv_norm_g': 1.0 + nrm(ks[23], (L, MLA_KV_RANK), 0.05),
        'mla_w_ukv': nrm(ks[24], (L, MLA_KV_RANK, MLA_HEADS * (MLA_NOPE + MLA_V)), MLA_KV_RANK ** -0.5),
        'ret_log_rate': ret_base + nrm(ks[25], (L, 2, RET_HEADS), 0.1),
        'ret_gn_g': 1.0 + nrm(ks[26], (L, RET_HEADS, HEAD_DIM), 0.05),
        'final_norm_g': 1.0 + nrm(ks[27], (D,), 0.05),
    }

def second_block(x, c, positions, w_ada, b_ada, w_ff1_in, w_ff1_out, w_ff2_in, w_ff2_out,
              w_in, w_out, rwkv_mu, rwkv_w0, rwkv_w_up, rwkv_a0, rwkv_a_up, rwkv_g_up,
              rwkv_k_k, rwkv_k_a, rwkv_r_k, rwkv_ln_g, rwkv_ln_b, mla_q_norm_g, mla_w_uq,
              mla_kv_norm_g, mla_w_ukv, ret_log_rate, ret_gn_g, final_norm_g):
    cond = jax.nn.silu(c)
    for l in range(DEPTH_2):
        mod = cond @ w_ada[l] + b_ada[l]
        sh1, sc1, g1, sh2, sc2, g2, sh3, sc3, g3 = jnp.split(mod, N_MOD, axis=-1)
        h = modulate_2(rms_norm_2(x), sh1, sc1)
        x = x + 0.5 * g1[:, None, :] * swiglu(h, w_ff1_in[l], w_ff1_out[l])
        h = modulate_2(rms_norm_2(x), sh2, sc2)
        z = h @ w_in[l]
        z_a, z_b, z_c = split_cols(z, [RWKV_COLS, MLA_COLS, RET_COLS])
        o_a = rwkv7_mixer(z_a, rwkv_mu[l], rwkv_w0[l], rwkv_w_up[l], rwkv_a0[l], rwkv_a_up[l],
                          rwkv_g_up[l], rwkv_k_k[l], rwkv_k_a[l], rwkv_r_k[l], rwkv_ln_g[l], rwkv_ln_b[l])
        o_b = mla_mixer(z_b, positions, mla_q_norm_g[l], mla_w_uq[l], mla_kv_norm_g[l], mla_w_ukv[l])
        o_c = retention_mixer(z_c, positions, ret_log_rate[l], ret_gn_g[l])
        mixed = jnp.concatenate([o_a, o_b, o_c], axis=-1) @ w_out[l]
        x = x + g2[:, None, :] * mixed
        h = modulate_2(rms_norm_2(x), sh3, sc3)
        x = x + 0.5 * g3[:, None, :] * swiglu(h, w_ff2_in[l], w_ff2_out[l])
    return rms_norm_2(x) * final_norm_g


def setup_inputs(seed=0):
    out = dict(first_inputs(seed))
    for name, value in second_inputs(seed + 1).items():
        if name != "x":
            out[name + "_2"] = value
    return out


def reference(
    x, c, ctx, c_ctx, w_mod, b_mod, norm1_g, norm2_g, w_in, q_gain, k_gain, hy_short_w,
    hy_short_b, hy_f_w1, hy_f_b1, hy_f_w2, hy_f_b2, hy_f_w3, hy_f_freq, hy_bias, w_branch,
    w_out, w_router, w_gate, w_up, w_down, final_g, c_2, positions_2, w_ada_2, b_ada_2,
    w_ff1_in_2, w_ff1_out_2, w_ff2_in_2, w_ff2_out_2, w_in_2, w_out_2, rwkv_mu_2, rwkv_w0_2,
    rwkv_w_up_2, rwkv_a0_2, rwkv_a_up_2, rwkv_g_up_2, rwkv_k_k_2, rwkv_k_a_2, rwkv_r_k_2,
    rwkv_ln_g_2, rwkv_ln_b_2, mla_q_norm_g_2, mla_w_uq_2, mla_kv_norm_g_2, mla_w_ukv_2,
    ret_log_rate_2, ret_gn_g_2, final_norm_g_2,
):
    x = first_block(
        x, c, ctx, c_ctx, w_mod, b_mod, norm1_g, norm2_g, w_in, q_gain, k_gain, hy_short_w,
        hy_short_b, hy_f_w1, hy_f_b1, hy_f_w2, hy_f_b2, hy_f_w3, hy_f_freq, hy_bias, w_branch,
        w_out, w_router, w_gate, w_up, w_down, final_g,
    )
    return second_block(
        x, c_2, positions_2, w_ada_2, b_ada_2, w_ff1_in_2, w_ff1_out_2, w_ff2_in_2, w_ff2_out_2,
        w_in_2, w_out_2, rwkv_mu_2, rwkv_w0_2, rwkv_w_up_2, rwkv_a0_2, rwkv_a_up_2, rwkv_g_up_2,
        rwkv_k_k_2, rwkv_k_a_2, rwkv_r_k_2, rwkv_ln_g_2, rwkv_ln_b_2, mla_q_norm_g_2,
        mla_w_uq_2, mla_kv_norm_g_2, mla_w_ukv_2, ret_log_rate_2, ret_gn_g_2, final_norm_g_2,
    )


_drawn_inputs = setup_inputs


def setup_inputs(seed=0):
    import zlib

    import numpy as np

    out = dict(_drawn_inputs(seed))
    spreads = {}
    factors = {'ctx': 3.986,
     'norm1_g': 5.975,
     'norm2_g': 6.934,
     'q_gain': 8.0,
     'k_gain': 8.0,
     'hy_short_b': 7.852,
     'hy_f_b1': 6.227,
     'hy_f_b2': 5.088,
     'hy_f_freq': 8.0,
     'rwkv_w_up_2': 8.0,
     'rwkv_a_up_2': 3.103,
     'rwkv_k_k_2': 5.522,
     'rwkv_k_a_2': 5.595,
     'rwkv_ln_g_2': 8.0,
     'rwkv_ln_b_2': 8.0,
     'mla_q_norm_g_2': 8.0,
     'mla_kv_norm_g_2': 8.0,
     'ret_gn_g_2': 7.663}
    for name, (base, spread) in spreads.items():
        noise = np.random.default_rng([zlib.crc32(name.encode()), seed]).standard_normal(out[name].shape)
        drawn = base * np.exp(spread * noise) if base else spread * noise
        out[name] = jnp.asarray(drawn.astype(out[name].dtype))
    for name, factor in factors.items():
        out[name] = (out[name] * factor).astype(out[name].dtype)
    return out
```

```python
from contextlib import ExitStack

import numpy as np

import concourse.bass as bass
from concourse import mybir

P = 128
D = 1024
KD = D // P
T = 256
NT = T // P
HEAD = 64
E = 16
CAP = 2 * T // E
FF_E = 2 * D
KE = FF_E // P
D_FF = 2816
KF = D_FF // P
RWKV_COLS = 1152
EPS = 1e-6
RET_EPS = 1e-5
RWKV_EPS = 64e-5
PI = 3.14159265358979
RING_COLS = 24576

F32 = mybir.dt.float32
I32 = mybir.dt.int32
ALU = mybir.AluOpType
ACT = mybir.ActivationFunctionType
AX = mybir.AxisListType
MUL, ADD, SUB, MAX = ALU.mult, ALU.add, ALU.subtract, ALU.max


def shape_tables():
    f = np.float32
    out = {}
    p = np.arange(P)
    ident = np.eye(P)
    out["ident"] = ident
    out["ones"] = np.ones((P, P))
    out["ones_head"] = (p[:, None] // HEAD == p[None, :] // HEAD) * 1.0
    out["swap_pair"] = ident[p ^ 1]
    out["swap_head"] = ident[p ^ HEAD]
    out["swap_half"] = ident[p ^ 32]
    swap_mla = np.zeros((P, P))
    for a in range(32):
        swap_mla[64 + a, 64 + (a ^ 16)] = 1
    out["swap_mla"] = swap_mla
    swap_kpe = np.zeros((P, P))
    swap_kpe[:32, :32] = swap_mla[64:96, 64:96]
    out["swap_kpe"] = swap_kpe
    out["ones_but_first"] = np.ones((P, P)) * (p[:, None] > 0)

    tok = np.arange(T)
    inv = 10000.0 ** (-np.arange(0, 32, 2) / 32)
    ang = np.concatenate([(tok // 64)[:, None] * inv, (tok % 64)[:, None] * inv], 1)
    of_pair = (p % HEAD) // 2
    out["axial_cos"] = np.cos(ang)[:, of_pair].T
    out["axial_sin"] = np.sin(ang)[:, of_pair].T * np.where(p % 2, 1.0, -1.0)[:, None]

    rot = np.zeros((P, 6))
    rot[:, 0] = 10000.0 ** (-2 * (p % 32) / 64)
    rot[:, 1] = np.where(p % 64 < 32, -1, 1)
    pe = p - 64
    rot[64:96, 2] = 10000.0 ** (-2 * (pe[64:96] % 16) / 32)
    rot[64:96, 3] = np.where(pe[64:96] < 16, -1, 1)
    rot[:32, 4] = rot[64:96, 2]
    rot[:32, 5] = rot[64:96, 3]
    out["rot_freq"] = rot

    t = tok / (T - 1)
    bands = np.linspace(1e-4, 15, 16)
    fa = 2 * np.pi / T * tok[:, None] * bands[None, :]
    feats = np.zeros((P, T))
    feats[:33] = np.concatenate([t[:, None], np.cos(fa), -np.sin(fa)], 1).T
    out["hy_feats"] = feats
    deltas = np.abs(np.linspace(np.log(1e-2) / 1.5, np.log(1e-2) / 0.3, 256))
    win = np.exp(-t[:, None] * deltas[None, :])
    out["hy_window"] = win.reshape(2, P, 256).transpose(1, 0, 2)
    n2 = 2 * T
    tau = np.concatenate([tok, (n2 - tok) % n2])
    keep = np.ones(n2)
    keep[T] = 0
    fr = np.arange(T)
    th = 2 * np.pi * ((tau[:, None] * fr[None, :]) % n2) / n2
    alt = np.where(tau % 2, -1.0, 1.0)
    cc = np.cos(th[:, :P]).copy()
    cc[:, 0] = alt
    fd = np.concatenate([np.cos(th), -np.sin(th), cc], 1) * keep[:, None]
    out["dft_filter"] = fd.reshape(4, P, 640).transpose(1, 0, 2)
    th = 2 * np.pi * ((tok[:, None] * fr[None, :]) % n2) / n2
    alt = np.where(tok % 2, -1.0, 1.0)
    im = -np.sin(th)
    im[:, 0] = alt
    out["dft_signal"] = np.concatenate([np.cos(th), im], 1).reshape(2, P, 512).transpose(1, 0, 2)
    gre = 2 * np.cos(th.T) / n2
    gre[0] /= 2
    gim = -2 * np.sin(th.T) / n2
    gim[0] = alt / n2
    out["dft_inverse"] = np.concatenate([gre, gim], 0).reshape(4, P, T).transpose(1, 0, 2)

    w = np.arange(64)
    tw = 2 * np.pi * ((w[:, None] * w[None, :]) % 64) / 64
    bd = lambda m: np.kron(np.eye(2), m)
    out["fn_channel"] = np.concatenate([bd(np.cos(tw)), bd(np.sin(tw))], 1)
    tn = 2 * np.pi * ((tok[:, None] * tok[None, :]) % T) / T
    out["fn_token"] = (np.concatenate([np.cos(tn), -np.sin(tn)], 1) / 128).reshape(2, P, 512).transpose(1, 0, 2)

    s_, t_ = p[:, None], p[None, :]
    lev = []
    for k in range(7):
        m = 1 << k
        lev.append(((s_ // m) % 2 == 0) & (t_ // m == s_ // m + 1))
    lev.append(lev[0] & False)
    out["level_fwd"] = np.stack(lev, 1)
    out["level_bwd"] = np.stack([x.T for x in lev], 1)
    out["tri"] = np.stack([s_ < t_, s_ > t_, s_ <= t_, s_ > t_], 1)
    ds = np.arange(T)[None, :] - np.arange(T)[:, None]
    out["ahead"] = np.maximum(ds, 0).reshape(2, P, T).transpose(1, 0, 2)
    out["behind"] = np.maximum(-ds, 0).reshape(2, P, T).transpose(1, 0, 2)
    out["slots"] = np.broadcast_to(np.arange(1, CAP + 1), (P, CAP))
    return {k: np.ascontiguousarray(v, dtype=f) for k, v in out.items()}


def blocks(w, n_order="kn"):
    *lead, k, n = w.shape
    w = w.reshape(*lead, k // P, P, n // P, P)
    nl = len(lead)
    w = w.transpose(*range(nl), nl + 1, nl + 2, nl, nl + 3)
    return w.reshape(*lead, P, (n // P) * (k // P) * P)


def panels(w, blk):
    *lead, k, n = w.shape
    b = blocks(w).reshape(*lead, P, -1, blk * P)
    nl = len(lead)
    return np.ascontiguousarray(b.transpose(*range(nl), nl + 1, nl, nl + 2))


def wide_tiles(w):
    *lead, k, n = w.shape
    nl = len(lead)
    w = w.reshape(*lead, k // (2 * P), 2, P, n // 1536, 1536)
    w = w.transpose(*range(nl), nl + 3, nl, nl + 2, nl + 1, nl + 4)
    return w.reshape(*lead, -1, P, 2 * 1536)


def column(v):
    v = np.asarray(v).reshape(-1)
    if v.size < P:
        v = np.concatenate([v, v])
    return v.reshape(-1, P).T


def interleave(a, b):
    *lead, k, n = a.shape
    return np.stack([a.reshape(*lead, k, n // P, P), b.reshape(*lead, k, n // P, P)], -2).reshape(*lead, k, 2 * n)


VEC1 = dict(c=8, c_ctx=8, b_mod=48, norm1=8, norm2=8, q_gain=1, k_gain=1, short_w=18, short_b=6,
            f_b1=1, f_b2=1, f_freq=1, hy_bias=4, final_g=8, c_2=8, final_2=8)
VEC2 = dict(b_ada=72, mu=9, w0=4, a0=4, k_k=2, k_a=2, r_k=2, ln_g=2, ln_b=2, mla_q_g=3, mla_kv_g=2,
            gn_g=2, log_rate=8)
SMALL1 = dict(f_w1=64, f_w2=64, f_w3=1024, router=128)
SMALL2 = dict(w_up=256, a_up=256, g_up=256, w_uq=2304, w_ukv=2048)


def fields(widths):
    at, out = 0, {}
    for k, n in widths.items():
        out[k] = (at, at + n)
        at += n
    return out, at


def host_layout(i):
    def pad(a):
        return np.concatenate([a, np.zeros((P - a.shape[0],) + a.shape[1:], a.dtype)], 0)

    rows = lambda a: a.reshape(-1, P, a.shape[-1]).transpose(1, 0, 2).reshape(P, -1)
    o = {}
    o["x"], o["ctx"] = i["x"][0], i["ctx"][0]
    w = i["w_in"][0]
    o["w_kv"] = panels(w[:, 512:768], 16)
    o["w_in"] = panels(np.concatenate([w[:, :512], w[:, 768:]], 1), 16)
    o["w_mod"] = wide_tiles(i["w_mod"][0])
    wb = i["w_branch"][0]
    o["w_branch"] = panels(wb, 16)
    o["w_out"] = panels(i["w_out"][0], 16)
    up = np.stack([i["w_gate"][0].reshape(E, KD, P, FF_E), i["w_up"][0].reshape(E, KD, P, FF_E)], 3)
    down = i["w_down"][0].reshape(E, 4, 4, P, D).transpose(0, 2, 3, 1, 4)
    o["w_expert"] = np.concatenate([up.reshape(E, KD, P, 4 * D), down.reshape(E, 4, P, 4 * D)], 1)
    o["vec1"] = np.concatenate([
        column(i["c"]), column(i["c_ctx"]), column(i["b_mod"]), column(i["norm1_g"]), column(i["norm2_g"]),
        column(i["q_gain"]), column(i["k_gain"]), column(i["hy_short_w"]), column(i["hy_short_b"]),
        column(i["hy_f_b1"]), column(i["hy_f_b2"]), column(i["hy_f_freq"]), column(i["hy_bias"]),
        column(i["final_g"]), column(i["c_2"]), column(i["final_norm_g_2"])], 1)
    o["small1"] = np.concatenate([pad(i["hy_f_w1"][0]), pad(i["hy_f_w2"][0]), pad(i["hy_f_w3"][0]),
                                  rows(i["w_router"][0])], 1)
    o["positions"] = np.broadcast_to(i["positions_2"].reshape(1, T), (P, T))
    o["w_ada"] = wide_tiles(i["w_ada_2"])
    for n in "12":
        wi = i[f"w_ff{n}_in_2"]
        o[f"w_ff{n}_in"] = panels(interleave(wi[..., :D_FF], wi[..., D_FF:]), 16)
        o[f"w_ff{n}_out"] = panels(i[f"w_ff{n}_out_2"], KF)
    wi = i["w_in_2"]
    kpe = RWKV_COLS + 640
    gap = np.zeros(wi.shape[:2] + (P - 32,), wi.dtype)
    o["w_in_2"] = panels(np.concatenate([wi[..., :kpe], wi[..., kpe + 32:], wi[..., kpe:kpe + 32], gap,
                                         np.zeros(wi.shape[:2] + (P,), wi.dtype)], 2), 16)
    o["w_out_2"] = panels(i["w_out_2"], 16)
    o["vec2"] = np.stack([np.concatenate([
        column(i["b_ada_2"][l]), column(i["rwkv_mu_2"][l]), column(i["rwkv_w0_2"][l]), column(i["rwkv_a0_2"][l]),
        column(i["rwkv_k_k_2"][l]), column(i["rwkv_k_a_2"][l]), column(i["rwkv_r_k_2"][l]),
        column(i["rwkv_ln_g_2"][l]), column(i["rwkv_ln_b_2"][l]), column(i["mla_q_norm_g_2"][l]),
        column(i["mla_kv_norm_g_2"][l]), column(i["ret_gn_g_2"][l]),
        np.broadcast_to(i["ret_log_rate_2"][l].reshape(1, 8), (P, 8))], 1) for l in range(2)])
    o["small2"] = np.stack([np.concatenate([
        i["rwkv_w_up_2"][l].reshape(P, 256), i["rwkv_a_up_2"][l].reshape(P, 256), i["rwkv_g_up_2"][l],
        rows(i["mla_w_uq_2"][l]), rows(i["mla_w_ukv_2"][l])], 1) for l in range(2)])
    return {k: np.ascontiguousarray(v) for k, v in o.items()}


class Stage:

    count = 0

    def __init__(self, nc, name):
        Stage.count += 1
        self.nc, self.name = nc, f"{name}_{Stage.count}"

    def __enter__(self):
        self.stack, self.sems = ExitStack(), []
        return self

    def sb(self, name, shape, dt=F32):
        return self.stack.enter_context(self.nc.sbuf_tensor(f"{self.name}_{name}", shape, dt))[:]

    def sem(self, name):
        self.sems.append(self.stack.enter_context(self.nc.semaphore(f"{self.name}_{name}")))
        return self.sems[-1]

    def block(self):
        return self.nc.Block()

    def __exit__(self, kind, value, trace):
        if kind is None and self.sems:
            with self.nc.Block() as block:
                @block.gpsimd
                def _(pool):
                    for s in self.sems:
                        pool.sem_clear(s)
        self.stack.close()


class Chain:

    def __init__(self, eng, sem):
        self.eng, self.sem, self.n = eng, sem, 0

    def __call__(self, ins):
        self.n += 1
        ins.then_inc(self.sem, 1)
        self.eng.wait_ge(self.sem, self.n)


def over(eng, n):
    return eng.Fori(0, n) if n > 1 else ExitStack()


def stream(nc, st, ring, src, turns, slots, blk, mm, act=None, dve=None, act_wait=()):
    loaded = [st.sem(f"loaded{u}") for u in range(slots)]
    panel_done = st.sem("panel_done")
    act_done = st.sem("act_done")
    bank_free = st.sem("bank_free")
    cols = blk * P
    slot = [ring[:, u * cols:(u + 1) * cols] for u in range(slots)]
    with st.block() as block:
        @block.sync
        def _(sp):
            for u in range(slots):
                sp.dma_start(slot[u], src[u]).then_inc(loaded[u], 16)
            if turns > 1:
                with sp.Fori(1, turns) as i:
                    for u in range(slots):
                        sp.wait_ge(panel_done, i * slots + (u + 1 - slots))
                        sp.dma_start(slot[u], src[i * slots + u]).then_inc(loaded[u], 16)

        @block.tensor
        def _(pe):
            with over(pe, turns) as i:
                i = i if turns > 1 else 0
                for u in range(slots):
                    q = i * slots + u
                    pe.wait_ge(loaded[u], i * 16 + 16)
                    if act or dve:
                        pe.wait_ge(bank_free, q + (2 if u == 0 and slots % 2 else 1))
                    mm(pe, q, u, slot[u].rearrange("p (b n) -> p b n", n=P)).then_inc(panel_done, 1)

        if act:
            @block.scalar
            def _(sc):
                if not dve:
                    sc.sem_inc(bank_free, 2)
                with over(sc, turns) as i:
                    i = i if turns > 1 else 0
                    for u in range(slots):
                        q = i * slots + u
                        sc.wait_ge(panel_done, q + 1)
                        act(sc, q, u).then_inc(act_done if dve else bank_free, 1)

        if dve:
            @block.vector
            def _(ve):
                ve.sem_inc(bank_free, 2)
                with over(ve, turns) as i:
                    i = i if turns > 1 else 0
                    for u in range(slots):
                        q = i * slots + u
                        ve.wait_ge(act_done if act else panel_done, q + 1)
                        dve(ve, q, u).then_inc(bank_free, 1)


def norm_modulate(nc, c, ps, groups):
    with Stage(nc, "norm") as st:
        w = T * len(groups)
        sq = st.sb("sq", [P, KD, w])
        root = st.sb("root", [P, w])
        rstd = st.sb("rstd", [P, w])
        squared, summed, rooted, inverted, scaled = (
            st.sem(n) for n in ("squared", "summed", "rooted", "inverted", "scaled"))
        with st.block() as block:
            @block.scalar
            def _(sc):
                for g, (x, _, _, _) in enumerate(groups):
                    sc.activation(sq[:, :, g * T:(g + 1) * T], x, ACT.Square).then_inc(squared, 1)
                sc.wait_ge(summed, 1)
                sc.activation(root[:, :], ps[0][:, 0:w], ACT.Sqrt, bias=c["eps"][:, 0:1],
                              scale=1.0 / D).then_inc(rooted, 1)
                for g, (_, out, _, shift) in enumerate(groups):
                    for k in range(KD):
                        if shift is None:
                            continue
                        sc.wait_ge(scaled, g * KD + k + 1)
                        sc.activation(out[:, k], out[:, k], ACT.Identity, bias=shift[:, k:k + 1])

            @block.tensor
            def _(pe):
                pe.wait_ge(squared, len(groups))
                for k in range(KD):
                    mm = pe.matmul(ps[0][:, 0:w], c["ones"][:, :], sq[:, k], start=k == 0, stop=k == KD - 1)
                mm.then_inc(summed, 1)

            @block.vector
            def _(ve):
                ve.wait_ge(rooted, 1)
                ve.reciprocal(rstd[:, :], root[:, :]).then_inc(inverted, 1)
                ve.wait_ge(inverted, 1)
                for g, (x, out, gain, _) in enumerate(groups):
                    for k in range(KD):
                        ve.scalar_tensor_tensor(out[:, k], x[:, k], gain[:, k:k + 1],
                                                rstd[:, g * T:(g + 1) * T], MUL, MUL).then_inc(scaled, 1)


def load_all(nc, pairs):
    with Stage(nc, "load") as st:
        landed = st.sem("landed")
        with st.block() as block:
            @block.sync
            def _(sp):
                for dst, src in pairs:
                    sp.dma_start(dst, src).then_inc(landed, 16)
                sp.wait_ge(landed, 16 * len(pairs))


def turn_features(nc, c, ps, loads, outs):
    with Stage(nc, "turn") as st:
        n = len(loads)
        rows = st.sb("rows", [P, n, NT, D])
        landed, turned, copied = st.sem("landed"), st.sem("turned"), st.sem("copied")
        jobs = [(g, t, h) for g in range(n) for t in range(NT) for h in range(2)]
        with st.block() as block:
            @block.sync
            def _(sp):
                for g, src in enumerate(loads):
                    sp.dma_start(rows[:, g], src.rearrange("(t p) d -> p t d", p=P)).then_inc(landed, 16)

            @block.tensor
            def _(pe):
                for j, (g, t, h) in enumerate(jobs):
                    pe.wait_ge(landed, 16 * n)
                    for k in range(4):
                        f = (4 * h + k) * P
                        mm = pe.transpose(ps[j][:, k * P:(k + 1) * P], rows[:, g, t, f:f + P], c["ident"][:, :])
                    mm.then_inc(turned, 1)

            @block.vector
            def _(ve):
                for j, (g, t, h) in enumerate(jobs):
                    ve.wait_ge(turned, j + 1)
                    ve.tensor_copy(outs[g][:, 4 * h:4 * h + 4, t * P:(t + 1) * P],
                                   ps[j][:, :].rearrange("p (k n) -> p k n", n=P)).then_inc(copied, 1)


def modulation(nc, st, c, ring, ps, src, n_tiles, cond, which, mod, bias):
    slots, per_tile, width = 8, KD // 2, 3 * P
    rows = st.sb("rows", [P, 2, width])
    loaded = [st.sem(f"loaded{u}") for u in range(slots)]
    panel_done, rows_out, turned, added = (st.sem(k) for k in ("panel_done", "rows_out", "turned", "added"))
    cols = 8 * width
    slot = [ring[:, u * cols:(u + 1) * cols] for u in range(slots)]
    turns = n_tiles // 2
    split = lambda a: a.rearrange("p (t g n) -> p t g n", g=4, n=3)
    with st.block() as block:
        @block.sync
        def _(sp):
            for u in range(slots):
                sp.dma_start(slot[u], src[u]).then_inc(loaded[u], 16)
            with sp.Fori(1, turns) as i:
                for u in range(slots):
                    sp.wait_ge(panel_done, i * slots + (u + 1 - slots))
                    sp.dma_start(slot[u], src[i * slots + u]).then_inc(loaded[u], 16)

        @block.tensor
        def _(pe):
            with pe.Fori(0, turns) as i:
                for t in range(2):
                    pe.wait_ge(rows_out, i * 2 + (t + 1))
                    for j in range(per_tile):
                        u = t * per_tile + j
                        w = slot[u].rearrange("p (k g n) -> p k g n", k=2, g=4)
                        pe.wait_ge(loaded[u], i * 16 + 16)
                        for k in range(2):
                            for g in range(4):
                                mm = pe.matmul(ps[t][32 * g:32 * g + 32, 0:width], cond[:, 2 * j + k], w[:, k, g],
                                               start=j == 0 and k == 0, stop=j == per_tile - 1 and k == 1)
                        mm.then_inc(panel_done, 1)
                    pe.wait_ge(rows_out, i * 2 + (t + 3))
                    pe.wait_ge(added, i * 2 + (t + 1))
                    for n in range(3):
                        mm = pe.transpose(ps[2 + t][:, n * P:(n + 1) * P], rows[:, t, n * P:(n + 1) * P], c["ident"])
                    mm.then_inc(turned, 1)

        @block.scalar
        def _(sc):
            sc.sem_inc(rows_out, 2)
            with sc.Fori(0, turns) as i:
                for t in range(2):
                    sc.wait_ge(panel_done, i * slots + (t + 1) * per_tile)
                    sc.wait_ge(added, i * 2 + (t + 1))
                    sc.activation(rows[:, t], ps[t][:, 0:width], ACT.Copy).then_inc(rows_out, 1)

        @block.vector
        def _(ve):
            ve.sem_inc(added, 2)
            with ve.Fori(0, turns) as i:
                for t in range(2):
                    ve.wait_ge(turned, i * 2 + (t + 1))
                    sums = ps[2 + t][:, 0:width].rearrange("p (n g v) -> p g n v", n=3, g=4)
                    for j, v in enumerate(which):
                        m = ve.tensor_tensor(split(mod[:, :, j])[:, i * 2 + t], sums[:, :, :, v],
                                             split(bias)[:, i * 2 + t], ADD)
                    m.then_inc(added, 1)


def attention(nc, c, ps, q_of, k_of, v_of, out_of, n_heads, n_keys):
    kt = n_keys // P
    with Stage(nc, "attention") as st:
        prob = st.sb("prob", [P, 4, n_keys])
        probT = st.sb("probT", [P, 2, kt, T])
        low = st.sb("low", [P, 4])
        tot = st.sb("tot", [P, 4])
        inv = st.sb("inv", [P, 4])
        scored, lowest, exped, inverted, scaled, turned, copied, mixed, stored = (st.sem(n) for n in (
            "scored", "lowest", "exped", "inverted", "scaled", "turned", "copied", "mixed", "stored"))
        units = [(h, t) for h in range(n_heads) for t in range(NT)]
        with st.block() as block:
            @block.tensor
            def _(pe):
                def scores(u):
                    h, t = units[u]
                    if u >= 4:
                        pe.wait_ge(exped, u - 3)
                    pe.matmul(ps[u % 4][:, 0:n_keys], q_of(h, t), k_of(h), start=True, stop=True).then_inc(scored, 1)

                def turn(u):
                    pe.wait_ge(scaled, u + 1)
                    if u >= 2:
                        pe.wait_ge(copied, u - 1)
                    for j in range(kt):
                        mm = pe.transpose(ps[4 + u % 2][:, j * P:(j + 1) * P], prob[:, u % 4, j * P:(j + 1) * P],
                                          c["ident"][:, :])
                    mm.then_inc(turned, 1)

                def mix(h):
                    pe.wait_ge(copied, 2 * h + 2)
                    if h >= 2:
                        pe.wait_ge(stored, h - 1)
                    o = out_of(h)
                    for j in range(kt):
                        mm = pe.matmul(ps[6 + h % 2][o[0]:o[0] + HEAD, 0:T], v_of(h, j), probT[:, h % 2, j],
                                       start=j == 0, stop=j == kt - 1)
                    mm.then_inc(mixed, 1)

                for u in range(len(units) + 3):
                    if u < len(units):
                        scores(u)
                    if 2 <= u < len(units) + 2:
                        turn(u - 2)
                    if u >= 4 and u % 2 == 0:
                        mix(u // 2 - 2)

            @block.vector
            def _(ve):
                def head(u):
                    ve.wait_ge(scored, u + 1)
                    if u >= 4:
                        ve.wait_ge(exped, u - 3)
                    ve.tensor_reduce(low[:, u % 4:u % 4 + 1], ps[u % 4][:, 0:n_keys], AX.X, MAX,
                                     negate=True).then_inc(lowest, 1)

                def tail(u):
                    ve.wait_ge(exped, u + 1)
                    ve.reciprocal(inv[:, u % 4:u % 4 + 1], tot[:, u % 4:u % 4 + 1]).then_inc(inverted, 1)
                    ve.wait_ge(inverted, u + 1)
                    ve.tensor_scalar(prob[:, u % 4], prob[:, u % 4], inv[:, u % 4:u % 4 + 1], None,
                                     MUL).then_inc(scaled, 1)

                for u in range(len(units) + 1):
                    if u < len(units):
                        head(u)
                    if u >= 1:
                        tail(u - 1)

            @block.scalar
            def _(sc):
                def turn_out(u):
                    h, t = units[u]
                    sc.wait_ge(turned, u + 1)
                    if u >= 4:
                        sc.wait_ge(mixed, h - 1)
                    sc.activation(probT[:, h % 2, :, t * P:(t + 1) * P],
                                  ps[4 + u % 2][:, 0:n_keys].rearrange("p (j n) -> p j n", n=P),
                                  ACT.Copy).then_inc(copied, 1)

                def store(h):
                    sc.wait_ge(mixed, h + 1)
                    o = out_of(h)
                    sc.activation(o[1], ps[6 + h % 2][o[0]:o[0] + HEAD, 0:T], ACT.Copy).then_inc(stored, 1)

                for u in range(len(units) + 4):
                    if u < len(units):
                        sc.wait_ge(lowest, u + 1)
                        if u >= 4:
                            sc.wait_ge(turned, u - 3)
                        sc.activation(prob[:, u % 4], ps[u % 4][:, 0:n_keys], ACT.Exp, bias=low[:, u % 4:u % 4 + 1],
                                      accum_out=tot[:, u % 4:u % 4 + 1]).then_inc(exped, 1)
                    if 2 <= u < len(units) + 2:
                        turn_out(u - 2)
                    if u >= 5 and u % 2 == 1:
                        store((u - 5) // 2)


def head_rms(nc, c, ps, x, n, w, gain, scale):
    with Stage(nc, "head_rms") as st:
        flat = x.rearrange("p a b -> p (a b)")
        groups = n * w // 512
        sq = st.sb("sq", [P, n * w])
        root = st.sb("root", [P, n * w])
        squared, summed, rooted, inverted, scaled = (
            st.sem(k) for k in ("squared", "summed", "rooted", "inverted", "scaled"))
        with st.block() as block:
            @block.scalar
            def _(sc):
                sc.activation(sq[:, :], flat, ACT.Square).then_inc(squared, 1)
                for g in range(groups):
                    sc.wait_ge(summed, g + 1)
                    sc.activation(root[:, g * 512:(g + 1) * 512], ps[g][:, :], ACT.Sqrt, bias=c["eps"][:, 0:1],
                                  scale=1.0 / HEAD).then_inc(rooted, 1)

            @block.tensor
            def _(pe):
                pe.wait_ge(squared, 1)
                for g in range(groups):
                    pe.matmul(ps[g][:, :], c["ones_head"][:, :], sq[:, g * 512:(g + 1) * 512],
                              start=True, stop=True).then_inc(summed, 1)

            @block.vector
            def _(ve):
                for g in range(groups):
                    col = slice(g * 512, (g + 1) * 512)
                    ve.wait_ge(rooted, g + 1)
                    ve.reciprocal(root[:, col], root[:, col]).then_inc(inverted, 1)
                    ve.wait_ge(inverted, g + 1)
                    ve.scalar_tensor_tensor(flat[:, col], flat[:, col], gain, root[:, col], MUL, MUL)\
                        .then_inc(scaled, 1)
                if scale != 1.0:
                    ve.wait_ge(scaled, groups)
                    ve.tensor_scalar(flat, flat, scale, None, MUL)


def rotate(nc, c, ps, x, n, rows, swap, cos, sin):
    with Stage(nc, "rotate") as st:
        turned = st.sb("turned", [rows, n, T])
        swapped, by_sin, by_cos = st.sem("swapped"), st.sem("by_sin"), st.sem("by_cos")
        pairs = (n + 1) // 2
        with st.block() as block:
            @block.tensor
            def _(pe):
                for j in range(pairs):
                    k = min(2, n - 2 * j)
                    pe.matmul(ps[j][0:rows, 0:k * T], swap, x[:, 2 * j:2 * j + k],
                              start=True, stop=True).then_inc(swapped, 1)

            @block.vector
            def _(ve):
                for j in range(pairs):
                    k = min(2, n - 2 * j)
                    tiles = slice(2 * j, 2 * j + k)
                    ve.wait_ge(swapped, j + 1)
                    ve.tensor_tensor(turned[:, tiles], ps[j][0:rows, 0:k * T].rearrange("p (a b) -> p a b", b=T),
                                     sin.unsqueeze(1).broadcast_to([rows, k, T]), MUL).then_inc(by_sin, 1)
                    ve.tensor_tensor(x[:, tiles], x[:, tiles], cos.unsqueeze(1).broadcast_to([rows, k, T]),
                                     MUL).then_inc(by_cos, 1)
                    ve.wait_ge(by_sin, j + 1)
                    ve.wait_ge(by_cos, j + 1)
                    ve.tensor_tensor(x[:, tiles], x[:, tiles], turned[:, tiles], ADD)


def turn_tokens(nc, c, ps, x_of, n, out_of):
    with Stage(nc, "turn_tiles") as st:
        turned, copied = st.sem("turned"), st.sem("copied")
        groups = (n + 3) // 4
        with st.block() as block:
            @block.tensor
            def _(pe):
                for g in range(groups):
                    if g >= 8:
                        pe.wait_ge(copied, g - 7)
                    for j in range(4 * g, min(4 * g + 4, n)):
                        mm = pe.transpose(ps[g % 8][:, (j % 4) * P:(j % 4 + 1) * P], x_of(j), c["ident"][:, :])
                    mm.then_inc(turned, 1)

            @block.vector
            def _(ve):
                for g in range(groups):
                    k = min(4, n - 4 * g)
                    ve.wait_ge(turned, g + 1)
                    ve.tensor_copy(out_of(g), ps[g % 8][:, 0:k * P].rearrange("p (a b) -> p a b", b=P))\
                        .then_inc(copied, 1)


def sine(ve, link, out, x, tmp, quarter):
    magic = 12582912.0
    link(ve.tensor_scalar(tmp, x, 1.0 / (2 * PI), 0.25 if quarter else 0.0, MUL, ADD))
    link(ve.tensor_scalar(tmp, tmp, magic, None, ADD))
    link(ve.tensor_scalar(tmp, tmp, magic, None, SUB))
    link(ve.scalar_tensor_tensor(out, tmp, -6.28125, x, MUL, ADD))
    link(ve.scalar_tensor_tensor(out, tmp, -0.0019350051879882812, out, MUL, ADD))
    link(ve.scalar_tensor_tensor(out, tmp, -3.0199159819567e-07, out, MUL, ADD))
    if quarter:
        link(ve.tensor_scalar(out, out, PI / 2, None, ADD))
    link(ve.tensor_scalar(out, out, 3.1415925, -3.1415925, ALU.min, MAX))


def hyena_spectrum(nc, c, ps, cst, small, vec, spec):
    sm = lambda k: small[:, SM1[k][0]:SM1[k][1]]
    v = lambda k: vec[0:HEAD, V1[k][0]:V1[k][0] + 1]
    with Stage(nc, "hy_filter") as st:
        feats = st.sb("feats", [P, T])
        window = st.sb("window", [P, NT, T])
        dft = st.sb("dft", [P, 4, 640])
        masked = st.sb("masked", [P, P])
        h1 = st.sb("h1", [HEAD, T])
        ang = st.sb("ang", [HEAD, T])
        tmp = st.sb("tmp", [HEAD, T])
        filt = st.sb("filt", [P, NT, 2, 512])
        size = st.sb("size", [P, NT, 2, 512])
        norm = st.sb("norm", [P, 512])
        consts, layer, angled, sined, filtered, windowed, sized, summed, normed, transformed, chain = (
            st.sem(n) for n in ("consts", "layer", "angled", "sined", "filtered", "windowed", "sized", "summed",
                                "normed", "transformed", "chain"))
        with st.block() as block:
            @block.sync
            def _(sp):
                sp.dma_start(feats[:, :], cst["hy_feats"]).then_inc(consts, 16)
                sp.dma_start(window[:, :, :], cst["hy_window"]).then_inc(consts, 16)
                sp.dma_start(dft[:, :, :], cst["dft_filter"]).then_inc(consts, 16)
                sp.dma_start(masked[:, :], cst["ones_but_first"]).then_inc(consts, 16)

            @block.tensor
            def _(pe):
                pe.wait_ge(consts, 64)
                pe.matmul(ps[0][0:HEAD, 0:T], sm("f_w1")[0:33, :], feats[0:33, :], start=True, stop=True)\
                    .then_inc(layer, 1)
                pe.wait_ge(sined, 1)
                pe.matmul(ps[1][0:HEAD, 0:T], sm("f_w2")[0:HEAD, :], h1[:, :], start=True, stop=True)\
                    .then_inc(layer, 1)
                pe.wait_ge(sined, 2)
                for t in range(NT):
                    for j in range(2):
                        pe.matmul(ps[2 + 2 * t + j][:, :], h1[:, t * P:(t + 1) * P],
                                  sm("f_w3")[0:HEAD, j * 512:(j + 1) * 512], start=True, stop=True)\
                            .then_inc(filtered, 1)
                pe.wait_ge(sized, 1)
                for j in range(4):
                    mm = pe.matmul(ps[6][:, :], masked[:, :] if j == 2 else c["ones"][:, :],
                                   size[:, j % 2, j // 2], start=j == 0, stop=j == 3)
                mm.then_inc(summed, 1)
                for f in range(5):
                    for j in range(4):
                        mm = pe.matmul(ps[f][:, :], dft[:, j, f * P:(f + 1) * P], filt[:, j % 2, j // 2],
                                       start=j == 0, stop=j == 3)
                    mm.then_inc(transformed, 1)

            @block.scalar
            def _(sc):
                for n in range(2):
                    sc.wait_ge(angled, n + 1)
                    sc.activation(h1[:, :], ang[:, :], ACT.Sin).then_inc(sined, 1)
                sc.wait_ge(windowed, 4)
                sc.activation(size[:, :, :, :], filt[:, :, :, :], ACT.Abs).then_inc(sized, 1)

            @block.vector
            def _(ve):
                link = Chain(ve, chain)
                for n, b in enumerate(("f_b1", "f_b2")):
                    ve.wait_ge(layer, n + 1)
                    if n:
                        ve.wait_ge(sined, n)
                    link(ve.tensor_scalar(ang[:, :], ps[n][0:HEAD, 0:T], v(b), v("f_freq"), ADD, MUL))
                    sine(ve, link, ang[:, :], ang[:, :], tmp[:, :], False)
                    ve.sem_inc(angled, 1)
                for t in range(NT):
                    for j in range(2):
                        ve.wait_ge(filtered, 2 * t + j + 1)
                        ve.tensor_tensor(filt[:, t, j].rearrange("p (o c) -> p o c", o=2),
                                         ps[2 + 2 * t + j][:, :].rearrange("p (o c) -> p o c", o=2),
                                         window[:, t].unsqueeze(1).broadcast_to([P, 2, T]), MUL)\
                            .then_inc(windowed, 1)
                ve.wait_ge(summed, 1)
                ve.reciprocal(norm[:, :], ps[6][:, :]).then_inc(normed, 1)
                ve.wait_ge(normed, 1)
                for f in range(5):
                    ve.wait_ge(transformed, f + 1)
                    ve.tensor_tensor(spec[:, f], ps[f][:, :], norm[:, :], MUL)


def long_conv(nc, c, ps, dft, inv, spec, order, z, bias, gate, out):
    with Stage(nc, "long_conv") as st:
        zt = st.sb("zt", [P, NT, T])
        f1 = st.sb("f1", [P, 4, T])
        f2 = st.sb("f2", [P, 4, T])
        turned, copied, transformed, mixed, inverse, gated, products = (
            st.sem(n) for n in ("turned", "copied", "transformed", "mixed", "inverse", "gated", "products"))
        s = lambda f: spec[:, f, order * T:(order + 1) * T]
        with st.block() as block:
            @block.tensor
            def _(pe):
                for t in range(NT):
                    for ch in range(2):
                        mm = pe.transpose(ps[0][:, (2 * t + ch) * P:(2 * t + ch + 1) * P],
                                          z[:, ch, t * P:(t + 1) * P], c["ident"][:, :])
                mm.then_inc(turned, 1)
                pe.wait_ge(copied, 1)
                for f in range(4):
                    for t in range(NT):
                        mm = pe.matmul(ps[1 + f][:, 0:T], dft[:, t, f * P:(f + 1) * P], zt[:, t],
                                       start=t == 0, stop=t == NT - 1)
                mm.then_inc(transformed, 1)
                pe.wait_ge(mixed, 1)
                for ch in range(2):
                    for f in range(4):
                        mm = pe.matmul(ps[5 + ch][:, 0:T], f1[:, f, ch * P:(ch + 1) * P], inv[:, f],
                                       start=f == 0, stop=f == 3)
                    mm.then_inc(inverse, 1)

            @block.vector
            def _(ve):
                ve.wait_ge(turned, 1)
                ve.tensor_copy(zt[:, :, :], ps[0][:, :].rearrange("p (a b) -> p a b", b=T)).then_inc(copied, 1)
                ve.wait_ge(transformed, 1)
                for f in range(2):
                    last = 4 if f == 0 else 1
                    ve.tensor_tensor(f1[:, f], ps[1 + f][:, 0:T], s(f), MUL)
                    ve.tensor_tensor(f2[:, f], ps[3 + f][:, 0:T], s(2 + f), MUL)
                    ve.tensor_tensor(f1[:, 2 + f], ps[3 + f][:, 0:T], s(last), MUL)
                    ve.tensor_tensor(f2[:, 2 + f], ps[1 + f][:, 0:T], s(2 + f), MUL).then_inc(products, 1)
                ve.wait_ge(products, 2)
                ve.tensor_tensor(f1[:, 0:2], f1[:, 0:2], f2[:, 0:2], SUB)
                ve.tensor_tensor(f1[:, 2:4], f1[:, 2:4], f2[:, 2:4], ADD).then_inc(mixed, 1)
                for ch in range(2):
                    ve.wait_ge(inverse, ch + 1)
                    ve.scalar_tensor_tensor(out[:, ch], z[:, ch], bias[:, ch:ch + 1], ps[5 + ch][:, 0:T], MUL, ADD)\
                        .then_inc(gated, 1)
                    ve.wait_ge(gated, ch + 1)
                    ve.tensor_tensor(out[:, ch], out[:, ch], gate[:, ch], MUL)


def fourier(nc, c, ps, cst, u, out):
    with Stage(nc, "fourier") as st:
        chan = st.sb("chan", [P, 2 * P])
        token = st.sb("token", [P, NT, 512])
        mid = st.sb("mid", [P, 2, NT, 2 * P])
        consts, first, copied, second = (st.sem(n) for n in ("consts", "first", "copied", "second"))
        with st.block() as block:
            @block.sync
            def _(sp):
                sp.dma_start(chan[:, :], cst["fn_channel"]).then_inc(consts, 16)
                sp.dma_start(token[:, :, :], cst["fn_token"]).then_inc(consts, 16)

            @block.tensor
            def _(pe):
                pe.wait_ge(consts, 32)
                for ch in range(2):
                    for t in range(NT):
                        pe.matmul(ps[2 * ch + t][:, 0:2 * P], u[:, ch, t * P:(t + 1) * P], chan[:, :],
                                  start=True, stop=True).then_inc(first, 1)
                pe.wait_ge(copied, 4)
                for ch in range(2):
                    for n, (t, part) in enumerate((t, part) for t in range(NT) for part in range(2)):
                        mm = pe.matmul(ps[4 + ch][:, 0:T], mid[:, ch, t, part * P:(part + 1) * P],
                                       token[:, t, part * T:(part + 1) * T], start=n == 0, stop=n == 3)
                    mm.then_inc(second, 1)

            @block.scalar
            def _(sc):
                for ch in range(2):
                    for t in range(NT):
                        sc.wait_ge(first, 2 * ch + t + 1)
                        sc.activation(mid[:, ch, t], ps[2 * ch + t][:, 0:2 * P], ACT.Copy).then_inc(copied, 1)
                for ch in range(2):
                    sc.wait_ge(second, ch + 1)
                    sc.activation(out[:, ch], ps[4 + ch][:, 0:T], ACT.Copy)


def first_mixer(nc, c, ps, ring, I, cst, vec, xT, hT, mod):
    v = lambda k, j=0, n=1: vec[:, V1[k][0] + j:V1[k][0] + j + n]
    with Stage(nc, "mixer") as mx:
        spec = mx.sb("spec", [P, 5, 512])
        with Stage(nc, "filters") as st:
            small = st.sb("small", [P, SM1_COLS])
            load_all(nc, [(small[:, :], I["small1"])])
            hyena_spectrum(nc, c, ps, cst, small, vec, spec)
        proj = mx.sb("proj", [P, 36, T])
        mix = mx.sb("mix", [P, 8, T])
        with Stage(nc, "qkv") as st:
            kv = st.sb("kv", [P, 2, 2 * T])
            with Stage(nc, "w_kv") as s2:
                def mm(pe, q, u, w):
                    for j in range(2):
                        for k in range(KD):
                            m = pe.matmul(ps[j][:, :], w[:, j * KD + k], hT[:, k], start=k == 0, stop=k == KD - 1)
                    return m

                def act(sc, q, u):
                    sc.activation(kv[:, 0], ps[0][:, :], ACT.Copy)
                    return sc.activation(kv[:, 1], ps[1][:, :], ACT.Copy)

                stream(nc, s2, ring, I["w_kv"], 1, 1, 16, mm, act)
            with Stage(nc, "w_in") as s2:
                def mm(pe, q, u, w):
                    for j in range(2):
                        for k in range(KD):
                            m = pe.matmul(ps[u % 2][:, j * T:(j + 1) * T], w[:, j * KD + k], hT[:, k, 0:T],
                                          start=k == 0, stop=k == KD - 1)
                    return m

                def act(sc, q, u):
                    return sc.activation(pairs[:, q], ps[u % 2][:, :], ACT.Copy)

                pairs = proj[:, :, :].rearrange("p (q a) t -> p q (a t)", a=2)
                stream(nc, s2, ring, I["w_in"], 3, 6, 16, mm, act)
            axial = st.sb("axial", [P, 2, T])
            perm = st.sb("perm", [P, 2, P])
            k_other = st.sb("k_other", [P, 2 * T])
            v_tok = st.sb("v_tok", [P, 4, P])
            load_all(nc, [(axial[:, 0], cst["axial_cos"]), (axial[:, 1], cst["axial_sin"]),
                          (perm[:, 0], cst["swap_pair"]), (perm[:, 1], cst["swap_head"])])
            head_rms(nc, c, ps, proj[:, 0:4], 4, T, v("q_gain"), HEAD ** -0.5)
            head_rms(nc, c, ps, kv[:, 0:1], 1, 2 * T, v("k_gain"), 1.0)
            rotate(nc, c, ps, proj[:, 0:4], 4, P, perm[:, 0], axial[:, 0], axial[:, 1])
            rotate(nc, c, ps, kv[:, 0:1, 0:T], 1, P, perm[:, 0], axial[:, 0], axial[:, 1])
            turn_tokens(nc, c, ps, lambda j: kv[:, 1, j * P:(j + 1) * P], 4, lambda g: v_tok[:, :, :])
            with Stage(nc, "k_other") as s2:
                swapped = s2.sem("swapped")
                with s2.block() as block:
                    @block.tensor
                    def _(pe):
                        pe.matmul(ps[0][:, :], perm[:, 1], kv[:, 0], start=True, stop=True).then_inc(swapped, 1)

                    @block.vector
                    def _(ve):
                        ve.wait_ge(swapped, 1)
                        ve.tensor_copy(k_other[:, :], ps[0][:, :])

            def q_of(h, t):
                b = h % 2 * HEAD
                return proj[b:b + HEAD, h // 2, t * P:(t + 1) * P]

            def k_of(h):
                b = h % 2 * HEAD
                return kv[b:b + HEAD, 0] if h // 4 == h % 2 else k_other[b:b + HEAD, :]

            attention(nc, c, ps, q_of, k_of, lambda h, j: v_tok[:, j, h // 4 * HEAD:(h // 4 + 1) * HEAD],
                      lambda h: (h % 2 * HEAD, mix[h % 2 * HEAD:h % 2 * HEAD + HEAD, h // 2]), 8, 2 * T)

        with Stage(nc, "hyena") as st:
            u = st.sb("u", [P, 6, T])
            dft = st.sb("dft", [P, NT, 512])
            inv = st.sb("inv", [P, 4, T])
            load_all(nc, [(dft[:, :, :], cst["dft_signal"]), (inv[:, :, :], cst["dft_inverse"])])
            with Stage(nc, "short_conv") as s2:
                mid, ahead = s2.sem("mid"), s2.sem("ahead")
                with s2.block() as block:
                    @block.vector
                    def _(ve):
                        for j in range(6):
                            x = proj[:, 4 + j]
                            ve.tensor_scalar(u[:, j], x, v("short_w", 6 + j), v("short_b", j), MUL, ADD)\
                                .then_inc(mid, 1)
                            ve.wait_ge(mid, j + 1)
                            ve.scalar_tensor_tensor(u[:, j, 1:T], x[:, 0:T - 1], v("short_w", j), u[:, j, 1:T],
                                                    MUL, ADD).then_inc(ahead, 1)
                            ve.wait_ge(ahead, j + 1)
                            ve.scalar_tensor_tensor(u[:, j, 0:T - 1], x[:, 1:T], v("short_w", 12 + j),
                                                    u[:, j, 0:T - 1], MUL, ADD)
            z = st.sb("z", [P, 2, T])
            long_conv(nc, c, ps, dft, inv, spec, 0, u[:, 0:2], v("hy_bias", 0, 2), u[:, 2:4], z)
            long_conv(nc, c, ps, dft, inv, spec, 1, z, v("hy_bias", 2, 2), u[:, 4:6], mix[:, 4:6])
        fourier(nc, c, ps, cst, proj[:, 10:12], mix[:, 6:8])

        with Stage(nc, "merge") as st:
            merged = st.sb("merged", [P, KD, T])
            part = st.sb("part", [P, 2, 3, T])
            with st.block() as block:
                @block.scalar
                def _(sc):
                    sc.activation(proj[:, 12:36], proj[:, 12:36], ACT.Sigmoid)
            with Stage(nc, "w_branch") as s2:
                summed = s2.sem("summed")

                def mm(pe, q, u, w):
                    for j in range(2):
                        for b, (lo, hi) in enumerate(((0, 4), (4, 6), (6, 8))):
                            bank = ps[4 * (u % 2) + b]
                            for k in range(lo, hi):
                                m = pe.matmul(bank[:, j * T:(j + 1) * T], w[:, j * KD + k], mix[:, k],
                                              start=k == lo, stop=k == hi - 1)
                    return m

                def dve(ve, q, u):
                    for j in range(2):
                        n = 2 * q + j
                        for b in range(3):
                            m = ve.tensor_tensor(part[:, j, b], ps[4 * (u % 2) + b][:, j * T:(j + 1) * T],
                                                 proj[:, 12 + b * KD + n], MUL)
                        m.then_inc(summed, 1)
                        ve.wait_ge(summed, 2 * n + 1)
                        ve.tensor_tensor(part[:, j, 0], part[:, j, 0], part[:, j, 1], ADD).then_inc(summed, 1)
                        ve.wait_ge(summed, 2 * n + 2)
                        m = ve.tensor_tensor(merged[:, n], part[:, j, 0], part[:, j, 2], ADD)
                    return m

                stream(nc, s2, ring, I["w_branch"], 1, 4, 16, mm, dve=dve)
            add_projection(nc, ring, ps, I["w_out"], 4, merged, xT, mod[:, 16:24, 0])


def add_projection(nc, ring, ps, src, n_panels, x, xT, gate):
    with Stage(nc, "w_out") as st:
        def mm(pe, q, u, w):
            for j in range(2):
                for k in range(KD):
                    m = pe.matmul(ps[u % 2][:, j * T:(j + 1) * T], w[:, j * KD + k], x[:, k],
                                  start=k == 0, stop=k == KD - 1)
            return m

        def dve(ve, q, u):
            for j in range(2):
                n = 2 * q + j
                m = ve.scalar_tensor_tensor(xT[:, n], ps[u % 2][:, j * T:(j + 1) * T], gate[:, n:n + 1], xT[:, n],
                                            MUL, ADD)
            return m

        stream(nc, st, ring, src, 1, n_panels, 16, mm, dve=dve)


def route(nc, c, ps, cst, router, hT, place_of, x_sel):
    with Stage(nc, "route") as st:
        e1 = st.sb("e1", [P, NT, E])
        top = st.sb("top", [P, NT])
        tot = st.sb("tot", [P, NT])
        aff = st.sb("aff", [P, NT, E])
        affT = st.sb("affT", [E, T])
        left = st.sb("left", [E, T])
        best = st.sb("best", [E, 8])
        mask = st.sb("mask", [E, T])
        place = st.sb("place", [E, T])
        zero = st.sb("zero", [E, T])
        placeT = st.sb("placeT", [P, NT, E])
        slots = st.sb("slots", [P, CAP])
        h_tok = st.sb("h_tok", [P, NT, D])
        sel = st.sb("sel", [P, NT, E, CAP])
        w_tok = st.sb("w_tok", [P, NT, E, 4, CAP])
        logits, highest, exped, shared, turned, chain, placed, placed_t, chosen, loaded = (
            st.sem(n) for n in ("logits", "highest", "exped", "shared", "turned", "chain", "placed", "placed_t",
                                "chosen", "loaded"))
        with st.block() as block:
            @block.sync
            def _(sp):
                sp.dma_start(slots[:, :], cst["slots"]).then_inc(loaded, 16)

            @block.tensor
            def _(pe):
                for t in range(NT):
                    for k in range(KD):
                        mm = pe.matmul(ps[0][:, t * E:(t + 1) * E], hT[:, k, t * P:(t + 1) * P],
                                       router[:, k * E:(k + 1) * E], start=k == 0, stop=k == KD - 1)
                mm.then_inc(logits, 1)
                pe.wait_ge(shared, 1)
                for t in range(NT):
                    mm = pe.transpose(ps[1][0:E, t * P:(t + 1) * P], aff[:, t], c["ident"][:, :])
                mm.then_inc(turned, 1)
                pe.wait_ge(placed, 1)
                for t in range(NT):
                    mm = pe.transpose(ps[2][:, t * E:(t + 1) * E], place[:, t * P:(t + 1) * P],
                                      c["ident"][0:E, 0:E])
                mm.then_inc(placed_t, 1)

            @block.scalar
            def _(sc):
                for t in range(NT):
                    sc.wait_ge(highest, NT)
                    sc.activation(e1[:, t], ps[0][:, t * E:(t + 1) * E], ACT.Exp, bias=top[:, t:t + 1],
                                  accum_out=tot[:, t:t + 1]).then_inc(exped, 1)

            @block.vector
            def _(ve):
                link = Chain(ve, chain)
                link(ve.memset(zero[:, :], 0.0))
                ve.wait_ge(logits, 1)
                for t in range(NT):
                    ve.tensor_reduce(top[:, t:t + 1], ps[0][:, t * E:(t + 1) * E], AX.X, MAX, negate=True)\
                        .then_inc(highest, 1)
                ve.wait_ge(exped, NT)
                link(ve.reciprocal(tot[:, :], tot[:, :]))
                for t in range(NT):
                    link(ve.tensor_scalar(aff[:, t], e1[:, t], tot[:, t:t + 1], None, MUL))
                ve.sem_inc(shared, 1)
                ve.wait_ge(turned, 1)
                link(ve.tensor_copy(affT[:, :], ps[1][0:E, 0:T]))
                link(ve.tensor_copy(left[:, :], ps[1][0:E, 0:T]))
                for _ in range(CAP // 8):
                    link(ve.max(best[:, :], left[:, :]))
                    link(ve.match_replace(left[:, :], best[:, :], left[:, :], -1.0))
                link(ve.tensor_tensor(mask[:, :], affT[:, :], left[:, :], ALU.not_equal))
                link(ve.tensor_tensor_scan(place[:, :], mask[:, :], zero[:, :], 0.0, ADD, ADD))
                link(ve.tensor_tensor(place[:, :], place[:, :], mask[:, :], MUL))
                ve.sem_inc(placed, 1)
                ve.wait_ge(placed_t, 1)
                link(ve.tensor_copy(placeT[:, :, :], ps[2][:, 0:NT * E].rearrange("p (a b) -> p a b", b=E)))
                ve.wait_ge(loaded, 16)
                for t in range(NT):
                    at = placeT[:, t].unsqueeze(2).broadcast_to([P, E, CAP])
                    link(ve.tensor_tensor(sel[:, t], at, slots[:, :].unsqueeze(1).broadcast_to([P, E, CAP]),
                                          ALU.is_equal))
                    for g in range(4):
                        ve.tensor_tensor(w_tok[:, t, :, g], sel[:, t],
                                         aff[:, t].unsqueeze(2).broadcast_to([P, E, CAP]), MUL)
        turn_tokens(nc, c, ps, lambda j: hT[:, j % KD, (j // KD) * P:(j // KD + 1) * P], NT * KD,
                    lambda g: h_tok[:, g // 2, (g % 2) * 512:(g % 2 + 1) * 512]
                    .rearrange("p (k n) -> p k n", n=P))
        turn_tokens(nc, c, ps, lambda j: w_tok[:, j % 2, j // 2].rearrange("p a b -> p (a b)"), NT * E,
                    lambda g: place_of[:, 2 * g:2 * g + 2].rearrange("p g (t n) -> p (g t) n", n=P))
        gathered = st.sem("gathered")
        with st.block() as block:
            @block.tensor
            def _(pe):
                for k in range(KD):
                    for t in range(NT):
                        mm = pe.matmul(ps[k][:, :], h_tok[:, t, k * P:(k + 1) * P],
                                       sel[:, t].rearrange("p a b -> p (a b)"), start=t == 0, stop=t == NT - 1)
                    mm.then_inc(gathered, 1)

            @block.vector
            def _(ve):
                for k in range(KD):
                    ve.wait_ge(gathered, k + 1)
                    ve.tensor_copy(x_sel[:, k], ps[k][:, :])


def experts(nc, c, ps, ring, src, x_sel, place, xT, gate):
    up_panels, down_panels = KD, 4
    slots, n = 6, KD + 4
    cols = 4 * D
    with Stage(nc, "experts") as st:
        x_cur = st.sb("x_cur", [P, KD, CAP])
        silu = st.sb("silu", [P, 512])
        hid = st.sb("hid", [P, 512])
        hidT = st.sb("hidT", [P, 4, 4, CAP])
        y = st.sb("y", [P, D])
        loaded = [st.sem(f"loaded{u}") for u in range(slots)]
        x_ready, panel_done, silu_done, hid_done, turned, turned_out, y_low, y_high, placed, added = (
            st.sem(k) for k in ("x_ready", "panel_done", "silu_done", "hid_done", "turned", "turned_out", "y_low",
                                "y_high", "placed", "added"))
        slot = [ring[:, u * cols:(u + 1) * cols] for u in range(slots)]
        xs = x_sel.rearrange("p k (e s) -> p k e s", s=CAP)
        quarter = [slice(g * CAP, (g + 1) * CAP) for g in range(4)]
        with st.block() as block:
            @block.sync
            def _(sp):
                for u in range(slots):
                    sp.dma_start(slot[u], src[0, u]).then_inc(loaded[u], 16)
                for u in range(slots, n):
                    sp.wait_ge(panel_done, u + 1 - slots)
                    sp.dma_start(slot[u % slots], src[0, u]).then_inc(loaded[u % slots], 16)
                with sp.Fori(1, E) as e:
                    for u in range(n):
                        sp.wait_ge(panel_done, e * n + (u + 1 - slots))
                        sp.dma_start(slot[u % slots], src[e, u]).then_inc(loaded[u % slots], 16)

            @block.tensor
            def _(pe):
                with pe.Fori(0, E) as e:
                    pe.wait_ge(x_ready, e + 1)
                    for u in range(up_panels):
                        w = slot[u % slots].rearrange("p (b g n) -> p b g n", b=2, g=4)
                        pe.wait_ge(loaded[u % slots], e * 32 + (u // slots + 1) * 16)
                        for b in range(2):
                            for g in range(4):
                                mm = pe.matmul(ps[b][quarter[g], :], x_cur[:, u], w[:, b, g], start=u == 0,
                                               stop=u == up_panels - 1)
                        mm.then_inc(panel_done, 1)
                    pe.wait_ge(hid_done, e + 1)
                    for s in range(4):
                        mm = pe.transpose(ps[4][:, s * P:(s + 1) * P], hid[:, s * P:(s + 1) * P], c["ident"])
                    mm.then_inc(turned, 1)
                    pe.wait_ge(turned_out, e + 1)
                    for s in range(down_panels):
                        u = up_panels + s
                        w = slot[u % slots].rearrange("p (g b n) -> p g b n", g=4, b=2)
                        pe.wait_ge(loaded[u % slots], e * 32 + (u // slots + 1) * 16)
                        for b in range(2):
                            for g in range(4):
                                mm = pe.matmul(ps[2 + b][quarter[g], :], hidT[:, s, g], w[:, g, b], start=s == 0,
                                               stop=s == down_panels - 1)
                        mm.then_inc(panel_done, 1)
                    pe.wait_ge(y_low, e + 1)
                    pe.wait_ge(y_high, e + 1)
                    for half in range(2):
                        pe.wait_ge(added, e * 2 + (half + 1))
                        for j in range(4):
                            k = 4 * half + j
                            mm = pe.matmul(ps[5 + j // 2][:, (j % 2) * T:(j % 2 + 1) * T], y[:, k * P:(k + 1) * P],
                                           place[:, e], start=True, stop=True)
                        mm.then_inc(placed, 1)

            @block.scalar
            def _(sc):
                with sc.Fori(0, E) as e:
                    sc.activation(x_cur, xs[:, :, e], ACT.Copy).then_inc(x_ready, 1)
                    sc.wait_ge(panel_done, e * n + up_panels)
                    sc.activation(silu, ps[0], ACT.Silu).then_inc(silu_done, 1)
                    sc.wait_ge(turned, e + 1)
                    sc.activation(hidT.rearrange("p s g c -> p (s g c)"), ps[4], ACT.Copy).then_inc(turned_out, 1)
                    sc.wait_ge(panel_done, e * n + n)
                    sc.activation(y[:, 0:512], ps[2], ACT.Copy).then_inc(y_low, 1)

            @block.vector
            def _(ve):
                ve.sem_inc(added, 1)
                with ve.Fori(0, E) as e:
                    ve.wait_ge(silu_done, e + 1)
                    ve.tensor_tensor(hid, ps[1], silu, MUL).then_inc(hid_done, 1)
                    ve.wait_ge(panel_done, e * n + n)
                    ve.tensor_copy(y[:, 512:D], ps[3]).then_inc(y_high, 1)
                    for half in range(2):
                        ve.wait_ge(placed, e * 2 + (half + 1))
                        for j in range(4):
                            k = 4 * half + j
                            m = ve.scalar_tensor_tensor(xT[:, k], ps[5 + j // 2][:, (j % 2) * T:(j % 2 + 1) * T],
                                                        gate[:, k:k + 1], xT[:, k], MUL, ADD)
                        m.then_inc(added, 1)


def first_block(nc, c, ps, ring, I, cst, vec, cond, xT, hT):
    v = lambda k: vec[:, V1[k][0]:V1[k][1]]
    with Stage(nc, "first") as st:
        mod = st.sb("mod", [P, 48, 2])
        gain = st.sb("gain", [P, 3, KD])
        with Stage(nc, "context") as s2:
            ctxT = s2.sb("ctxT", [P, KD, T])
            turn_features(nc, c, ps, [I["x"], I["ctx"]], [xT, ctxT])
            modulation(nc, s2, c, ring, ps, I["w_mod"], 4, cond, (0, 1), mod, v("b_mod"))
            with s2.block() as block:
                @block.vector
                def _(ve):
                    for j in range(2):
                        ve.scalar_tensor_tensor(gain[:, j], mod[:, 8:16, j], 1.0, v("norm1"), ADD, MUL)
                    ve.scalar_tensor_tensor(gain[:, 2], mod[:, 32:40, 0], 1.0, v("norm2"), ADD, MUL)
            norm_modulate(nc, c, ps, [(xT, hT[:, :, 0:T], gain[:, 0], mod[:, 0:8, 0]),
                                      (ctxT, hT[:, :, T:2 * T], gain[:, 1], mod[:, 0:8, 1])])
        first_mixer(nc, c, ps, ring, I, cst, vec, xT, hT, mod)
        norm_modulate(nc, c, ps, [(xT, hT[:, :, 0:T], gain[:, 2], mod[:, 24:32, 0])])
        with Stage(nc, "moe") as s2:
            place = s2.sb("place", [P, E, T])
            x_sel = s2.sb("x_sel", [P, KD, 512])
            with Stage(nc, "choose") as s3:
                router = s3.sb("router", [P, KD * E])
                load_all(nc, [(router, I["small1"][:, SM1["router"][0]:SM1["router"][1]])])
                route(nc, c, ps, cst, router, hT, place, x_sel)
            experts(nc, c, ps, ring, I["w_expert"], x_sel, place, xT, mod[:, 40:48, 0])
        norm_modulate(nc, c, ps, [(xT, xT, v("final_g"), None)])


class Arena:

    def __init__(self, ring):
        self.ring, self.at = ring, 0

    def take(self, *dims, rows=P):
        n = 1
        for d in dims:
            n *= d
        a = self.ring[0:rows, self.at:self.at + n]
        self.at += n
        assert self.at <= RING_COLS
        if len(dims) == 1:
            return a
        names = "abcd"[:len(dims)]
        return a.rearrange(f"p ({' '.join(names)}) -> p {' '.join(names)}", **dict(zip(names[1:], dims[1:])))


def rotary_tables(nc, cst, positions, tables):
    with Stage(nc, "rotary") as st:
        pos_i = st.sb("pos_i", [P, T], I32)
        pos = st.sb("pos", [P, T])
        freq = st.sb("freq", [P, 6])
        ang = st.sb("ang", [P, 3, 2, T])
        tmp = st.sb("tmp", [P, T])
        landed, chain, angles, sines = (st.sem(n) for n in ("landed", "chain", "angles", "sines"))
        with st.block() as block:
            @block.sync
            def _(sp):
                sp.dma_start(pos_i, positions).then_inc(landed, 16)
                sp.dma_start(freq, cst["rot_freq"]).then_inc(landed, 16)

            @block.vector
            def _(ve):
                link = Chain(ve, chain)
                ve.wait_ge(landed, 32)
                link(ve.tensor_copy(pos, pos_i))
                for j in range(3):
                    link(ve.tensor_scalar(ang[:, j, 0], pos, freq[:, 2 * j:2 * j + 1], None, MUL))
                    sine(ve, link, ang[:, j, 1], ang[:, j, 0], tmp, False)
                    sine(ve, link, tables[:, j, 0], ang[:, j, 0], tmp, True)
                ve.sem_inc(angles, 1)
                ve.wait_ge(sines, 1)
                for j in range(3):
                    ve.tensor_scalar(tables[:, j, 1], ang[:, j, 0], freq[:, 2 * j + 1:2 * j + 2], None, MUL)

            @block.scalar
            def _(sc):
                sc.wait_ge(angles, 1)
                for j in range(3):
                    sc.activation(ang[:, j, 0], ang[:, j, 1], ACT.Sin)
                    m = sc.activation(tables[:, j, 0], tables[:, j, 0], ACT.Sin)
                m.then_inc(sines, 1)


def feed_forward(nc, c, ps, ring, w_in, w_out, xT, hT, gate):
    with Stage(nc, "ff") as st:
        hid = st.sb("hid", [P, KF, T])
        silu = st.sb("silu", [P, 2, T])
        with Stage(nc, "ff_in") as s2:
            def mm(pe, q, u, w):
                for j in range(2):
                    for k in range(KD):
                        m = pe.matmul(ps[u % 2][:, j * T:(j + 1) * T], w[:, j * KD + k], hT[:, k, 0:T],
                                      start=k == 0, stop=k == KD - 1)
                return m

            def act(sc, q, u):
                return sc.activation(silu[:, u % 2], ps[u % 2][:, 0:T], ACT.Silu)

            def dve(ve, q, u):
                return ve.tensor_tensor(hid[:, q], ps[u % 2][:, T:2 * T], silu[:, u % 2], MUL)

            stream(nc, s2, ring, w_in, 2, KF // 2, 16, mm, act, dve)
        with Stage(nc, "ff_out") as s2:
            def mm(pe, q, u, w):
                for k in range(KF):
                    m = pe.matmul(ps[u % 2][:, 0:T], w[:, k], hid[:, k], start=k == 0, stop=k == KF - 1)
                return m

            def dve(ve, q, u):
                return ve.scalar_tensor_tensor(xT[:, q], ps[u % 2][:, 0:T], gate[:, q:q + 1], xT[:, q], MUL, ADD)

            stream(nc, s2, ring, w_out, 1, KD, KF, mm, dve=dve)


def head_sums(pe, c, bank, x):
    return pe.matmul(bank[:, 0:512], c["ones_head"], x.rearrange("p a b -> p (a b)"), start=True, stop=True)


def head_norm(nc, c, ps, ar, x, eps, gain, bias, out):
    with Stage(nc, "head_norm") as st:
        sq = ar.take(2, T)
        root = ar.take(2, T)
        flat = lambda a: a.rearrange("p a b -> p (a b)")
        meaned, centred, squared, summed, rooted, chain = (
            st.sem(n) for n in ("meaned", "centred", "squared", "summed", "rooted", "chain"))
        with st.block() as block:
            @block.tensor
            def _(pe):
                head_sums(pe, c, ps[0], x).then_inc(meaned, 1)
                pe.wait_ge(squared, 1)
                head_sums(pe, c, ps[1], sq).then_inc(summed, 1)

            @block.scalar
            def _(sc):
                sc.wait_ge(centred, 1)
                sc.activation(sq, x, ACT.Square).then_inc(squared, 1)
                sc.wait_ge(summed, 1)
                sc.activation(flat(root), ps[1], ACT.Sqrt, bias=eps, scale=1.0 / HEAD).then_inc(rooted, 1)

            @block.vector
            def _(ve):
                link = Chain(ve, chain)
                ve.wait_ge(meaned, 1)
                ve.scalar_tensor_tensor(flat(x), ps[0], -1.0 / HEAD, flat(x), MUL, ADD).then_inc(centred, 1)
                ve.wait_ge(rooted, 1)
                link(ve.reciprocal(flat(root), flat(root)))
                link(ve.tensor_tensor(x, x, root, MUL))
                for j in range(2):
                    if bias is None:
                        ve.tensor_scalar(out[:, j], x[:, j], gain[:, j:j + 1], None, MUL)
                    else:
                        ve.tensor_scalar(out[:, j], x[:, j], gain[:, j:j + 1], bias[:, j:j + 1], MUL, ADD)


def retention(nc, c, ps, ring, cst, proj, tables, vec, out):
    v = lambda k: vec[:, V2[k][0]:V2[k][1]]
    ar = Arena(ring)
    rel = ar.take(2, NT, T)
    lg = ar.take(8)
    decay = ar.take(4, NT, T)
    score = ar.take(4, NT, T)
    v_tok = ar.take(NT, T)
    y = ar.take(2, T)
    perm = ar.take(P)
    load_all(nc, [(rel[:, 0], cst["ahead"]), (rel[:, 1], cst["behind"]), (perm, cst["swap_half"])])
    rotate(nc, c, ps, proj[:, 14:18], 4, P, perm, tables[:, 0, 0], tables[:, 0, 1])
    turn_tokens(nc, c, ps, lambda j: proj[:, 18 + j % 2, (j // 2) * P:(j // 2 + 1) * P], 4,
                lambda g: v_tok.rearrange("p t (k n) -> p (t k) n", n=P))
    with Stage(nc, "retention") as st:
        rated, signed, spread, decayed, scored, weighted, mixed = (
            st.sem(n) for n in ("rated", "signed", "spread", "decayed", "scored", "weighted", "mixed"))
        with st.block() as block:
            @block.scalar
            def _(sc):
                sc.activation(lg, v("log_rate"), ACT.Exp).then_inc(rated, 1)
                for h in range(4):
                    sc.wait_ge(spread, 2 * h + 2)
                    sc.activation(decay[:, h], decay[:, h], ACT.Exp).then_inc(decayed, 1)

            @block.tensor
            def _(pe):
                for h in range(4):
                    b = slice(h % 2 * HEAD, h % 2 * HEAD + HEAD)
                    for t in range(NT):
                        mm = pe.matmul(ps[h][:, t * T:(t + 1) * T], proj[b, 16 + h // 2, t * P:(t + 1) * P],
                                       proj[b, 14 + h // 2], start=True, stop=True)
                    mm.then_inc(scored, 1)
                for h in range(4):
                    b = slice(h % 2 * HEAD, h % 2 * HEAD + HEAD)
                    pe.wait_ge(weighted, h + 1)
                    for t in range(NT):
                        mm = pe.matmul(ps[4 + h // 2][b, 0:T], v_tok[:, t, h * HEAD:(h + 1) * HEAD], score[:, h, t],
                                       start=t == 0, stop=t == NT - 1)
                    mm.then_inc(mixed, 1)

            @block.vector
            def _(ve):
                ve.wait_ge(rated, 1)
                ve.tensor_scalar(lg, lg, -1.0, None, MUL).then_inc(signed, 1)
                ve.wait_ge(signed, 1)
                for h in range(4):
                    ve.tensor_scalar(decay[:, h], rel[:, 0], lg[:, h:h + 1], None, MUL).then_inc(spread, 1)
                    ve.wait_ge(spread, 2 * h + 1)
                    ve.scalar_tensor_tensor(decay[:, h], rel[:, 1], lg[:, 4 + h:5 + h], decay[:, h], MUL, ADD)\
                        .then_inc(spread, 1)
                for h in range(4):
                    ve.wait_ge(decayed, h + 1)
                    ve.wait_ge(scored, h + 1)
                    ve.scalar_tensor_tensor(score[:, h], ps[h].rearrange("p (a b) -> p a b", b=T), HEAD ** -0.5,
                                            decay[:, h], MUL, MUL).then_inc(weighted, 1)
                for j in range(2):
                    ve.wait_ge(mixed, 2 * j + 2)
                    ve.tensor_copy(y[:, j], ps[4 + j][:, 0:T])
    head_norm(nc, c, ps, ar, y, c["eps"][:, 1:2], v("gn_g"), None, y)
    with Stage(nc, "ret_gate") as st:
        opened = st.sem("opened")
        with st.block() as block:
            @block.scalar
            def _(sc):
                sc.activation(proj[:, 20:22], proj[:, 20:22], ACT.Silu).then_inc(opened, 1)

            @block.vector
            def _(ve):
                ve.wait_ge(opened, 1)
                ve.tensor_tensor(out, y, proj[:, 20:22], MUL)


def latent_attention(nc, c, ps, ring, cst, proj, tables, vec, small, out):
    v = lambda k: vec[:, V2[k][0]:V2[k][1]]
    w_uq = small[:, SM2["w_uq"][0]:SM2["w_uq"][1]].rearrange("p (k n) -> p k n", k=3)
    w_ukv = small[:, SM2["w_ukv"][0]:SM2["w_ukv"][1]].rearrange("p (k n) -> p k n", k=2)
    ar = Arena(ring)
    sq = ar.take(5, T)
    root = ar.take(2, T)
    q = ar.take(8, T, rows=96)
    k = ar.take(8, T, rows=96)
    v_tok = ar.take(NT, 512)
    perm = ar.take(P)
    perm_k = ar.take(P)
    load_all(nc, [(perm, cst["swap_mla"]), (perm_k, cst["swap_kpe"])])
    rotate(nc, c, ps, proj[0:32, 22:23], 1, 32, perm_k[0:32, 0:32], tables[0:32, 2, 0], tables[0:32, 2, 1])
    with Stage(nc, "latent_norm") as st:
        squared, summed, rooted, inverted, scaled, projected, copied = (
            st.sem(n) for n in ("squared", "summed", "rooted", "inverted", "scaled", "projected", "copied"))
        groups = ((9, 3, "mla_q_g"), (12, 2, "mla_kv_g"))
        with st.block() as block:
            @block.scalar
            def _(sc):
                sc.activation(sq, proj[:, 9:14], ACT.Square).then_inc(squared, 1)
                for g, (_, n, _) in enumerate(groups):
                    sc.wait_ge(summed, g + 1)
                    sc.activation(root[:, g], ps[g][:, 0:T], ACT.Sqrt, bias=c["eps"][:, 0:1], scale=1.0 / (n * P))\
                        .then_inc(rooted, 1)

            @block.tensor
            def _(pe):
                pe.wait_ge(squared, 1)
                for g, (at, n, _) in enumerate(groups):
                    for j in range(n):
                        mm = pe.matmul(ps[g][:, 0:T], c["ones"], sq[:, at - 9 + j], start=j == 0, stop=j == n - 1)
                    mm.then_inc(summed, 1)

            @block.vector
            def _(ve):
                for g, (at, n, gain) in enumerate(groups):
                    ve.wait_ge(rooted, g + 1)
                    ve.reciprocal(root[:, g], root[:, g]).then_inc(inverted, 1)
                    ve.wait_ge(inverted, g + 1)
                    for j in range(n):
                        ve.scalar_tensor_tensor(proj[:, at + j], proj[:, at + j], v(gain)[:, j:j + 1], root[:, g],
                                                MUL, MUL).then_inc(scaled, 1)
        with st.block() as block:
            @block.tensor
            def _(pe):
                for h in range(8):
                    if h >= 4:
                        pe.wait_ge(copied, 2 * (h - 4) + 1)
                    for j in range(3):
                        mm = pe.matmul(ps[h % 4][0:96, 0:T], w_uq[:, j, h * 96:(h + 1) * 96], proj[:, 9 + j],
                                       start=j == 0, stop=j == 2)
                    mm.then_inc(projected, 1)
                    if h >= 4:
                        pe.wait_ge(copied, 2 * (h - 4) + 2)
                    for j in range(2):
                        mm = pe.matmul(ps[4 + h % 4][0:HEAD, 0:T], w_ukv[:, j, h * P:h * P + HEAD], proj[:, 12 + j],
                                       start=j == 0, stop=j == 1)
                    mm = pe.matmul(ps[4 + h % 4][HEAD:96, 0:T], c["ident"][0:32, 0:32], proj[0:32, 22],
                                   start=True, stop=True)
                    mm.then_inc(projected, 1)
                for t in range(NT):
                    pe.wait_ge(copied, 16)
                    for j in range(2):
                        mm = pe.matmul(ps[t][:, :], proj[:, 12 + j, t * P:(t + 1) * P],
                                       w_ukv[:, j].rearrange("p (h n) -> p h n", n=P)[:, :, HEAD:P],
                                       start=j == 0, stop=j == 1)
                    mm.then_inc(projected, 1)

            @block.scalar
            def _(sc):
                for h in range(8):
                    sc.wait_ge(projected, 2 * h + 1)
                    sc.activation(q[:, h], ps[h % 4][0:96, 0:T], ACT.Copy, scale=96 ** -0.5).then_inc(copied, 1)
                    sc.wait_ge(projected, 2 * h + 2)
                    sc.activation(k[:, h], ps[4 + h % 4][0:96, 0:T], ACT.Copy).then_inc(copied, 1)
                for t in range(NT):
                    sc.wait_ge(projected, 17 + t)
                    sc.activation(v_tok[:, t], ps[t], ACT.Copy)
    rotate(nc, c, ps, q, 8, 96, perm[0:96, 0:96], tables[0:96, 1, 0], tables[0:96, 1, 1])
    attention(nc, c, ps, lambda h, t: q[:, h, t * P:(t + 1) * P], lambda h: k[:, h],
              lambda h, j: v_tok[:, j, h * HEAD:(h + 1) * HEAD],
              lambda h: (h % 2 * HEAD, out[h % 2 * HEAD:h % 2 * HEAD + HEAD, h // 2]), 8, T)


def rwkv(nc, c, ps, ring, cst, z, vec, small, out):
    v = lambda k, j=0, n=1: vec[:, V2[k][0] + j:V2[k][0] + j + n]
    rate = float(np.exp(-0.5))
    flat = lambda a: a.rearrange("p a b -> p (a b)")
    with Stage(nc, "rwkv") as rw:
        ar = Arena(ring)
        zs = ar.take(9, T)
        sw = ar.take(4, T)
        a = ar.take(4, T)
        gate = rw.sb("gate", [P, 2, T])
        kh, kt, bt, rh = (ar.take(4, T) for _ in range(4))
        v_tok = ar.take(NT, T)
        tot = rw.sb("tot", [P, 4, NT])
        ehalf = rw.sb("ehalf", [P, 4, NT])
        mark = ar.at
        with Stage(nc, "shift") as st:
            near = ar.take(9, T)
            hmu = st.sb("hmu", [P, 9])
            omu = st.sb("omu", [P, 9])
            chain, kept = st.sem("chain"), st.sem("kept")
            with st.block() as block:
                @block.vector
                def _(ve):
                    link = Chain(ve, chain)
                    link(ve.tensor_scalar(hmu, v("mu", 0, 9), 0.5, None, MUL))
                    link(ve.tensor_scalar(omu, v("mu", 0, 9), -1.0, 1.0, MUL, ADD))
                    ve.tensor_copy(near[:, :, 0:1], z[:, :, 1:2])
                    ve.tensor_copy(near[:, :, T - 1:T], z[:, :, T - 2:T - 1])
                    link(ve.tensor_tensor(near[:, :, 1:T - 1], z[:, :, 0:T - 2], z[:, :, 2:T], ADD))
                    for j in range(9):
                        ve.tensor_scalar(zs[:, j], z[:, j], omu[:, j:j + 1], None, MUL).then_inc(kept, 1)
                    for j in range(9):
                        ve.wait_ge(kept, j + 1)
                        ve.scalar_tensor_tensor(zs[:, j], near[:, j], hmu[:, j:j + 1], zs[:, j], MUL, ADD)
        r, k, vv = zs[:, 0:2], zs[:, 2:4], zs[:, 4:6]
        ar.at = mark
        with Stage(nc, "gates") as st:
            kk, sq = ar.take(2, T), ar.take(2, T)
            root = ar.take(2, T)
            cs, cx = ar.take(4, T), ar.take(4, T)
            e1, e2, e3 = ar.take(4, T), ar.take(4, T), ar.take(2, T)
            kmod = ar.take(4, T)
            hb = st.sb("hb", [P, 4, NT, 2])
            oka = st.sb("oka", [P, 2])
            up, lifted, opened, keyed, squared, summed, rooted, chain, decays, halves, exped, turned = (
                st.sem(n) for n in ("up", "lifted", "opened", "keyed", "squared", "summed", "rooted", "chain",
                                    "decays", "halves", "exped", "turned"))
            w = lambda n: small[:, SM2[n][0]:SM2[n][1]]
            with st.block() as block:
                @block.scalar
                def _(sc):
                    sc.activation(zs[:, 7], zs[:, 7], ACT.Tanh)
                    sc.activation(zs[:, 6], zs[:, 6], ACT.Sigmoid).then_inc(up, 1)
                    sc.wait_ge(lifted, 1)
                    for d in range(2):
                        for j in range(2):
                            sc.activation(sw[:, 2 * d + j], ps[d][:, j * T:(j + 1) * T], ACT.Sigmoid,
                                          bias=v("w0", 2 * d + j))
                            m = sc.activation(a[:, 2 * d + j], ps[2 + d][:, j * T:(j + 1) * T], ACT.Sigmoid,
                                              bias=v("a0", 2 * d + j))
                    sc.activation(flat(gate), ps[4], ACT.Copy).then_inc(opened, 1)
                    sc.wait_ge(keyed, 1)
                    sc.activation(sq, kk, ACT.Square).then_inc(squared, 1)
                    sc.wait_ge(summed, 1)
                    sc.activation(flat(root), ps[5], ACT.Sqrt).then_inc(rooted, 1)
                    sc.wait_ge(halves, 1)
                    for u in range(4):
                        for n in range(NT):
                            col = slice(n * P, (n + 1) * P)
                            plus, minus = hb[:, u, n, 0:1], hb[:, u, n, 1:2]
                            sc.activation(e1[:, u, col], cx[:, u, col], ACT.Exp, bias=plus, scale=-rate)
                            sc.activation(e2[:, u, col], cs[:, u, col], ACT.Exp, bias=minus, scale=rate)
                            if u < 2:
                                sc.activation(e3[:, u, col], cs[:, u, col], ACT.Exp, bias=plus, scale=-rate)
                    sc.activation(ehalf, hb[:, :, :, 1], ACT.Exp).then_inc(exped, 1)

                @block.tensor
                def _(pe):
                    pe.wait_ge(up, 1)
                    for d in range(2):
                        rows = slice(d * HEAD, (d + 1) * HEAD)
                        for j in range(2):
                            pe.matmul(ps[d][:, j * T:(j + 1) * T], w("w_up")[rows, j * P:(j + 1) * P], zs[rows, 7],
                                      start=True, stop=True)
                            pe.matmul(ps[2 + d][:, j * T:(j + 1) * T], w("a_up")[rows, j * P:(j + 1) * P],
                                      zs[rows, 8], start=True, stop=True)
                    for j in range(2):
                        mm = pe.matmul(ps[4][:, j * T:(j + 1) * T], w("g_up")[:, j * P:(j + 1) * P], zs[:, 6],
                                       start=True, stop=True)
                    mm.then_inc(lifted, 1)
                    for n in range(NT):
                        for j in range(2):
                            mm = pe.transpose(ps[6][:, (2 * n + j) * P:(2 * n + j + 1) * P],
                                              vv[:, j, n * P:(n + 1) * P], c["ident"])
                    mm.then_inc(turned, 1)
                    pe.wait_ge(squared, 1)
                    head_sums(pe, c, ps[5], sq).then_inc(summed, 1)

                @block.vector
                def _(ve):
                    link = Chain(ve, chain)
                    for j in range(2):
                        link(ve.tensor_scalar(kk[:, j], k[:, j], v("k_k", j), None, MUL))
                    ve.sem_inc(keyed, 1)
                    link(ve.tensor_scalar(oka, v("k_a", 0, 2), -1.0, 1.0, MUL, ADD))
                    ve.wait_ge(turned, 1)
                    ve.tensor_copy(v_tok, ps[6].rearrange("p (a b) -> p a b", b=T))
                    ve.wait_ge(opened, 1)
                    for u in range(4):
                        for n in range(NT):
                            col = slice(n * P, (n + 1) * P)
                            m = ve.tensor_tensor_scan(cs[:, u, col], sw[:, u, col], c["zeros"][:, 0:P], 0.0,
                                                      ADD, ADD)
                            link(m)
                            link(ve.tensor_copy(tot[:, u, n:n + 1], cs[:, u, (n + 1) * P - 1:(n + 1) * P]))
                    link(ve.tensor_tensor(cx, cs, sw, SUB))
                    link(ve.tensor_scalar(hb[:, :, :, 0], tot, rate / 2, None, MUL))
                    link(ve.tensor_scalar(hb[:, :, :, 1], tot, -rate / 2, None, MUL))
                    ve.sem_inc(halves, 1)
                    ve.wait_ge(rooted, 1)
                    link(ve.tensor_scalar(root, root, 1e-12, None, MAX))
                    link(ve.reciprocal(flat(root), flat(root)))
                    link(ve.tensor_tensor(kk, kk, root, MUL))
                    for d in range(2):
                        for j in range(2):
                            u = 2 * d + j
                            link(ve.tensor_scalar(kmod[:, u], a[:, u], v("k_a", j), oka[:, j:j + 1], MUL, ADD))
                        link(ve.tensor_tensor(kmod[:, 2 * d:2 * d + 2], kmod[:, 2 * d:2 * d + 2], k, MUL))
                        link(ve.tensor_tensor(a[:, 2 * d:2 * d + 2], a[:, 2 * d:2 * d + 2], kk, MUL))
                    ve.wait_ge(exped, 1)
                    for d in range(2):
                        u = slice(2 * d, 2 * d + 2)
                        key, tilde, read = ((e1[:, u], e2[:, u], e3), (e2[:, u], e1[:, u], e2[:, u]))[d]
                        ve.tensor_tensor(kh[:, u], key, kk, MUL)
                        ve.tensor_tensor(kt[:, u], tilde, kmod[:, u], MUL)
                        ve.tensor_tensor(bt[:, u], tilde, a[:, u], MUL)
                        ve.tensor_tensor(rh[:, u], read, r, MUL)
        ar.at = mark
        tok = ar.take(2, 2, 2 * P)
        abT, akT, bkT, bbT = (ar.take(4, 4, P) for _ in range(4))
        turn_tokens(nc, c, ps, lambda j: (kt, bt)[j // 4][:, j % 4, (j % 4 // 2) * P:(j % 4 // 2 + 1) * P], 8,
                    lambda g: tok[:, g].rearrange("p d (k n) -> p (d k) n", n=P))
        with Stage(nc, "products") as st:
            tri = st.sb("tri", [P, 4, P])
            landed, made, masked = st.sem("landed"), st.sem("made"), st.sem("masked")
            kinds = ((bt, kh, abT), (kt, kh, akT), (kt, rh, bkT), (bt, rh, bbT))
            with st.block() as block:
                @block.sync
                def _(sp):
                    sp.dma_start(tri, cst["tri"]).then_inc(landed, 16)

                @block.tensor
                def _(pe):
                    for g in range(4):
                        d, n = g // 2, g % 2
                        col = slice(n * P, (n + 1) * P)
                        for i, (src, dst, _) in enumerate(kinds):
                            for half in range(2):
                                rows = slice(half * HEAD, (half + 1) * HEAD)
                                if g:
                                    pe.wait_ge(masked, 8 * (g - 1) + 2 * i + half + 1)
                                for pair in range(2):
                                    mm = pe.matmul(ps[2 * i + half][:, pair * P:(pair + 1) * P],
                                                   src[rows, 2 * d + pair, col], dst[rows, 2 * d + pair, col],
                                                   start=True, stop=True)
                                mm.then_inc(made, 1)

                @block.vector
                def _(ve):
                    ve.wait_ge(landed, 16)
                    for g in range(4):
                        for i, (_, _, res) in enumerate(kinds):
                            mask = tri[:, g // 2 + (2 if i >= 2 else 0)].unsqueeze(1).broadcast_to([P, 2, P])
                            for half in range(2):
                                ve.wait_ge(made, 8 * g + 2 * i + half + 1)
                                ve.tensor_tensor(res[:, g, 2 * half:2 * half + 2],
                                                 ps[2 * i + half][:, 0:2 * P].rearrange("p (a b) -> p a b", b=P),
                                                 mask, MUL).then_inc(masked, 1)
        x = rw.sb("x", [P, 4, 4, P])
        xt = ar.take(4, 4, P)
        with Stage(nc, "inverse") as st:
            levels = st.sb("levels", [P, 2, 8, P])
            off = ring[:, 9 * T:17 * T].rearrange("p (a b c) -> p a b c", a=4, b=4)
            t1 = ar.take(4, 4, P)
            landed, begun, offs, t1_made, t1_copied, made, updated = (
                st.sem(n) for n in ("landed", "begun", "offs", "t1_made", "t1_copied", "made", "updated"))
            mask = lambda g, k: levels[:, g // 2, k].unsqueeze(1).broadcast_to([P, 4, P])
            with st.block() as block:
                @block.sync
                def _(sp):
                    sp.dma_start(levels[:, 0], cst["level_fwd"]).then_inc(landed, 16)
                    sp.dma_start(levels[:, 1], cst["level_bwd"]).then_inc(landed, 16)

                @block.vector
                def _(ve):
                    ve.wait_ge(landed, 32)
                    for g in range(4):
                        ve.tensor_tensor(xt[:, g], abT[:, g], mask(g, 0), MUL).then_inc(begun, 1)
                    for g in range(4):
                        ve.wait_ge(begun, g + 1)
                        ve.tensor_tensor(xt[:, g], c["ident"].unsqueeze(1).broadcast_to([P, 4, P]), xt[:, g], SUB)
            turn_tokens(nc, c, ps, lambda j: xt[:, j // 4, j % 4], 16, lambda g: x[:, g])
            bank = lambda b, j: ps[b][:, j * P:(j + 1) * P]
            quad = lambda b: ps[b].rearrange("p (a b) -> p a b", b=P)
            with st.block() as block:
                @block.tensor
                def _(pe):
                    def first(i, g):
                        pe.wait_ge(offs, i * 4 + (g - 3))
                        pe.wait_ge(t1_copied, i * 4 + (g - 3))
                        for j in range(4):
                            mm = pe.matmul(bank(g % 2, j), off[:, g, j], x[:, g, j], start=True, stop=True)
                        mm.then_inc(t1_made, 1)

                    def second(i, g):
                        pe.wait_ge(t1_copied, i * 4 + (g - 1))
                        pe.wait_ge(updated, i * 4 + (g - 1))
                        for j in range(4):
                            pe.matmul(bank(2 + g % 2, j), xt[:, g, j], t1[:, g, j], start=True, stop=True)
                        for j in range(4):
                            mm = pe.matmul(bank(4 + g % 2, j), t1[:, g, j], xt[:, g, j], start=True, stop=True)
                        mm.then_inc(made, 1)

                    with pe.Fori(1, 7) as i:
                        first(i, 0)
                        for g in range(1, 4):
                            first(i, g)
                            second(i, g - 1)
                        second(i, 3)

                @block.scalar
                def _(sc):
                    sc.sem_inc(t1_copied, 2)
                    with sc.Fori(1, 7) as i:
                        for g in range(4):
                            sc.wait_ge(t1_made, i * 4 + (g - 3))
                            sc.activation(t1[:, g], quad(g % 2), ACT.Copy).then_inc(t1_copied, 1)

                @block.vector
                def _(ve):
                    for g in range(4):
                        ve.tensor_tensor(off[:, g], abT[:, g], mask(g, 1), MUL).then_inc(offs, 1)
                    ve.sem_inc(updated, 4)
                    with ve.Fori(1, 7) as i:
                        for g in range(4):
                            ve.wait_ge(made, i * 4 + (g - 3))
                            ve.tensor_tensor(x[:, g], x[:, g], quad(2 + g % 2), SUB)
                            ve.tensor_tensor(xt[:, g], xt[:, g], quad(4 + g % 2), SUB).then_inc(updated, 1)
                            ve.tensor_tensor(off[:, g], abT[:, g], mask(g, i + 1), MUL).then_inc(offs, 1)
        y = rw.sb("y", [P, 2, T])
        with Stage(nc, "chunks") as st:
            rhs = ar.take(4, 4, HEAD)
            neg_p = ar.take(4, 4, HEAD)
            state = st.sb("state", [P, 2, 2, HEAD])
            told, copied, solved, negated, carried, scaled, read = (
                st.sem(n) for n in ("told", "copied", "solved", "negated", "carried", "scaled", "read"))
            head = lambda half, pair: slice((2 * pair + half) * HEAD, (2 * pair + half + 1) * HEAD)
            order = [(0, 0), (1, 1), (0, 1), (1, 0)]
            with st.block() as block:
                @block.tensor
                def _(pe):
                    for s, (d, n) in enumerate(order):
                        g = 2 * d + n
                        col = slice(n * P, (n + 1) * P)
                        if s >= 2:
                            pe.wait_ge(scaled, 2 * d + 2)
                        for half in range(2):
                            rows = slice(half * HEAD, (half + 1) * HEAD)
                            for pair in range(2):
                                o = ps[half][:, pair * HEAD:(pair + 1) * HEAD]
                                if s and pair == 0:
                                    pe.wait_ge(copied, 2 * (s - 1) + half + 1)
                                mm = pe.matmul(o, akT[:, g, 2 * half + pair], v_tok[:, n, head(half, pair)],
                                               start=True, stop=s < 2)
                                if s >= 2:
                                    mm = pe.matmul(o, kh[rows, 2 * d + pair, col], state[rows, d, pair],
                                                   start=False, stop=True)
                            mm.then_inc(told, 1)
                        pe.wait_ge(copied, 2 * s + 2)
                        if s:
                            pe.wait_ge(negated, s)
                        for j in range(4):
                            mm = pe.matmul(ps[2][:, j * HEAD:(j + 1) * HEAD], xt[:, g, j], rhs[:, g, j],
                                           start=True, stop=True)
                        mm.then_inc(solved, 1)
                        if s < 2:
                            pe.wait_ge(negated, s + 1)
                            for half in range(2):
                                rows = slice(half * HEAD, (half + 1) * HEAD)
                                for pair in range(2):
                                    ch = slice(pair * P + half * HEAD, pair * P + half * HEAD + HEAD)
                                    o = ps[3 + d][rows, pair * HEAD:(pair + 1) * HEAD]
                                    pe.matmul(o, tok[:, 0, d, ch], v_tok[:, n, head(half, pair)],
                                              start=True, stop=False)
                                    mm = pe.matmul(o, tok[:, 1, d, ch], neg_p[:, g, 2 * half + pair],
                                                   start=False, stop=True)
                            mm.then_inc(carried, 1)
                    pe.wait_ge(negated, 4)
                    for n in range(NT):
                        col = slice(n * P, (n + 1) * P)
                        for half in range(2):
                            rows = slice(half * HEAD, (half + 1) * HEAD)
                            for pair in range(2):
                                o = ps[5 + n][rows, pair * P:(pair + 1) * P]
                                for d in range(2):
                                    g, j = 2 * d + n, 2 * half + pair
                                    pe.matmul(o, v_tok[:, n, head(half, pair)], bkT[:, g, j],
                                              start=d == 0, stop=False)
                                    pe.matmul(o, neg_p[:, g, j], bbT[:, g, j], start=False, stop=False)
                                d = 1 - n
                                mm = pe.matmul(o, state[rows, d, pair], rh[rows, 2 * d + pair, col],
                                               start=False, stop=True)
                        mm.then_inc(read, 1)

                @block.scalar
                def _(sc):
                    for s, (d, n) in enumerate(order):
                        for half in range(2):
                            sc.wait_ge(told, 2 * s + half + 1)
                            sc.activation(rhs[:, 2 * d + n, 2 * half:2 * half + 2],
                                          ps[half][:, 0:P].rearrange("p (a b) -> p a b", b=HEAD),
                                          ACT.Copy).then_inc(copied, 1)

                @block.vector
                def _(ve):
                    for s, (d, n) in enumerate(order):
                        ve.wait_ge(solved, s + 1)
                        ve.tensor_scalar(neg_p[:, 2 * d + n], ps[2][:, 0:T].rearrange("p (a b) -> p a b", b=HEAD),
                                         -1.0, None, MUL).then_inc(negated, 1)
                        if s < 2:
                            ve.wait_ge(carried, s + 1)
                            for pair in range(2):
                                u = 2 * d + pair
                                ve.tensor_scalar(state[:, d, pair], ps[3 + d][:, pair * HEAD:(pair + 1) * HEAD],
                                                 ehalf[:, u, 0:1], ehalf[:, u, 1:2], MUL, MUL).then_inc(scaled, 1)
                    for n in range(NT):
                        ve.wait_ge(read, n + 1)
                        ve.tensor_copy(y[:, :, n * P:(n + 1) * P],
                                       ps[5 + n][:, 0:2 * P].rearrange("p (a b) -> p a b", b=P))
        ar.at = mark
        head_norm(nc, c, ps, ar, y, c["eps"][:, 2:3], v("ln_g", 0, 2), v("ln_b", 0, 2), y)
        with Stage(nc, "bonus") as st:
            prod = ar.take(2, T)
            multiplied, summed, chain = st.sem("multiplied"), st.sem("summed"), st.sem("chain")
            with st.block() as block:
                @block.tensor
                def _(pe):
                    pe.wait_ge(multiplied, 1)
                    head_sums(pe, c, ps[0], prod).then_inc(summed, 1)

                @block.vector
                def _(ve):
                    link = Chain(ve, chain)
                    for j in range(2):
                        link(ve.scalar_tensor_tensor(prod[:, j], r[:, j], v("r_k", j), k[:, j], MUL, MUL))
                    ve.sem_inc(multiplied, 1)
                    ve.wait_ge(summed, 1)
                    link(ve.tensor_tensor(prod, ps[0].rearrange("p (a b) -> p a b", b=T), vv, MUL))
                    link(ve.tensor_tensor(prod, prod, y, ADD))
                    ve.tensor_tensor(out, prod, gate, MUL)


def second_block(nc, c, ps, ring, I, cst, vec1, cond, xT, hT, tables, dbg=None):
    with nc.Fori(0, 2) as l, Stage(nc, "layer") as ly:
        vec = ly.sb("vec", [P, V2_COLS])
        mod = ly.sb("mod", [P, 72, 1])
        gain = ly.sb("gain", [P, 5, KD])
        v = lambda k: vec[:, V2[k][0]:V2[k][1]]
        load_all(nc, [(vec, I["vec2"][l])])
        with Stage(nc, "modulate") as st:
            modulation(nc, st, c, ring, ps, I["w_ada"][l], 6, cond, (2,), mod, v("b_ada"))
            with st.block() as block:
                @block.vector
                def _(ve):
                    for j in range(3):
                        ve.tensor_scalar(gain[:, j], mod[:, 24 * j + 8:24 * j + 16, 0], 1.0, None, ADD)
                    for j in range(2):
                        ve.tensor_scalar(gain[:, 3 + j], mod[:, 48 * j + 16:48 * j + 24, 0], 0.5, None, MUL)
        norm_modulate(nc, c, ps, [(xT, hT[:, :, 0:T], gain[:, 0], mod[:, 0:8, 0])])
        feed_forward(nc, c, ps, ring, I["w_ff1_in"][l], I["w_ff1_out"][l], xT, hT, gain[:, 3])
        norm_modulate(nc, c, ps, [(xT, hT[:, :, 0:T], gain[:, 1], mod[:, 24:32, 0])])
        with Stage(nc, "mixer2") as st:
            proj = st.sb("proj", [P, 24, T])
            mix = st.sb("mix", [P, 8, T])
            with Stage(nc, "w_in_2") as s2:
                pairs = proj.rearrange("p (q a) t -> p q (a t)", a=2)

                def mm(pe, q, u, w):
                    for j in range(2):
                        for k in range(KD):
                            m = pe.matmul(ps[u % 2][:, j * T:(j + 1) * T], w[:, j * KD + k], hT[:, k, 0:T],
                                          start=k == 0, stop=k == KD - 1)
                    return m

                def act(sc, q, u):
                    return sc.activation(pairs[:, q], ps[u % 2], ACT.Copy)

                stream(nc, s2, ring, I["w_in_2"][l], 2, 6, 16, mm, act)
            with Stage(nc, "branches") as s2:
                small = s2.sb("small", [P, SM2_COLS])
                load_all(nc, [(small, I["small2"][l])])
                latent_attention(nc, c, ps, ring, cst, proj, tables, vec, small, mix[:, 2:6])
                retention(nc, c, ps, ring, cst, proj, tables, vec, mix[:, 6:8])
                rwkv(nc, c, ps, ring, cst, proj[:, 0:9], vec, small, mix[:, 0:2])
            if dbg:
                dbg(nc, l, mix=mix)
            add_projection(nc, ring, ps, I["w_out_2"][l], 4, mix, xT, mod[:, 40:48, 0])
        norm_modulate(nc, c, ps, [(xT, hT[:, :, 0:T], gain[:, 2], mod[:, 48:56, 0])])
        feed_forward(nc, c, ps, ring, I["w_ff2_in"][l], I["w_ff2_out"][l], xT, hT, gain[:, 4])
        if dbg:
            dbg(nc, l, xT=xT)
    norm_modulate(nc, c, ps, [(xT, xT, vec1[:, V1["final_2"][0]:V1["final_2"][1]], None)])


V1, V1_COLS = fields(VEC1)
V2, V2_COLS = fields(VEC2)
SM1, SM1_COLS = fields(SMALL1)
SM2, SM2_COLS = fields(SMALL2)


def store(nc, c, ps, xT, out):
    with Stage(nc, "store") as st:
        rows = st.sb("rows", [P, NT, D])
        turn_tokens(nc, c, ps, lambda j: xT[:, j % KD, (j // KD) * P:(j // KD + 1) * P], NT * KD,
                    lambda g: rows[:, g // 2, (g % 2) * 512:(g % 2 + 1) * 512].rearrange("p (k n) -> p k n", n=P))
        stored = st.sem("stored")
        with st.block() as block:
            @block.sync
            def _(sp):
                sp.dma_start(out.rearrange("(t p) d -> p t d", p=P), rows).then_inc(stored, 16)
                sp.wait_ge(stored, 16)


def program(nc, I, cst, out, dbg=None, first=True):
    with ExitStack() as ctx:
        def sb(name, shape):
            return ctx.enter_context(nc.sbuf_tensor(name, shape, F32))[:]

        ps = [ctx.enter_context(nc.psum_tensor(f"bank{j}", [P, 512], F32))[:] for j in range(8)]
        ring = sb("ring", [P, RING_COLS])
        xT = sb("xT", [P, KD, T])
        vec = sb("vec", [P, V1_COLS])
        cond = sb("cond", [P, KD, 32])
        c = {k: sb(k, [P, P]) for k in ("ident", "ones", "ones_head", "zeros")}
        c["eps"] = sb("eps", [P, 3])
        load_all(nc, [(c[k], cst[k]) for k in ("ident", "ones", "ones_head")] + [(vec, I["vec1"])])
        with nc.Block() as block:
            @block.gpsimd
            def _(pool):
                pool.memset(cond[:, :, 3:32], 0.0)

            @block.scalar
            def _(sc):
                for j, k in enumerate(("c", "c_ctx", "c_2")):
                    sc.activation(cond[:, :, j], vec[:, V1[k][0]:V1[k][1]], ACT.Silu)

            @block.vector
            def _(ve):
                ve.memset(c["zeros"], 0.0)
                for j, e in enumerate((EPS, RET_EPS, RWKV_EPS)):
                    ve.memset(c["eps"][:, j:j + 1], e)
        if first:
            with Stage(nc, "hidden") as st:
                first_block(nc, c, ps, ring, I, cst, vec, cond, xT, st.sb("hT", [P, KD, 2 * T]))
        else:
            turn_features(nc, c, ps, [I["x"]], [xT])
        with Stage(nc, "hidden") as st:
            hT = st.sb("hT", [P, KD, T])
            tables = st.sb("tables", [P, 3, 2, T])
            rotary_tables(nc, cst, I["positions"], tables)
            second_block(nc, c, ps, ring, I, cst, vec, cond, xT, hT, tables, dbg)
        store(nc, c, ps, xT, out)


def kernel(**inputs):
    import concourse.bacc as bacc
    from concourse.bass_utils import run_bass_kernel_spmd

    data = host_layout({k: np.asarray(a) for k, a in inputs.items()})
    tables = shape_tables()
    nc = bacc.Bacc("TRN2", target_bir_lowering=False, num_devices=1)
    arrays, ins, consts = {}, {}, {}
    for group, prefix, aps in ((data, "in_", ins), (tables, "table_", consts)):
        for name, a in group.items():
            arrays[prefix + name] = a
            aps[name] = nc.dram_tensor(prefix + name, a.shape, mybir.dt.from_np(a.dtype), kind="ExternalInput").ap()
    out = nc.dram_tensor("out", (T, D), F32, kind="ExternalOutput").ap()
    program(nc, ins, consts, out)
    result = run_bass_kernel_spmd(nc, [arrays], core_ids=[0])
    return result.results[0]["out"].reshape(1, T, D)
```

```python
from contextlib import ExitStack

import numpy as np

import concourse.bass as bass
from concourse import mybir

P = 128
D = 1024
KD = D // P
T = 256
NT = T // P
HEAD = 64
E = 16
CAP = 2 * T // E
FF_E = 2 * D
KE = FF_E // P
D_FF = 2816
KF = D_FF // P
RWKV_COLS = 1152
EPS = 1e-6
RET_EPS = 1e-5
RWKV_EPS = 64e-5
PI = 3.14159265358979
RING_COLS = 24576

F32 = mybir.dt.float32
I32 = mybir.dt.int32
ALU = mybir.AluOpType
ACT = mybir.ActivationFunctionType
AX = mybir.AxisListType
MUL, ADD, SUB, MAX = ALU.mult, ALU.add, ALU.subtract, ALU.max


def shape_tables():
    f = np.float32
    out = {}
    p = np.arange(P)
    ident = np.eye(P)
    out["ident"] = ident
    out["ones"] = np.ones((P, P))
    out["ones_head"] = (p[:, None] // HEAD == p[None, :] // HEAD) * 1.0
    out["swap_pair"] = ident[p ^ 1]
    out["swap_head"] = ident[p ^ HEAD]
    out["swap_half"] = ident[p ^ 32]
    swap_mla = np.zeros((P, P))
    for a in range(32):
        swap_mla[64 + a, 64 + (a ^ 16)] = 1
    out["swap_mla"] = swap_mla
    swap_kpe = np.zeros((P, P))
    swap_kpe[:32, :32] = swap_mla[64:96, 64:96]
    out["swap_kpe"] = swap_kpe
    out["ones_but_first"] = np.ones((P, P)) * (p[:, None] > 0)

    tok = np.arange(T)
    inv = 10000.0 ** (-np.arange(0, 32, 2) / 32)
    ang = np.concatenate([(tok // 64)[:, None] * inv, (tok % 64)[:, None] * inv], 1)
    of_pair = (p % HEAD) // 2
    out["axial_cos"] = np.cos(ang)[:, of_pair].T
    out["axial_sin"] = np.sin(ang)[:, of_pair].T * np.where(p % 2, 1.0, -1.0)[:, None]

    rot = np.zeros((P, 6))
    rot[:, 0] = 10000.0 ** (-2 * (p % 32) / 64)
    rot[:, 1] = np.where(p % 64 < 32, -1, 1)
    pe = p - 64
    rot[64:96, 2] = 10000.0 ** (-2 * (pe[64:96] % 16) / 32)
    rot[64:96, 3] = np.where(pe[64:96] < 16, -1, 1)
    rot[:32, 4] = rot[64:96, 2]
    rot[:32, 5] = rot[64:96, 3]
    out["rot_freq"] = rot

    t = tok / (T - 1)
    bands = np.linspace(1e-4, 15, 16)
    fa = 2 * np.pi / T * tok[:, None] * bands[None, :]
    feats = np.zeros((P, T))
    feats[:33] = np.concatenate([t[:, None], np.cos(fa), -np.sin(fa)], 1).T
    out["hy_feats"] = feats
    deltas = np.abs(np.linspace(np.log(1e-2) / 1.5, np.log(1e-2) / 0.3, 256))
    win = np.exp(-t[:, None] * deltas[None, :])
    out["hy_window"] = win.reshape(2, P, 256).transpose(1, 0, 2)
    n2 = 2 * T
    tau = np.concatenate([tok, (n2 - tok) % n2])
    keep = np.ones(n2)
    keep[T] = 0
    fr = np.arange(T)
    th = 2 * np.pi * ((tau[:, None] * fr[None, :]) % n2) / n2
    alt = np.where(tau % 2, -1.0, 1.0)
    cc = np.cos(th[:, :P]).copy()
    cc[:, 0] = alt
    fd = np.concatenate([np.cos(th), -np.sin(th), cc], 1) * keep[:, None]
    out["dft_filter"] = fd.reshape(4, P, 640).transpose(1, 0, 2)
    th = 2 * np.pi * ((tok[:, None] * fr[None, :]) % n2) / n2
    alt = np.where(tok % 2, -1.0, 1.0)
    im = -np.sin(th)
    im[:, 0] = alt
    out["dft_signal"] = np.concatenate([np.cos(th), im], 1).reshape(2, P, 512).transpose(1, 0, 2)
    gre = 2 * np.cos(th.T) / n2
    gre[0] /= 2
    gim = -2 * np.sin(th.T) / n2
    gim[0] = alt / n2
    out["dft_inverse"] = np.concatenate([gre, gim], 0).reshape(4, P, T).transpose(1, 0, 2)

    w = np.arange(64)
    tw = 2 * np.pi * ((w[:, None] * w[None, :]) % 64) / 64
    bd = lambda m: np.kron(np.eye(2), m)
    out["fn_channel"] = np.concatenate([bd(np.cos(tw)), bd(np.sin(tw))], 1)
    tn = 2 * np.pi * ((tok[:, None] * tok[None, :]) % T) / T
    out["fn_token"] = (np.concatenate([np.cos(tn), -np.sin(tn)], 1) / 128).reshape(2, P, 512).transpose(1, 0, 2)

    s_, t_ = p[:, None], p[None, :]
    lev = []
    for k in range(7):
        m = 1 << k
        lev.append(((s_ // m) % 2 == 0) & (t_ // m == s_ // m + 1))
    lev.append(lev[0] & False)
    out["level_fwd"] = np.stack(lev, 1)
    out["level_bwd"] = np.stack([x.T for x in lev], 1)
    out["tri"] = np.stack([s_ < t_, s_ > t_, s_ <= t_, s_ > t_], 1)
    ds = np.arange(T)[None, :] - np.arange(T)[:, None]
    out["ahead"] = np.maximum(ds, 0).reshape(2, P, T).transpose(1, 0, 2)
    out["behind"] = np.maximum(-ds, 0).reshape(2, P, T).transpose(1, 0, 2)
    out["slots"] = np.broadcast_to(np.arange(1, CAP + 1), (P, CAP))
    return {k: np.ascontiguousarray(v, dtype=f) for k, v in out.items()}


def blocks(w, n_order="kn"):
    *lead, k, n = w.shape
    w = w.reshape(*lead, k // P, P, n // P, P)
    nl = len(lead)
    w = w.transpose(*range(nl), nl + 1, nl + 2, nl, nl + 3)
    return w.reshape(*lead, P, (n // P) * (k // P) * P)


def panels(w, blk):
    *lead, k, n = w.shape
    b = blocks(w).reshape(*lead, P, -1, blk * P)
    nl = len(lead)
    return np.ascontiguousarray(b.transpose(*range(nl), nl + 1, nl, nl + 2))


def wide_tiles(w, width):
    *lead, k, n = w.shape
    nl = len(lead)
    w = w.reshape(*lead, k // (2 * P), 2, P, n // width, width)
    w = w.transpose(*range(nl), nl + 3, nl, nl + 2, nl + 1, nl + 4)
    return w.reshape(*lead, -1, P, 2 * width)


def column(v):
    v = np.asarray(v).reshape(-1)
    if v.size < P:
        v = np.concatenate([v, v])
    return v.reshape(-1, P).T


def interleave(a, b):
    *lead, k, n = a.shape
    return np.stack([a.reshape(*lead, k, n // P, P), b.reshape(*lead, k, n // P, P)], -2).reshape(*lead, k, 2 * n)


VEC1 = dict(c=8, c_ctx=8, b_mod=48, norm1=8, norm2=8, q_gain=1, k_gain=1, short_w=18, short_b=6,
            f_b1=1, f_b2=1, f_freq=1, hy_bias=4, final_g=8, c_2=8, final_2=8)
VEC2 = dict(b_ada=72, mu=9, w0=4, a0=4, k_k=2, k_a=2, r_k=2, ln_g=2, ln_b=2, mla_q_g=3, mla_kv_g=2,
            gn_g=2, log_rate=8)
SMALL1 = dict(f_w1=64, f_w2=64, f_w3=1024, router=128)
SMALL2 = dict(w_up=256, a_up=256, g_up=256, w_uq=2304, w_ukv=2048)


def fields(widths):
    at, out = 0, {}
    for k, n in widths.items():
        out[k] = (at, at + n)
        at += n
    return out, at


def host_layout(i):
    def pad(a):
        return np.concatenate([a, np.zeros((P - a.shape[0],) + a.shape[1:], a.dtype)], 0)

    rows = lambda a: a.reshape(-1, P, a.shape[-1]).transpose(1, 0, 2).reshape(P, -1)
    o = {}
    o["x"], o["ctx"] = i["x"][0], i["ctx"][0]
    w = i["w_in"][0]
    o["w_kv"] = panels(w[:, 512:768], 16)
    o["w_in"] = panels(np.concatenate([w[:, :512], w[:, 768:]], 1), 16)
    o["w_mod"] = wide_tiles(i["w_mod"][0], 1536)
    wb = i["w_branch"][0]
    o["w_branch"] = panels(wb, 16)
    o["w_out"] = panels(i["w_out"][0], 16)
    up = np.stack([i["w_gate"][0].reshape(E, KD, P, FF_E), i["w_up"][0].reshape(E, KD, P, FF_E)], 3)
    down = i["w_down"][0].reshape(E, 4, 4, P, D).transpose(0, 2, 3, 1, 4)
    o["w_expert"] = np.concatenate([up.reshape(E, KD, P, 4 * D), down.reshape(E, 4, P, 4 * D)], 1)
    o["vec1"] = np.concatenate([
        column(i["c"]), column(i["c_ctx"]), column(i["b_mod"]), column(i["norm1_g"]), column(i["norm2_g"]),
        column(i["q_gain"]), column(i["k_gain"]), column(i["hy_short_w"]), column(i["hy_short_b"]),
        column(i["hy_f_b1"]), column(i["hy_f_b2"]), column(i["hy_f_freq"]), column(i["hy_bias"]),
        column(i["final_g"]), column(i["c_2"]), column(i["final_norm_g_2"])], 1)
    o["small1"] = np.concatenate([pad(i["hy_f_w1"][0]), pad(i["hy_f_w2"][0]), pad(i["hy_f_w3"][0]),
                                  rows(i["w_router"][0])], 1)
    o["positions"] = np.broadcast_to(i["positions_2"].reshape(1, T), (P, T))
    o["w_ada"] = wide_tiles(i["w_ada_2"], 1024)
    for n in "12":
        wi = i[f"w_ff{n}_in_2"]
        o[f"w_ff{n}"] = np.concatenate([panels(interleave(wi[..., :D_FF], wi[..., D_FF:]), 16),
                                        panels(i[f"w_ff{n}_out_2"], 16)], 1)
    wi = i["w_in_2"]
    kpe = RWKV_COLS + 640
    gap = np.zeros(wi.shape[:2] + (P - 32,), wi.dtype)
    o["w_in_2"] = panels(np.concatenate([wi[..., :kpe], wi[..., kpe + 32:], wi[..., kpe:kpe + 32], gap,
                                         np.zeros(wi.shape[:2] + (P,), wi.dtype)], 2), 16)
    o["w_out_2"] = panels(i["w_out_2"], 16)
    o["vec2"] = np.stack([np.concatenate([
        column(i["b_ada_2"][l]), column(i["rwkv_mu_2"][l]), column(i["rwkv_w0_2"][l]), column(i["rwkv_a0_2"][l]),
        column(i["rwkv_k_k_2"][l]), column(i["rwkv_k_a_2"][l]), column(i["rwkv_r_k_2"][l]),
        column(i["rwkv_ln_g_2"][l]), column(i["rwkv_ln_b_2"][l]), column(i["mla_q_norm_g_2"][l]),
        column(i["mla_kv_norm_g_2"][l]), column(i["ret_gn_g_2"][l]),
        np.broadcast_to(i["ret_log_rate_2"][l].reshape(1, 8), (P, 8))], 1) for l in range(2)])
    o["small2"] = np.stack([np.concatenate([
        i["rwkv_w_up_2"][l].reshape(P, 256), i["rwkv_a_up_2"][l].reshape(P, 256), i["rwkv_g_up_2"][l],
        rows(i["mla_w_uq_2"][l]), rows(i["mla_w_ukv_2"][l])], 1) for l in range(2)])
    return {k: np.ascontiguousarray(v) for k, v in o.items()}


class Stage:

    count = 0

    def __init__(self, nc, name):
        Stage.count += 1
        self.nc, self.name = nc, f"{name}_{Stage.count}"

    def __enter__(self):
        self.stack, self.sems = ExitStack(), []
        return self

    def sb(self, name, shape, dt=F32):
        return self.stack.enter_context(self.nc.sbuf_tensor(f"{self.name}_{name}", shape, dt))[:]

    def sem(self, name):
        self.sems.append(self.stack.enter_context(self.nc.semaphore(f"{self.name}_{name}")))
        return self.sems[-1]

    def block(self):
        return self.nc.Block()

    def __exit__(self, kind, value, trace):
        if kind is None and self.sems:
            with self.nc.Block() as block:
                @block.gpsimd
                def _(pool):
                    for s in self.sems:
                        pool.sem_clear(s)
        self.stack.close()


class Arena:

    def __init__(self, ring, cols):
        self.ring, self.at, self.cols = ring, 0, cols

    def take(self, *dims, rows=P):
        n = 1
        for d in dims:
            n *= d
        a = self.ring[0:rows, self.at:self.at + n]
        self.at += n
        assert self.at <= self.cols
        if len(dims) == 1:
            return a
        names = "abcd"[:len(dims)]
        return a.rearrange(f"p ({' '.join(names)}) -> p {' '.join(names)}", **dict(zip(names[1:], dims[1:])))


class Chain:

    def __init__(self, eng, sem):
        self.eng, self.sem, self.n = eng, sem, 0

    def __call__(self, ins):
        self.n += 1
        ins.then_inc(self.sem, 1)
        self.eng.wait_ge(self.sem, self.n)


def over(eng, n):
    return eng.Fori(0, n) if n > 1 else ExitStack()


def stream(nc, st, ring, src, turns, slots, blk, mm, act=None, dve=None, act_wait=()):
    loaded = [st.sem(f"loaded{u}") for u in range(slots)]
    panel_done = st.sem("panel_done")
    act_done = st.sem("act_done")
    bank_free = st.sem("bank_free")
    cols = blk * P
    slot = [ring[:, u * cols:(u + 1) * cols] for u in range(slots)]
    with st.block() as block:
        @block.sync
        def _(sp):
            for u in range(slots):
                sp.dma_start(slot[u], src[u]).then_inc(loaded[u], 16)
            if turns > 1:
                with sp.Fori(1, turns) as i:
                    for u in range(slots):
                        sp.wait_ge(panel_done, i * slots + (u + 1 - slots))
                        sp.dma_start(slot[u], src[i * slots + u]).then_inc(loaded[u], 16)

        @block.tensor
        def _(pe):
            with over(pe, turns) as i:
                i = i if turns > 1 else 0
                for u in range(slots):
                    q = i * slots + u
                    pe.wait_ge(loaded[u], i * 16 + 16)
                    if act or dve:
                        pe.wait_ge(bank_free, q + (2 if u == 0 and slots % 2 else 1))
                    mm(pe, q, u, slot[u].rearrange("p (b n) -> p b n", n=P)).then_inc(panel_done, 1)

        if act:
            @block.scalar
            def _(sc):
                if not dve:
                    sc.sem_inc(bank_free, 2)
                with over(sc, turns) as i:
                    i = i if turns > 1 else 0
                    for u in range(slots):
                        q = i * slots + u
                        sc.wait_ge(panel_done, q + 1)
                        act(sc, q, u).then_inc(act_done if dve else bank_free, 1)

        if dve:
            @block.vector
            def _(ve):
                ve.sem_inc(bank_free, 2)
                with over(ve, turns) as i:
                    i = i if turns > 1 else 0
                    for u in range(slots):
                        q = i * slots + u
                        ve.wait_ge(act_done if act else panel_done, q + 1)
                        dve(ve, q, u).then_inc(bank_free, 1)


def norm_modulate(nc, c, ps, groups):
    with Stage(nc, "norm") as st:
        w = T * len(groups)
        sq = st.sb("sq", [P, KD, w])
        root = st.sb("root", [P, w])
        rstd = st.sb("rstd", [P, w])
        squared, summed, rooted, inverted, scaled = (
            st.sem(n) for n in ("squared", "summed", "rooted", "inverted", "scaled"))
        with st.block() as block:
            @block.scalar
            def _(sc):
                for g, (x, _, _, _) in enumerate(groups):
                    sc.activation(sq[:, :, g * T:(g + 1) * T], x, ACT.Square).then_inc(squared, 1)
                sc.wait_ge(summed, 1)
                sc.activation(root[:, :], ps[0][:, 0:w], ACT.Sqrt, bias=c["eps"][:, 0:1],
                              scale=1.0 / D).then_inc(rooted, 1)
                for g, (_, out, _, shift) in enumerate(groups):
                    for k in range(KD):
                        if shift is None:
                            continue
                        sc.wait_ge(scaled, g * KD + k + 1)
                        sc.activation(out[:, k], out[:, k], ACT.Identity, bias=shift[:, k:k + 1])

            @block.tensor
            def _(pe):
                pe.wait_ge(squared, len(groups))
                for k in range(KD):
                    mm = pe.matmul(ps[0][:, 0:w], c["ones"][:, :], sq[:, k], start=k == 0, stop=k == KD - 1)
                mm.then_inc(summed, 1)

            @block.vector
            def _(ve):
                ve.wait_ge(rooted, 1)
                ve.reciprocal(rstd[:, :], root[:, :]).then_inc(inverted, 1)
                ve.wait_ge(inverted, 1)
                for g, (x, out, gain, _) in enumerate(groups):
                    for k in range(KD):
                        ve.scalar_tensor_tensor(out[:, k], x[:, k], gain[:, k:k + 1],
                                                rstd[:, g * T:(g + 1) * T], MUL, MUL).then_inc(scaled, 1)


def load_all(nc, pairs):
    with Stage(nc, "load") as st:
        landed = st.sem("landed")
        with st.block() as block:
            @block.sync
            def _(sp):
                for dst, src in pairs:
                    sp.dma_start(dst, src).then_inc(landed, 16)
                sp.wait_ge(landed, 16 * len(pairs))


def turn_features(nc, c, ps, loads, outs):
    with Stage(nc, "turn") as st:
        n = len(loads)
        rows = st.sb("rows", [P, n, NT, D])
        landed, turned, copied = st.sem("landed"), st.sem("turned"), st.sem("copied")
        jobs = [(g, t, h) for g in range(n) for t in range(NT) for h in range(2)]
        with st.block() as block:
            @block.sync
            def _(sp):
                for g, src in enumerate(loads):
                    sp.dma_start(rows[:, g], src.rearrange("(t p) d -> p t d", p=P)).then_inc(landed, 16)

            @block.tensor
            def _(pe):
                for j, (g, t, h) in enumerate(jobs):
                    pe.wait_ge(landed, 16 * n)
                    for k in range(4):
                        f = (4 * h + k) * P
                        mm = pe.transpose(ps[j][:, k * P:(k + 1) * P], rows[:, g, t, f:f + P], c["ident"][:, :])
                    mm.then_inc(turned, 1)

            @block.vector
            def _(ve):
                for j, (g, t, h) in enumerate(jobs):
                    ve.wait_ge(turned, j + 1)
                    ve.tensor_copy(outs[g][:, 4 * h:4 * h + 4, t * P:(t + 1) * P],
                                   ps[j][:, :].rearrange("p (k n) -> p k n", n=P)).then_inc(copied, 1)


def modulation(nc, st, c, ring, ps, src, n_tiles, cond, which, mod, bias):
    slots, per_tile, width = 8, KD // 2, 3 * P
    rows = st.sb("rows", [P, 2, width])
    loaded = [st.sem(f"loaded{u}") for u in range(slots)]
    panel_done, rows_out, turned, added = (st.sem(k) for k in ("panel_done", "rows_out", "turned", "added"))
    cols = 8 * width
    slot = [ring[:, u * cols:(u + 1) * cols] for u in range(slots)]
    turns = n_tiles // 2
    split = lambda a: a.rearrange("p (t g n) -> p t g n", g=4, n=3)
    with st.block() as block:
        @block.sync
        def _(sp):
            for u in range(slots):
                sp.dma_start(slot[u], src[u]).then_inc(loaded[u], 16)
            with sp.Fori(1, turns) as i:
                for u in range(slots):
                    sp.wait_ge(panel_done, i * slots + (u + 1 - slots))
                    sp.dma_start(slot[u], src[i * slots + u]).then_inc(loaded[u], 16)

        @block.tensor
        def _(pe):
            with pe.Fori(0, turns) as i:
                for t in range(2):
                    pe.wait_ge(rows_out, i * 2 + (t + 1))
                    for j in range(per_tile):
                        u = t * per_tile + j
                        w = slot[u].rearrange("p (k g n) -> p k g n", k=2, g=4)
                        pe.wait_ge(loaded[u], i * 16 + 16)
                        for k in range(2):
                            for g in range(4):
                                mm = pe.matmul(ps[t][32 * g:32 * g + 32, 0:width], cond[:, 2 * j + k], w[:, k, g],
                                               start=j == 0 and k == 0, stop=j == per_tile - 1 and k == 1)
                        mm.then_inc(panel_done, 1)
                    pe.wait_ge(rows_out, i * 2 + (t + 3))
                    pe.wait_ge(added, i * 2 + (t + 1))
                    for n in range(3):
                        mm = pe.transpose(ps[2 + t][:, n * P:(n + 1) * P], rows[:, t, n * P:(n + 1) * P], c["ident"])
                    mm.then_inc(turned, 1)

        @block.scalar
        def _(sc):
            sc.sem_inc(rows_out, 2)
            with sc.Fori(0, turns) as i:
                for t in range(2):
                    sc.wait_ge(panel_done, i * slots + (t + 1) * per_tile)
                    sc.wait_ge(added, i * 2 + (t + 1))
                    sc.activation(rows[:, t], ps[t][:, 0:width], ACT.Copy).then_inc(rows_out, 1)

        @block.vector
        def _(ve):
            ve.sem_inc(added, 2)
            with ve.Fori(0, turns) as i:
                for t in range(2):
                    ve.wait_ge(turned, i * 2 + (t + 1))
                    sums = ps[2 + t][:, 0:width].rearrange("p (n g v) -> p g n v", n=3, g=4)
                    for j, v in enumerate(which):
                        m = ve.tensor_tensor(split(mod[:, :, j])[:, i * 2 + t], sums[:, :, :, v],
                                             split(bias)[:, i * 2 + t], ADD)
                    m.then_inc(added, 1)


def attention(nc, c, ps, ar, q_of, k_of, v_of, out_of, n_heads, n_keys):
    kt = n_keys // P
    with Stage(nc, "attention") as st:
        prob = ar.take(4, n_keys)
        probT = ar.take(2, kt, T)
        low = st.sb("low", [P, 4])
        tot = st.sb("tot", [P, 4])
        inv = st.sb("inv", [P, 4])
        scored, lowest, exped, inverted, scaled, turned, copied, mixed, stored = (st.sem(n) for n in (
            "scored", "lowest", "exped", "inverted", "scaled", "turned", "copied", "mixed", "stored"))
        units = [(h, t) for h in range(n_heads) for t in range(NT)]
        with st.block() as block:
            @block.tensor
            def _(pe):
                def scores(u):
                    h, t = units[u]
                    if u >= 4:
                        pe.wait_ge(exped, u - 3)
                    pe.matmul(ps[u % 4][:, 0:n_keys], q_of(h, t), k_of(h), start=True, stop=True).then_inc(scored, 1)

                def turn(u):
                    pe.wait_ge(scaled, u + 1)
                    if u >= 2:
                        pe.wait_ge(copied, u - 1)
                    for j in range(kt):
                        mm = pe.transpose(ps[4 + u % 2][:, j * P:(j + 1) * P], prob[:, u % 4, j * P:(j + 1) * P],
                                          c["ident"][:, :])
                    mm.then_inc(turned, 1)

                def mix(h):
                    pe.wait_ge(copied, 2 * h + 2)
                    if h >= 2:
                        pe.wait_ge(stored, h - 1)
                    o = out_of(h)
                    for j in range(kt):
                        mm = pe.matmul(ps[6 + h % 2][o[0]:o[0] + HEAD, 0:T], v_of(h, j), probT[:, h % 2, j],
                                       start=j == 0, stop=j == kt - 1)
                    mm.then_inc(mixed, 1)

                for u in range(len(units) + 3):
                    if u < len(units):
                        scores(u)
                    if 2 <= u < len(units) + 2:
                        turn(u - 2)
                    if u >= 4 and u % 2 == 0:
                        mix(u // 2 - 2)

            @block.vector
            def _(ve):
                def head(u):
                    ve.wait_ge(scored, u + 1)
                    if u >= 4:
                        ve.wait_ge(exped, u - 3)
                    ve.tensor_reduce(low[:, u % 4:u % 4 + 1], ps[u % 4][:, 0:n_keys], AX.X, MAX,
                                     negate=True).then_inc(lowest, 1)

                def tail(u):
                    ve.wait_ge(exped, u + 1)
                    ve.reciprocal(inv[:, u % 4:u % 4 + 1], tot[:, u % 4:u % 4 + 1]).then_inc(inverted, 1)
                    ve.wait_ge(inverted, u + 1)
                    ve.tensor_scalar(prob[:, u % 4], prob[:, u % 4], inv[:, u % 4:u % 4 + 1], None,
                                     MUL).then_inc(scaled, 1)

                for u in range(len(units) + 1):
                    if u < len(units):
                        head(u)
                    if u >= 1:
                        tail(u - 1)

            @block.scalar
            def _(sc):
                def turn_out(u):
                    h, t = units[u]
                    sc.wait_ge(turned, u + 1)
                    if u >= 4:
                        sc.wait_ge(mixed, h - 1)
                    sc.activation(probT[:, h % 2, :, t * P:(t + 1) * P],
                                  ps[4 + u % 2][:, 0:n_keys].rearrange("p (j n) -> p j n", n=P),
                                  ACT.Copy).then_inc(copied, 1)

                def store(h):
                    sc.wait_ge(mixed, h + 1)
                    o = out_of(h)
                    sc.activation(o[1], ps[6 + h % 2][o[0]:o[0] + HEAD, 0:T], ACT.Copy).then_inc(stored, 1)

                for u in range(len(units) + 4):
                    if u < len(units):
                        sc.wait_ge(lowest, u + 1)
                        if u >= 4:
                            sc.wait_ge(turned, u - 3)
                        sc.activation(prob[:, u % 4], ps[u % 4][:, 0:n_keys], ACT.Exp, bias=low[:, u % 4:u % 4 + 1],
                                      accum_out=tot[:, u % 4:u % 4 + 1]).then_inc(exped, 1)
                    if 2 <= u < len(units) + 2:
                        turn_out(u - 2)
                    if u >= 5 and u % 2 == 1:
                        store((u - 5) // 2)


def head_rms(nc, c, ps, x, n, w, gain, scale):
    with Stage(nc, "head_rms") as st:
        flat = x.rearrange("p a b -> p (a b)")
        groups = n * w // 512
        sq = st.sb("sq", [P, n * w])
        root = st.sb("root", [P, n * w])
        squared, summed, rooted, inverted, scaled = (
            st.sem(k) for k in ("squared", "summed", "rooted", "inverted", "scaled"))
        with st.block() as block:
            @block.scalar
            def _(sc):
                sc.activation(sq[:, :], flat, ACT.Square).then_inc(squared, 1)
                for g in range(groups):
                    sc.wait_ge(summed, g + 1)
                    sc.activation(root[:, g * 512:(g + 1) * 512], ps[g][:, :], ACT.Sqrt, bias=c["eps"][:, 0:1],
                                  scale=1.0 / HEAD).then_inc(rooted, 1)

            @block.tensor
            def _(pe):
                pe.wait_ge(squared, 1)
                for g in range(groups):
                    pe.matmul(ps[g][:, :], c["ones_head"][:, :], sq[:, g * 512:(g + 1) * 512],
                              start=True, stop=True).then_inc(summed, 1)

            @block.vector
            def _(ve):
                for g in range(groups):
                    col = slice(g * 512, (g + 1) * 512)
                    ve.wait_ge(rooted, g + 1)
                    ve.reciprocal(root[:, col], root[:, col]).then_inc(inverted, 1)
                    ve.wait_ge(inverted, g + 1)
                    ve.scalar_tensor_tensor(flat[:, col], flat[:, col], gain, root[:, col], MUL, MUL)\
                        .then_inc(scaled, 1)
                if scale != 1.0:
                    ve.wait_ge(scaled, groups)
                    ve.tensor_scalar(flat, flat, scale, None, MUL)


def rotate(nc, c, ps, x, n, rows, swap, cos, sin):
    with Stage(nc, "rotate") as st:
        turned = st.sb("turned", [rows, n, T])
        swapped, by_sin, by_cos = st.sem("swapped"), st.sem("by_sin"), st.sem("by_cos")
        pairs = (n + 1) // 2
        with st.block() as block:
            @block.tensor
            def _(pe):
                for j in range(pairs):
                    k = min(2, n - 2 * j)
                    pe.matmul(ps[j][0:rows, 0:k * T], swap, x[:, 2 * j:2 * j + k],
                              start=True, stop=True).then_inc(swapped, 1)

            @block.vector
            def _(ve):
                for j in range(pairs):
                    k = min(2, n - 2 * j)
                    tiles = slice(2 * j, 2 * j + k)
                    ve.wait_ge(swapped, j + 1)
                    ve.tensor_tensor(turned[:, tiles], ps[j][0:rows, 0:k * T].rearrange("p (a b) -> p a b", b=T),
                                     sin.unsqueeze(1).broadcast_to([rows, k, T]), MUL).then_inc(by_sin, 1)
                    ve.tensor_tensor(x[:, tiles], x[:, tiles], cos.unsqueeze(1).broadcast_to([rows, k, T]),
                                     MUL).then_inc(by_cos, 1)
                    ve.wait_ge(by_sin, j + 1)
                    ve.wait_ge(by_cos, j + 1)
                    ve.tensor_tensor(x[:, tiles], x[:, tiles], turned[:, tiles], ADD)


def turn_tokens(nc, c, ps, x_of, n, out_of):
    with Stage(nc, "turn_tiles") as st:
        turned, copied = st.sem("turned"), st.sem("copied")
        groups = (n + 3) // 4
        with st.block() as block:
            @block.tensor
            def _(pe):
                for g in range(groups):
                    if g >= 8:
                        pe.wait_ge(copied, g - 7)
                    for j in range(4 * g, min(4 * g + 4, n)):
                        mm = pe.transpose(ps[g % 8][:, (j % 4) * P:(j % 4 + 1) * P], x_of(j), c["ident"][:, :])
                    mm.then_inc(turned, 1)

            @block.vector
            def _(ve):
                for g in range(groups):
                    k = min(4, n - 4 * g)
                    ve.wait_ge(turned, g + 1)
                    ve.tensor_copy(out_of(g), ps[g % 8][:, 0:k * P].rearrange("p (a b) -> p a b", b=P))\
                        .then_inc(copied, 1)


def sine(ve, link, out, x, tmp, quarter):
    magic = 12582912.0
    link(ve.tensor_scalar(tmp, x, 1.0 / (2 * PI), 0.25 if quarter else 0.0, MUL, ADD))
    link(ve.tensor_scalar(tmp, tmp, magic, None, ADD))
    link(ve.tensor_scalar(tmp, tmp, magic, None, SUB))
    link(ve.scalar_tensor_tensor(out, tmp, -6.28125, x, MUL, ADD))
    link(ve.scalar_tensor_tensor(out, tmp, -0.0019350051879882812, out, MUL, ADD))
    link(ve.scalar_tensor_tensor(out, tmp, -3.0199159819567e-07, out, MUL, ADD))
    if quarter:
        link(ve.tensor_scalar(out, out, PI / 2, None, ADD))
    link(ve.tensor_scalar(out, out, 3.1415925, -3.1415925, ALU.min, MAX))


def long_conv(nc, c, ps, dft, inv, spec, order, z, bias, gate, out):
    with Stage(nc, "long_conv") as st:
        zt = st.sb("zt", [P, NT, T])
        f1 = st.sb("f1", [P, 4, T])
        f2 = st.sb("f2", [P, 4, T])
        turned, copied, transformed, mixed, inverse, gated, products = (
            st.sem(n) for n in ("turned", "copied", "transformed", "mixed", "inverse", "gated", "products"))
        s = lambda f: spec[:, f, order * T:(order + 1) * T]
        with st.block() as block:
            @block.tensor
            def _(pe):
                for t in range(NT):
                    for ch in range(2):
                        mm = pe.transpose(ps[0][:, (2 * t + ch) * P:(2 * t + ch + 1) * P],
                                          z[:, ch, t * P:(t + 1) * P], c["ident"][:, :])
                mm.then_inc(turned, 1)
                pe.wait_ge(copied, 1)
                for f in range(4):
                    for t in range(NT):
                        mm = pe.matmul(ps[1 + f][:, 0:T], dft[:, t, f * P:(f + 1) * P], zt[:, t],
                                       start=t == 0, stop=t == NT - 1)
                mm.then_inc(transformed, 1)
                pe.wait_ge(mixed, 1)
                for ch in range(2):
                    for f in range(4):
                        mm = pe.matmul(ps[5 + ch][:, 0:T], f1[:, f, ch * P:(ch + 1) * P], inv[:, f],
                                       start=f == 0, stop=f == 3)
                    mm.then_inc(inverse, 1)

            @block.vector
            def _(ve):
                ve.wait_ge(turned, 1)
                ve.tensor_copy(zt[:, :, :], ps[0][:, :].rearrange("p (a b) -> p a b", b=T)).then_inc(copied, 1)
                ve.wait_ge(transformed, 1)
                for f in range(2):
                    last = 4 if f == 0 else 1
                    ve.tensor_tensor(f1[:, f], ps[1 + f][:, 0:T], s(f), MUL)
                    ve.tensor_tensor(f2[:, f], ps[3 + f][:, 0:T], s(2 + f), MUL)
                    ve.tensor_tensor(f1[:, 2 + f], ps[3 + f][:, 0:T], s(last), MUL)
                    ve.tensor_tensor(f2[:, 2 + f], ps[1 + f][:, 0:T], s(2 + f), MUL).then_inc(products, 1)
                ve.wait_ge(products, 2)
                ve.tensor_tensor(f1[:, 0:2], f1[:, 0:2], f2[:, 0:2], SUB)
                ve.tensor_tensor(f1[:, 2:4], f1[:, 2:4], f2[:, 2:4], ADD).then_inc(mixed, 1)
                for ch in range(2):
                    ve.wait_ge(inverse, ch + 1)
                    ve.scalar_tensor_tensor(out[:, ch], z[:, ch], bias[:, ch:ch + 1], ps[5 + ch][:, 0:T], MUL, ADD)\
                        .then_inc(gated, 1)
                    ve.wait_ge(gated, ch + 1)
                    ve.tensor_tensor(out[:, ch], out[:, ch], gate[:, ch], MUL)


def fourier(nc, c, ps, cst, u, out):
    with Stage(nc, "fourier") as st:
        chan = st.sb("chan", [P, 2 * P])
        token = st.sb("token", [P, NT, 512])
        mid = st.sb("mid", [P, 2, NT, 2 * P])
        consts, first, copied, second = (st.sem(n) for n in ("consts", "first", "copied", "second"))
        with st.block() as block:
            @block.sync
            def _(sp):
                sp.dma_start(chan[:, :], cst["fn_channel"]).then_inc(consts, 16)
                sp.dma_start(token[:, :, :], cst["fn_token"]).then_inc(consts, 16)

            @block.tensor
            def _(pe):
                pe.wait_ge(consts, 32)
                for ch in range(2):
                    for t in range(NT):
                        pe.matmul(ps[2 * ch + t][:, 0:2 * P], u[:, ch, t * P:(t + 1) * P], chan[:, :],
                                  start=True, stop=True).then_inc(first, 1)
                pe.wait_ge(copied, 4)
                for ch in range(2):
                    for n, (t, part) in enumerate((t, part) for t in range(NT) for part in range(2)):
                        mm = pe.matmul(ps[4 + ch][:, 0:T], mid[:, ch, t, part * P:(part + 1) * P],
                                       token[:, t, part * T:(part + 1) * T], start=n == 0, stop=n == 3)
                    mm.then_inc(second, 1)

            @block.scalar
            def _(sc):
                for ch in range(2):
                    for t in range(NT):
                        sc.wait_ge(first, 2 * ch + t + 1)
                        sc.activation(mid[:, ch, t], ps[2 * ch + t][:, 0:2 * P], ACT.Copy).then_inc(copied, 1)
                for ch in range(2):
                    sc.wait_ge(second, ch + 1)
                    sc.activation(out[:, ch], ps[4 + ch][:, 0:T], ACT.Copy)


def project_in(nc, c, ps, ring, I, xT, ctxT, hT, mod, gain, proj, kv):
    with Stage(nc, "project_in") as st:
        h = hT[:, :, 0:T]
        d = Dense(nc, st, c, ring, ps, xT, h)
        d.norms[1] = (ctxT, hT[:, :, T:2 * T], ps[7])
        kv_made = st.sem("kv_made")
        slots, turns = 6, 3
        none = [0] * SLOTS
        pairs = proj.rearrange("p (q a) t -> p q (a t)", a=2)
        with st.block() as block:
            @block.sync
            def _(sp):
                for u in range(slots):
                    sp.dma_start(d.slots[u], I["w_in"][u]).then_inc(d.loaded[u], 16)
                sp.dma_start(d.slots[slots], I["w_kv"][0]).then_inc(d.loaded[slots], 16)
                with sp.Fori(1, turns) as i:
                    for u in range(slots):
                        sp.wait_ge(d.panel_done, i * slots + (u + 1 - slots))
                        sp.dma_start(d.slots[u], I["w_in"][i * slots + u]).then_inc(d.loaded[u], 16)

            @block.tensor
            def _(pe):
                for m in range(2):
                    for k in range(KD):
                        d.pe_sum(pe, m, k)
                with pe.Fori(0, turns) as i:
                    for u in range(slots):
                        d.pe_pair(pe, i, u, i * slots, none, 0)
                pe.wait_ge(d.loaded[slots], 16)
                pe.wait_ge(d.h_ready, 2 * KD)
                w = d.slots[slots].rearrange("p (b n) -> p b n", n=P)
                for j in range(2):
                    for k in range(KD):
                        mm = pe.matmul(ps[3 + j], w[:, j * KD + k], hT[:, k], start=k == 0, stop=k == KD - 1)
                    mm.then_inc(kv_made, 1)

            @block.scalar
            def _(sc):
                for m in range(2):
                    for k in range(KD):
                        d.act_square(sc, m, k)

                def take(q, u, func):
                    sc.wait_ge(d.panel_done, q + u + 1)
                    sc.activation(pairs[:, q + u], ps[u % 3], func).then_inc(d.bank_free, 1)

                d.act_norm(sc, 0, mod[:, 0:8, 0])
                for u in range(slots):
                    take(0, u, ACT.Copy)
                d.act_norm(sc, 1, mod[:, 0:8, 1])
                with sc.Fori(1, turns) as i:
                    for u in range(slots):
                        take(i * slots, u, ACT.Sigmoid)
                for j in range(2):
                    sc.wait_ge(kv_made, j + 1)
                    sc.activation(kv[:, j], ps[3 + j], ACT.Copy)

            @block.vector
            def _(ve):
                ve.sem_inc(d.bank_free, 2)
                d.dve_norm(ve, 0, gain[:, 0])
                d.dve_norm(ve, 1, gain[:, 1])


def project_out(nc, c, ps, ring, I, xT, h, mod, gain, proj, mix, router):
    with Stage(nc, "project_out") as st:
        d = Dense(nc, st, c, ring, ps, xT, h)
        spare = Arena(ring[:, 8 * BLK * P:], RING_COLS - 8 * BLK * P)
        merged, part = spare.take(KD, T), spare.take(2, 3, T)
        merging, router_here = st.sem("merging"), st.sem("router_here")
        panels, none = 4, [0] * SLOTS
        with st.block() as block:
            @block.sync
            def _(sp):
                for u in range(panels):
                    sp.dma_start(d.slots[u], I["w_branch"][u]).then_inc(d.loaded[u], 16)
                for u in range(panels):
                    sp.dma_start(d.slots[panels + u], I["w_out"][u]).then_inc(d.loaded[panels + u], 16)
                sp.dma_start(router, I["small1"][:, SM1["router"][0]:SM1["router"][1]]).then_inc(router_here, 16)
                sp.wait_ge(router_here, 16)

            @block.tensor
            def _(pe):
                for q in range(panels):
                    w = d.slots[q].rearrange("p (b n) -> p b n", n=P)
                    pe.wait_ge(d.loaded[q], 16)
                    if q >= 2:
                        pe.wait_ge(d.bank_free, 2 + q - 1)
                    for j in range(2):
                        for b, (lo, hi) in enumerate(((0, 4), (4, 6), (6, 8))):
                            for k in range(lo, hi):
                                mm = pe.matmul(ps[5 * (q % 2) + b][:, j * T:(j + 1) * T], w[:, j * KD + k],
                                               mix[:, k], start=k == lo, stop=k == hi - 1)
                    mm.then_inc(d.panel_done, 1)
                d.pe_add(pe, merged, KD, 0, none, panels, 0, ready=lambda k: k // 2 + 1)

            @block.scalar
            def _(sc):
                d.act_squares(sc, 0, 0)
                d.act_norm(sc, 0, mod[:, 24:32, 0])

            @block.vector
            def _(ve):
                ve.sem_inc(d.bank_free, 2)
                for q in range(panels):
                    ve.wait_ge(d.panel_done, q + 1)
                    for j in range(2):
                        n = 2 * q + j
                        for b in range(3):
                            m = ve.tensor_tensor(part[:, j, b], ps[5 * (q % 2) + b][:, j * T:(j + 1) * T],
                                                 proj[:, 12 + b * KD + n], MUL)
                        m.then_inc(merging, 1)
                        ve.wait_ge(merging, 2 * n + 1)
                        ve.tensor_tensor(part[:, j, 0], part[:, j, 0], part[:, j, 1], ADD).then_inc(merging, 1)
                        ve.wait_ge(merging, 2 * n + 2)
                        m = ve.tensor_tensor(merged[:, n], part[:, j, 0], part[:, j, 2], ADD)
                    m.then_inc(d.bank_free, 1)
                d.dve_add(ve, 0, mod[:, 16:24, 0])
                d.dve_norm(ve, 0, gain[:, 2])


def first_branches(nc, c, ps, ring, cst, vec, spec, proj, kv, mix):
    v = lambda k, j=0, n=1: vec[:, V1[k][0] + j:V1[k][0] + j + n]
    with Stage(nc, "qkv") as st:
        axial = st.sb("axial", [P, 2, T])
        perm = st.sb("perm", [P, 2, P])
        k_other = st.sb("k_other", [P, 2 * T])
        v_tok = st.sb("v_tok", [P, 4, P])
        load_all(nc, [(axial[:, 0], cst["axial_cos"]), (axial[:, 1], cst["axial_sin"]),
                      (perm[:, 0], cst["swap_pair"]), (perm[:, 1], cst["swap_head"])])
        head_rms(nc, c, ps, proj[:, 0:4], 4, T, v("q_gain"), HEAD ** -0.5)
        head_rms(nc, c, ps, kv[:, 0:1], 1, 2 * T, v("k_gain"), 1.0)
        rotate(nc, c, ps, proj[:, 0:4], 4, P, perm[:, 0], axial[:, 0], axial[:, 1])
        rotate(nc, c, ps, kv[:, 0:1, 0:T], 1, P, perm[:, 0], axial[:, 0], axial[:, 1])
        turn_tokens(nc, c, ps, lambda j: kv[:, 1, j * P:(j + 1) * P], 4, lambda g: v_tok[:, :, :])
        with Stage(nc, "k_other") as s2:
            swapped = s2.sem("swapped")
            with s2.block() as block:
                @block.tensor
                def _(pe):
                    pe.matmul(ps[0][:, :], perm[:, 1], kv[:, 0], start=True, stop=True).then_inc(swapped, 1)

                @block.vector
                def _(ve):
                    ve.wait_ge(swapped, 1)
                    ve.tensor_copy(k_other[:, :], ps[0][:, :])

        def q_of(h, t):
            b = h % 2 * HEAD
            return proj[b:b + HEAD, h // 2, t * P:(t + 1) * P]

        def k_of(h):
            b = h % 2 * HEAD
            return kv[b:b + HEAD, 0] if h // 4 == h % 2 else k_other[b:b + HEAD, :]

        attention(nc, c, ps, Arena(ring, RING_COLS), q_of, k_of, lambda h, j: v_tok[:, j, h // 4 * HEAD:(h // 4 + 1) * HEAD],
                  lambda h: (h % 2 * HEAD, mix[h % 2 * HEAD:h % 2 * HEAD + HEAD, h // 2]), 8, 2 * T)

    with Stage(nc, "hyena") as st:
        ar = Arena(ring, RING_COLS)
        u, dft, inv = ar.take(6, T), ar.take(NT, 512), ar.take(4, T)
        load_all(nc, [(dft[:, :, :], cst["dft_signal"]), (inv[:, :, :], cst["dft_inverse"])])
        with Stage(nc, "short_conv") as s2:
            mid, ahead = s2.sem("mid"), s2.sem("ahead")
            with s2.block() as block:
                @block.vector
                def _(ve):
                    for j in range(6):
                        x = proj[:, 4 + j]
                        ve.tensor_scalar(u[:, j], x, v("short_w", 6 + j), v("short_b", j), MUL, ADD)\
                            .then_inc(mid, 1)
                        ve.wait_ge(mid, j + 1)
                        ve.scalar_tensor_tensor(u[:, j, 1:T], x[:, 0:T - 1], v("short_w", j), u[:, j, 1:T],
                                                MUL, ADD).then_inc(ahead, 1)
                        ve.wait_ge(ahead, j + 1)
                        ve.scalar_tensor_tensor(u[:, j, 0:T - 1], x[:, 1:T], v("short_w", 12 + j),
                                                u[:, j, 0:T - 1], MUL, ADD)
        z = st.sb("z", [P, 2, T])
        long_conv(nc, c, ps, dft, inv, spec, 0, u[:, 0:2], v("hy_bias", 0, 2), u[:, 2:4], z)
        long_conv(nc, c, ps, dft, inv, spec, 1, z, v("hy_bias", 2, 2), u[:, 4:6], mix[:, 4:6])
    fourier(nc, c, ps, cst, proj[:, 10:12], mix[:, 6:8])


def route(nc, c, ps, cst, router, hT, place_of, x_sel, slot, slot_loaded, src):
    with Stage(nc, "route") as st:
        e1 = st.sb("e1", [P, NT, E])
        top = st.sb("top", [P, NT])
        tot = st.sb("tot", [P, NT])
        aff = st.sb("aff", [P, NT, E])
        affT = st.sb("affT", [E, T])
        left = st.sb("left", [E, T])
        best = st.sb("best", [E, 8])
        mask = st.sb("mask", [E, T])
        place = st.sb("place", [E, T])
        zero = st.sb("zero", [E, T])
        placeT = st.sb("placeT", [P, NT, E])
        slots = st.sb("slots", [P, CAP])
        h_tok = st.sb("h_tok", [P, NT, D])
        sel = st.sb("sel", [P, NT, E, CAP])
        w_tok = st.sb("w_tok", [P, NT, E, 4, CAP])
        logits, highest, exped, shared, turned, chain, placed, placed_t, chosen, loaded = (
            st.sem(n) for n in ("logits", "highest", "exped", "shared", "turned", "chain", "placed", "placed_t",
                                "chosen", "loaded"))
        with st.block() as block:
            @block.sync
            def _(sp):
                sp.dma_start(slots[:, :], cst["slots"]).then_inc(loaded, 16)
                for u, panel in enumerate(slot):
                    sp.dma_start(panel, src[0, u]).then_inc(slot_loaded[u], 16)

            @block.tensor
            def _(pe):
                for t in range(NT):
                    for k in range(KD):
                        mm = pe.matmul(ps[0][:, t * E:(t + 1) * E], hT[:, k, t * P:(t + 1) * P],
                                       router[:, k * E:(k + 1) * E], start=k == 0, stop=k == KD - 1)
                mm.then_inc(logits, 1)
                pe.wait_ge(shared, 1)
                for t in range(NT):
                    mm = pe.transpose(ps[1][0:E, t * P:(t + 1) * P], aff[:, t], c["ident"][:, :])
                mm.then_inc(turned, 1)
                pe.wait_ge(placed, 1)
                for t in range(NT):
                    mm = pe.transpose(ps[2][:, t * E:(t + 1) * E], place[:, t * P:(t + 1) * P],
                                      c["ident"][0:E, 0:E])
                mm.then_inc(placed_t, 1)

            @block.scalar
            def _(sc):
                for t in range(NT):
                    sc.wait_ge(highest, NT)
                    sc.activation(e1[:, t], ps[0][:, t * E:(t + 1) * E], ACT.Exp, bias=top[:, t:t + 1],
                                  accum_out=tot[:, t:t + 1]).then_inc(exped, 1)

            @block.vector
            def _(ve):
                link = Chain(ve, chain)
                link(ve.memset(zero[:, :], 0.0))
                ve.wait_ge(logits, 1)
                for t in range(NT):
                    ve.tensor_reduce(top[:, t:t + 1], ps[0][:, t * E:(t + 1) * E], AX.X, MAX, negate=True)\
                        .then_inc(highest, 1)
                ve.wait_ge(exped, NT)
                link(ve.reciprocal(tot[:, :], tot[:, :]))
                for t in range(NT):
                    link(ve.tensor_scalar(aff[:, t], e1[:, t], tot[:, t:t + 1], None, MUL))
                ve.sem_inc(shared, 1)
                ve.wait_ge(turned, 1)
                link(ve.tensor_copy(affT[:, :], ps[1][0:E, 0:T]))
                link(ve.tensor_copy(left[:, :], ps[1][0:E, 0:T]))
                for _ in range(CAP // 8):
                    link(ve.max(best[:, :], left[:, :]))
                    link(ve.match_replace(left[:, :], best[:, :], left[:, :], -1.0))
                link(ve.tensor_tensor(mask[:, :], affT[:, :], left[:, :], ALU.not_equal))
                link(ve.tensor_tensor_scan(place[:, :], mask[:, :], zero[:, :], 0.0, ADD, ADD))
                link(ve.tensor_tensor(place[:, :], place[:, :], mask[:, :], MUL))
                ve.sem_inc(placed, 1)
                ve.wait_ge(placed_t, 1)
                link(ve.tensor_copy(placeT[:, :, :], ps[2][:, 0:NT * E].rearrange("p (a b) -> p a b", b=E)))
                ve.wait_ge(loaded, 16)
                for t in range(NT):
                    at = placeT[:, t].unsqueeze(2).broadcast_to([P, E, CAP])
                    link(ve.tensor_tensor(sel[:, t], at, slots[:, :].unsqueeze(1).broadcast_to([P, E, CAP]),
                                          ALU.is_equal))
                    for g in range(4):
                        ve.tensor_tensor(w_tok[:, t, :, g], sel[:, t],
                                         aff[:, t].unsqueeze(2).broadcast_to([P, E, CAP]), MUL)
        turn_tokens(nc, c, ps, lambda j: hT[:, j % KD, (j // KD) * P:(j // KD + 1) * P], NT * KD,
                    lambda g: h_tok[:, g // 2, (g % 2) * 512:(g % 2 + 1) * 512]
                    .rearrange("p (k n) -> p k n", n=P))
        turn_tokens(nc, c, ps, lambda j: w_tok[:, j % 2, j // 2].rearrange("p a b -> p (a b)"), NT * E,
                    lambda g: place_of[:, 2 * g:2 * g + 2].rearrange("p g (t n) -> p (g t) n", n=P))
        gathered = st.sem("gathered")
        with st.block() as block:
            @block.tensor
            def _(pe):
                for k in range(KD):
                    for t in range(NT):
                        mm = pe.matmul(ps[k][:, :], h_tok[:, t, k * P:(k + 1) * P],
                                       sel[:, t].rearrange("p a b -> p (a b)"), start=t == 0, stop=t == NT - 1)
                    mm.then_inc(gathered, 1)

            @block.vector
            def _(ve):
                for k in range(KD):
                    ve.wait_ge(gathered, k + 1)
                    ve.tensor_copy(x_sel[:, k], ps[k][:, :])


class Rotary:

    def __init__(self, st, cst, positions, tables):
        self.cst, self.positions, self.tables = cst, positions, tables
        self.pos_i = st.sb("pos_i", [P, T], I32)
        self.pos = st.sb("pos", [P, T])
        self.freq = st.sb("freq", [P, 6])
        self.ang = st.sb("ang", [P, 3, 2, T])
        self.tmp = st.sb("tmp", [P, T])
        self.landed, self.chain, self.angles, self.sines = (
            st.sem(n) for n in ("landed", "chain", "angles", "sines"))

    def sync(self, sp):
        sp.dma_start(self.pos_i, self.positions).then_inc(self.landed, 16)
        sp.dma_start(self.freq, self.cst["rot_freq"]).then_inc(self.landed, 16)

    def vector(self, ve):
        link = Chain(ve, self.chain)
        ve.wait_ge(self.landed, 32)
        link(ve.tensor_copy(self.pos, self.pos_i))
        for j in range(3):
            link(ve.tensor_scalar(self.ang[:, j, 0], self.pos, self.freq[:, 2 * j:2 * j + 1], None, MUL))
            sine(ve, link, self.ang[:, j, 1], self.ang[:, j, 0], self.tmp, False)
            sine(ve, link, self.tables[:, j, 0], self.ang[:, j, 0], self.tmp, True)
        ve.sem_inc(self.angles, 1)
        ve.wait_ge(self.sines, 1)
        for j in range(3):
            ve.tensor_scalar(self.tables[:, j, 1], self.ang[:, j, 0], self.freq[:, 2 * j + 1:2 * j + 2], None, MUL)

    def scalar(self, sc):
        sc.wait_ge(self.angles, 1)
        for j in range(3):
            sc.activation(self.ang[:, j, 0], self.ang[:, j, 1], ACT.Sin)
            m = sc.activation(self.tables[:, j, 0], self.tables[:, j, 0], ACT.Sin)
        m.then_inc(self.sines, 1)


def experts(nc, c, ps, slot, loaded, src, x_sel, place, xT, gate, cst, positions, tables):
    up_panels, down_panels = KD, 4
    slots, n = len(slot), KD + 4
    with Stage(nc, "experts") as st:
        x_cur = st.sb("x_cur", [P, KD, CAP])
        silu = st.sb("silu", [P, 512])
        hid = st.sb("hid", [P, 512])
        hidT = st.sb("hidT", [P, 4, 4, CAP])
        y = st.sb("y", [P, D])
        rotary = Rotary(st, cst, positions, tables)
        x_ready, panel_done, silu_done, hid_done, turned, turned_out, y_low, y_high, placed, added = (
            st.sem(k) for k in ("x_ready", "panel_done", "silu_done", "hid_done", "turned", "turned_out", "y_low",
                                "y_high", "placed", "added"))
        xs = x_sel.rearrange("p k (e s) -> p k e s", s=CAP)
        quarter = [slice(g * CAP, (g + 1) * CAP) for g in range(4)]
        with st.block() as block:
            @block.sync
            def _(sp):
                rotary.sync(sp)
                for u in range(slots, n):
                    sp.wait_ge(panel_done, u + 1 - slots)
                    sp.dma_start(slot[u % slots], src[0, u]).then_inc(loaded[u % slots], 16)
                with sp.Fori(1, E) as e:
                    for u in range(n):
                        sp.wait_ge(panel_done, e * n + (u + 1 - slots))
                        sp.dma_start(slot[u % slots], src[e, u]).then_inc(loaded[u % slots], 16)

            @block.tensor
            def _(pe):
                with pe.Fori(0, E) as e:
                    pe.wait_ge(x_ready, e + 1)
                    for u in range(up_panels):
                        w = slot[u % slots].rearrange("p (b g n) -> p b g n", b=2, g=4)
                        pe.wait_ge(loaded[u % slots], e * 32 + (u // slots + 1) * 16)
                        for b in range(2):
                            for g in range(4):
                                mm = pe.matmul(ps[b][quarter[g], :], x_cur[:, u], w[:, b, g], start=u == 0,
                                               stop=u == up_panels - 1)
                        mm.then_inc(panel_done, 1)
                    pe.wait_ge(hid_done, e + 1)
                    for s in range(4):
                        mm = pe.transpose(ps[4][:, s * P:(s + 1) * P], hid[:, s * P:(s + 1) * P], c["ident"])
                    mm.then_inc(turned, 1)
                    pe.wait_ge(turned_out, e + 1)
                    for s in range(down_panels):
                        u = up_panels + s
                        w = slot[u % slots].rearrange("p (g b n) -> p g b n", g=4, b=2)
                        pe.wait_ge(loaded[u % slots], e * 32 + (u // slots + 1) * 16)
                        for b in range(2):
                            for g in range(4):
                                mm = pe.matmul(ps[2 + b][quarter[g], :], hidT[:, s, g], w[:, g, b], start=s == 0,
                                               stop=s == down_panels - 1)
                        mm.then_inc(panel_done, 1)
                    pe.wait_ge(y_low, e + 1)
                    pe.wait_ge(y_high, e + 1)
                    for half in range(2):
                        pe.wait_ge(added, e * 2 + (half + 1))
                        for j in range(4):
                            k = 4 * half + j
                            mm = pe.matmul(ps[5 + j // 2][:, (j % 2) * T:(j % 2 + 1) * T], y[:, k * P:(k + 1) * P],
                                           place[:, e], start=True, stop=True)
                        mm.then_inc(placed, 1)

            @block.scalar
            def _(sc):
                def tokens(e):
                    sc.activation(x_cur, xs[:, :, e], ACT.Copy).then_inc(x_ready, 1)

                def middle(e, more):
                    sc.wait_ge(panel_done, e * n + up_panels)
                    sc.activation(silu, ps[0], ACT.Silu).then_inc(silu_done, 1)
                    if more:
                        tokens(e + 1)
                    sc.wait_ge(turned, e + 1)
                    sc.activation(hidT.rearrange("p s g c -> p (s g c)"), ps[4], ACT.Copy).then_inc(turned_out, 1)
                    sc.wait_ge(panel_done, e * n + n)
                    sc.activation(y[:, 0:512], ps[2], ACT.Copy).then_inc(y_low, 1)

                tokens(0)
                rotary.scalar(sc)
                with sc.Fori(0, E - 1) as e:
                    middle(e, True)
                middle(E - 1, False)

            @block.vector
            def _(ve):
                ve.sem_inc(added, 1)
                rotary.vector(ve)
                with ve.Fori(0, E) as e:
                    ve.wait_ge(silu_done, e + 1)
                    ve.tensor_tensor(hid, ps[1], silu, MUL).then_inc(hid_done, 1)
                    ve.wait_ge(panel_done, e * n + n)
                    ve.tensor_copy(y[:, 512:D], ps[3]).then_inc(y_high, 1)
                    for half in range(2):
                        ve.wait_ge(placed, e * 2 + (half + 1))
                        for j in range(4):
                            k = 4 * half + j
                            m = ve.scalar_tensor_tensor(xT[:, k], ps[5 + j // 2][:, (j % 2) * T:(j % 2 + 1) * T],
                                                        gate[:, k:k + 1], xT[:, k], MUL, ADD)
                        m.then_inc(added, 1)


BLK = 16
SLOTS = 11
SIDE = 4


class Dense:

    def __init__(self, nc, st, c, ring, ps, xT, hT, first_slot=0):
        self.c, self.ps, self.xT, self.hT, self.first_slot = c, ps, xT, hT, first_slot
        self.slots = [ring[:, u * BLK * P:(u + 1) * BLK * P] for u in range(SLOTS)]
        self.loaded = [st.sem(f"loaded{u}") for u in range(SLOTS)]
        self.panel_done, self.bank_free, self.silu_done = (st.sem(n) for n in ("panel_done", "bank_free", "silu_done"))
        self.chunk_done, self.x_updated, self.squared = (st.sem(n) for n in ("chunk_done", "x_updated", "squared"))
        self.summed, self.rooted, self.inverted = (st.sem(n) for n in ("summed", "rooted", "inverted"))
        self.scaled, self.h_ready = st.sem("scaled"), st.sem("h_ready")
        self.sq = st.sb("sq", [P, 4, T])
        self.root = st.sb("root", [P, T])
        self.rstd = st.sb("rstd", [P, T])
        self.silu = st.sb("silu", [P, 3, T])
        self.norms = {}

    def norm(self, m):
        return self.norms.get(m, (self.xT, self.hT, self.ps[6]))

    def slot(self, u):
        return (u + self.first_slot) % SLOTS

    def act_square(self, sc, m, k):
        if 8 * m + k >= 4:
            sc.wait_ge(self.summed, 8 * m + k - 3)
        sc.activation(self.sq[:, k % 4], self.norm(m)[0][:, k], ACT.Square).then_inc(self.squared, 1)

    def pe_sum(self, pe, m, k):
        pe.wait_ge(self.squared, 8 * m + k + 1)
        if m and k == 0 and m not in self.norms:
            pe.wait_ge(self.rooted, m)
        pe.matmul(self.norm(m)[2][:, 0:T], self.c["ones"], self.sq[:, k % 4], start=k == 0, stop=k == KD - 1)\
            .then_inc(self.summed, 1)

    def act_norm(self, sc, m, shift):
        sc.wait_ge(self.summed, 8 * m + 8)
        _, out, bank = self.norm(m)
        if m:
            sc.wait_ge(self.inverted, m)
        sc.activation(self.root, bank[:, 0:T], ACT.Sqrt, bias=self.c["eps"][:, 0:1], scale=1.0 / D)\
            .then_inc(self.rooted, 1)
        for k in range(KD):
            sc.wait_ge(self.scaled, 8 * m + k + 1)
            sc.activation(out[:, k], out[:, k], ACT.Identity, bias=shift[:, k:k + 1])\
                .then_inc(self.h_ready, 1)

    def dve_norm(self, ve, m, gain):
        ve.wait_ge(self.rooted, m + 1)
        ve.reciprocal(self.rstd, self.root).then_inc(self.inverted, 1)
        ve.wait_ge(self.inverted, m + 1)
        x, out, _ = self.norm(m)
        for k in range(KD):
            ve.scalar_tensor_tensor(out[:, k], x[:, k], gain[:, k:k + 1], self.rstd, MUL, MUL)\
                .then_inc(self.scaled, 1)

    def pe_pair(self, pe, i, u, q, loads, m):
        s = self.slot(u)
        w = self.slots[s].rearrange("p (b n) -> p b n", n=P)
        pe.wait_ge(self.loaded[s], i * 16 + 16 * (loads[s] + 1))
        pe.wait_ge(self.bank_free, q + u + 1)
        for j in range(2):
            for k in range(KD):
                if u == 0 and j == 0:
                    pe.wait_ge(self.h_ready, 8 * m + k + 1)
                mm = pe.matmul(self.ps[u % 3][:, j * T:(j + 1) * T], w[:, j * KD + k], self.hT[:, k],
                               start=k == 0, stop=k == KD - 1)
        mm.then_inc(self.panel_done, 1)

    def act_gate(self, sc, u, q):
        sc.wait_ge(self.panel_done, q + u + 1)
        sc.activation(self.silu[:, u % 3], self.ps[u % 3][:, 0:T], ACT.Silu).then_inc(self.silu_done, 1)

    def dve_gate(self, ve, u, q, hid):
        ve.wait_ge(self.silu_done, q + u + 1)
        ve.tensor_tensor(hid[:, q + u], self.ps[u % 3][:, T:2 * T], self.silu[:, u % 3], MUL)\
            .then_inc(self.bank_free, 1)

    def pe_add(self, pe, x, nk, n, loads, u0, m=None, ready=None):
        for q in range(KD):
            if n + q >= 2:
                pe.wait_ge(self.x_updated, n + q - 1)
            for k in range(nk):
                b = q * nk + k
                s = self.slot(u0 + b // BLK)
                if ready and q == 0:
                    pe.wait_ge(self.bank_free, ready(k) + 2)
                if b % BLK == 0:
                    pe.wait_ge(self.loaded[s], 16 * (loads[s] + 1))
                w = self.slots[s][:, b % BLK * P:(b % BLK + 1) * P]
                mm = pe.matmul(self.ps[3 + q % 2][:, 0:T], w, x[:, k], start=k == 0, stop=k == nk - 1)
            mm.then_inc(self.chunk_done, 1)
            if m is not None and q:
                self.pe_sum(pe, m, q - 1)
        if m is not None:
            self.pe_sum(pe, m, KD - 1)

    def dve_add(self, ve, n, gain):
        for q in range(KD):
            ve.wait_ge(self.chunk_done, n + q + 1)
            ve.scalar_tensor_tensor(self.xT[:, q], self.ps[3 + q % 2][:, 0:T], gain[:, q:q + 1], self.xT[:, q],
                                    MUL, ADD).then_inc(self.x_updated, 1)

    def act_squares(self, sc, n, m):
        for q in range(KD):
            sc.wait_ge(self.x_updated, n + q + 1)
            self.act_square(sc, m, q)


def chunks_of(panel, nk):
    return -(-(panel + 1) * BLK // nk)


def layer_in(nc, st, c, ring, ps, xT, hT, cond, vec, small, mod, gain, proj, vec_src, small_src, w_ada, w_ff, w_in):
    d = Dense(nc, st, c, ring, ps, xT, hT)
    side = ring[:, SLOTS * BLK * P:]
    side_loaded = [st.sem(f"side_loaded{u}") for u in range(SIDE)]
    side_done, rows_out, turned, added, gained, vec_here, small_here = (
        st.sem(n) for n in ("side_done", "rows_out", "turned", "added", "gained", "vec_here", "small_here"))
    rows = st.sb("rows", [P, 3, 2 * P])
    side_slots = [side[:, u * BLK * P:(u + 1) * BLK * P] for u in range(SIDE)]
    hid = proj[:, 0:KF]
    head, rest = 12, 24
    beside = [(0, 1), (2,), (3,), (4,), (5,), (6,), (7,), (8,), (9,), (10, 11), ()]
    ends = {2: 0, 6: 1, 9: 2}
    turns_tile = {3: 0, 7: 1, 10: 2}
    bias = vec[:, V2["b_ada"][0]:V2["b_ada"][1]].rearrange("p (t g n) -> p t g n", g=4, n=2)
    mods = mod.rearrange("p (t g n) -> p t g n", g=4, n=2)
    before = [0] * 3 + [1] * 8
    with st.block() as block:
        @block.sync
        def _(sp):
            sp.dma_start(vec, vec_src).then_inc(vec_here, 16)
            for a in range(head):
                if a < SIDE:
                    sp.dma_start(side_slots[a], w_ada[a]).then_inc(side_loaded[a], 16)
                else:
                    sp.dma_start(d.slots[a - 1], w_ada[a]).then_inc(d.loaded[a - 1], 16)
            for u in range(3):
                sp.dma_start(d.slots[u], w_ff[u]).then_inc(d.loaded[u], 16)
            for n in range(SIDE):
                sp.wait_ge(side_done, n + 1)
                sp.dma_start(side_slots[n], w_ada[head + n]).then_inc(side_loaded[n], 16)
            for u in range(3, SLOTS):
                sp.wait_ge(side_done, u + 2)
                sp.dma_start(d.slots[u], w_ff[u]).then_inc(d.loaded[u], 16)
            for i in range(2):
                for u in range(SLOTS):
                    sp.wait_ge(d.panel_done, i * SLOTS + u + 1)
                    sp.dma_start(d.slots[u], w_ff[(i + 1) * SLOTS + u]).then_inc(d.loaded[u], 16)
                    for n in beside[u]:
                        n += i * 12
                        if n + SIDE < rest:
                            sp.wait_ge(side_done, head + n + 1)
                            sp.dma_start(side_slots[n % SIDE], w_ada[head + n + SIDE])\
                                .then_inc(side_loaded[n % SIDE], 16)
            for j in range(12):
                if j < 6:
                    sp.wait_ge(d.chunk_done, chunks_of(j, KF))
                else:
                    sp.wait_ge(d.panel_done, KF + j - 5)
                sp.dma_start(d.slots[j % 6], w_in[j]).then_inc(d.loaded[j % 6], 16)
                if j == 5:
                    sp.wait_ge(side_done, head + rest)
                    sp.dma_start(small, small_src).then_inc(small_here, 16)
            sp.wait_ge(small_here, 16)

        @block.tensor
        def _(pe):
            def tile_panel(w, j, n):
                if j == 0:
                    pe.wait_ge(rows_out, n + 1)
                w = w.rearrange("p (k g n) -> p k g n", k=2, g=4)
                for k in range(2):
                    for g in range(4):
                        mm = pe.matmul(ps[5][32 * g:32 * g + 32, 0:2 * P], cond[:, 2 * j + k], w[:, k, g],
                                       start=j == 0 and k == 0, stop=j == 3 and k == 1)
                mm.then_inc(side_done, 1)

            def turn(t, n):
                pe.wait_ge(rows_out, n + 2)
                pe.wait_ge(added, n + 1)
                for j in range(2):
                    mm = pe.transpose(ps[7][:, j * P:(j + 1) * P], rows[:, t, j * P:(j + 1) * P], c["ident"])
                mm.then_inc(turned, 1)

            for k in range(KD):
                d.pe_sum(pe, 0, k)
            for t in range(3):
                for j in range(4):
                    a = 4 * t + j
                    if a < SIDE:
                        pe.wait_ge(side_loaded[a], 16)
                        tile_panel(side_slots[a], j, t)
                    else:
                        pe.wait_ge(d.loaded[a - 1], 16)
                        tile_panel(d.slots[a - 1], j, t)
                turn(t, t)
            with pe.Fori(0, 2) as i:
                for u in range(SLOTS):
                    d.pe_pair(pe, i, u, i * SLOTS, before, 0)
                    for n in beside[u]:
                        pe.wait_ge(side_loaded[n % SIDE], i * 48 + 16 * (n // SIDE + 2))
                        tile_panel(side_slots[n % SIDE], n % 4, i * 3 + (3 + n // 4))
                    if u in turns_tile:
                        turn(turns_tile[u], i * 3 + (3 + turns_tile[u]))
            loads = [b + 2 for b in before]
            d.pe_add(pe, hid, KF, 0, loads, 0, 1, ready=lambda k: k + 1)
            loads = [n + 1 for n in loads]
            with pe.Fori(0, 2) as i:
                for u in range(6):
                    d.pe_pair(pe, i, u, i * 6 + KF, loads, 1)

        @block.scalar
        def _(sc):
            sc.sem_inc(rows_out, 1)

            def tile_rows(t, n):
                sc.wait_ge(side_done, n * 4 + 4)
                sc.wait_ge(added, n + 1)
                sc.activation(rows[:, t], ps[5][:, 0:2 * P], ACT.Copy).then_inc(rows_out, 1)

            for k in range(KD):
                d.act_square(sc, 0, k)
            for t in range(3):
                tile_rows(t, t)
            d.act_norm(sc, 0, mod[:, 0:8])
            with sc.Fori(0, 2) as i:
                for u in range(SLOTS):
                    d.act_gate(sc, u, i * SLOTS)
                    if u in ends:
                        tile_rows(ends[u], i * 3 + (3 + ends[u]))
            d.act_squares(sc, 0, 1)
            d.act_norm(sc, 1, mod[:, 24:32])
            pairs = proj.rearrange("p (q a) t -> p q (a t)", a=2)
            with sc.Fori(0, 2) as i:
                for u in range(6):
                    sc.wait_ge(d.panel_done, i * 6 + (KF + u + 1))
                    sc.activation(pairs[:, i * 6 + u], ps[u % 3], ACT.Copy).then_inc(d.bank_free, 1)

        @block.vector
        def _(ve):
            ve.sem_inc(d.bank_free, 2)
            ve.sem_inc(added, 1)

            def tile_add(n):
                ve.wait_ge(turned, n + 1)
                sums = ps[7][:, 0:2 * P].rearrange("p (n g v) -> p g n v", n=2, g=4)
                ve.tensor_tensor(mods[:, n], sums[:, :, :, 2], bias[:, n], ADD).then_inc(added, 1)

            ve.wait_ge(vec_here, 16)
            for t in range(3):
                tile_add(t)
            ve.wait_ge(added, 4)
            ve.tensor_scalar(gain[:, 0], mod[:, 8:16], 1.0, None, ADD)
            ve.tensor_scalar(gain[:, 3], mod[:, 16:24], 0.5, None, MUL).then_inc(gained, 1)
            ve.wait_ge(gained, 1)
            d.dve_norm(ve, 0, gain[:, 0])
            with ve.Fori(0, 2) as i:
                for u in range(SLOTS):
                    d.dve_gate(ve, u, i * SLOTS, hid)
                    if u in turns_tile:
                        tile_add(i * 3 + (3 + turns_tile[u]))
            ve.wait_ge(added, 10)
            for j in (1, 2):
                ve.tensor_scalar(gain[:, j], mod[:, 24 * j + 8:24 * j + 16], 1.0, None, ADD)
            ve.tensor_scalar(gain[:, 4], mod[:, 64:72], 0.5, None, MUL).then_inc(gained, 1)
            ve.wait_ge(gained, 2)
            d.dve_add(ve, 0, gain[:, 3])
            d.dve_norm(ve, 1, gain[:, 1])


def layer_out(nc, st, c, ring, ps, xT, hT, vec, mod, gain, mix, hid, w_out, w_ff):
    d = Dense(nc, st, c, ring, ps, xT, hT, 4)
    before = [1] * 4 + [0] * 7
    with st.block() as block:
        @block.sync
        def _(sp):
            for j in range(4):
                sp.dma_start(d.slots[j], w_out[j]).then_inc(d.loaded[j], 16)
            for u in range(SLOTS):
                if u >= 7:
                    sp.wait_ge(d.chunk_done, chunks_of(u - 7, KD))
                sp.dma_start(d.slots[d.slot(u)], w_ff[u]).then_inc(d.loaded[d.slot(u)], 16)
            with sp.Fori(1, 3) as i:
                for u in range(SLOTS):
                    sp.wait_ge(d.panel_done, i * SLOTS + (u + 1 - SLOTS))
                    sp.dma_start(d.slots[d.slot(u)], w_ff[i * SLOTS + u]).then_inc(d.loaded[d.slot(u)], 16)

        @block.tensor
        def _(pe):
            d.pe_add(pe, mix, KD, 0, [0] * SLOTS, 7, 0)
            with pe.Fori(0, 2) as i:
                for u in range(SLOTS):
                    d.pe_pair(pe, i, u, i * SLOTS, before, 0)
            d.pe_add(pe, hid, KF, KD, [b + 2 for b in before], 0, ready=lambda k: k + 1)

        @block.scalar
        def _(sc):
            d.act_squares(sc, 0, 0)
            d.act_norm(sc, 0, mod[:, 48:56])
            with sc.Fori(0, 2) as i:
                for u in range(SLOTS):
                    d.act_gate(sc, u, i * SLOTS)

        @block.vector
        def _(ve):
            ve.sem_inc(d.bank_free, 2)
            d.dve_add(ve, 0, mod[:, 40:48])
            d.dve_norm(ve, 0, gain[:, 2])
            with ve.Fori(0, 2) as i:
                for u in range(SLOTS):
                    d.dve_gate(ve, u, i * SLOTS, hid)
            d.dve_add(ve, KD, gain[:, 4])


class Spectrum:

    def __init__(self, st, c, ps, cst, src, vec, spec):
        self.c, self.ps, self.cst, self.src, self.vec, self.spec = c, ps, cst, src, vec, spec
        self.small = st.sb("small", [P, SM1["router"][0]])
        self.feats = st.sb("feats", [P, T])
        self.window = st.sb("window", [P, NT, T])
        self.dft = st.sb("dft", [P, 4, 640])
        self.masked = st.sb("masked", [P, P])
        self.h1 = st.sb("h1", [HEAD, T])
        self.ang = st.sb("ang", [HEAD, T])
        self.tmp = st.sb("tmp", [HEAD, T])
        self.filt = st.sb("filt", [P, NT, 2, 512])
        self.size = st.sb("size", [P, NT, 2, 512])
        self.norm = st.sb("norm", [P, 512])
        self.consts, self.layer, self.angled, self.sined = (
            st.sem(n) for n in ("consts", "layer", "angled", "sined"))
        self.filtered, self.windowed, self.sized, self.summed = (
            st.sem(n) for n in ("filtered", "windowed", "sized", "summed"))
        self.normed, self.transformed, self.chain = (st.sem(n) for n in ("normed", "transformed", "spec_chain"))

    def weights(self, name):
        return self.small[:, SM1[name][0]:SM1[name][1]]

    def sync(self, sp):
        sp.dma_start(self.small, self.src).then_inc(self.consts, 16)
        for dst, name in ((self.feats, "hy_feats"), (self.window, "hy_window"), (self.dft, "dft_filter"),
                          (self.masked, "ones_but_first")):
            sp.dma_start(dst, self.cst[name]).then_inc(self.consts, 16)

    def pe_layer(self, pe, n):
        if n == 0:
            pe.wait_ge(self.consts, 80)
            w, x = self.weights("f_w1")[0:33, :], self.feats[0:33, :]
        else:
            pe.wait_ge(self.sined, 1)
            w, x = self.weights("f_w2")[0:HEAD, :], self.h1
        pe.matmul(self.ps[n][0:HEAD, 0:T], w, x, start=True, stop=True).then_inc(self.layer, 1)

    def pe_filter(self, pe):
        pe.wait_ge(self.sined, 2)
        for t in range(NT):
            for j in range(2):
                pe.matmul(self.ps[2 + 2 * t + j], self.h1[:, t * P:(t + 1) * P],
                          self.weights("f_w3")[0:HEAD, j * 512:(j + 1) * 512], start=True, stop=True)\
                    .then_inc(self.filtered, 1)

    def pe_sizes(self, pe):
        pe.wait_ge(self.sized, 1)
        for j in range(4):
            mm = pe.matmul(self.ps[0], self.masked if j == 2 else self.c["ones"], self.size[:, j % 2, j // 2],
                           start=j == 0, stop=j == 3)
        mm.then_inc(self.summed, 1)

    def pe_transform(self, pe):
        for f in range(5):
            for j in range(4):
                mm = pe.matmul(self.ps[1 + f], self.dft[:, j, f * P:(f + 1) * P], self.filt[:, j % 2, j // 2],
                               start=j == 0, stop=j == 3)
            mm.then_inc(self.transformed, 1)

    def act_sine(self, sc, n):
        sc.wait_ge(self.angled, n + 1)
        sc.activation(self.h1, self.ang, ACT.Sin).then_inc(self.sined, 1)

    def act_size(self, sc):
        sc.wait_ge(self.windowed, 4)
        sc.activation(self.size, self.filt, ACT.Abs).then_inc(self.sized, 1)

    def dve_layer(self, ve, n):
        v = lambda k: self.vec[0:HEAD, V1[k][0]:V1[k][0] + 1]
        link = Chain(ve, self.chain)
        link.n = 8 * n
        ve.wait_ge(self.layer, n + 1)
        if n:
            ve.wait_ge(self.sined, n)
        link(ve.tensor_scalar(self.ang, self.ps[n][0:HEAD, 0:T], v(("f_b1", "f_b2")[n]), v("f_freq"), ADD, MUL))
        sine(ve, link, self.ang, self.ang, self.tmp, False)
        ve.sem_inc(self.angled, 1)

    def dve_window(self, ve):
        for t in range(NT):
            for j in range(2):
                ve.wait_ge(self.filtered, 2 * t + j + 1)
                ve.tensor_tensor(self.filt[:, t, j].rearrange("p (o c) -> p o c", o=2),
                                 self.ps[2 + 2 * t + j].rearrange("p (o c) -> p o c", o=2),
                                 self.window[:, t].unsqueeze(1).broadcast_to([P, 2, T]), MUL)\
                    .then_inc(self.windowed, 1)

    def dve_invert(self, ve):
        ve.wait_ge(self.summed, 1)
        ve.reciprocal(self.norm, self.ps[0]).then_inc(self.normed, 1)

    def dve_divide(self, ve):
        ve.wait_ge(self.normed, 1)
        for f in range(5):
            ve.wait_ge(self.transformed, f + 1)
            ve.tensor_tensor(self.spec[:, f], self.ps[1 + f], self.norm, MUL)


def front(nc, c, ps, ring, I, cst, vec, cond, xT, ctxT, rows, mod, gain, spec):
    v = lambda k: vec[:, V1[k][0]:V1[k][1]]
    n_slots, per_tile, width, tiles = 8, KD // 2, 3 * P, 4
    cols = 8 * width
    with Stage(nc, "front") as st:
        spectrum = Spectrum(st, c, ps, cst, I["small1"][:, 0:SM1["router"][0]], vec, spec)
        sums = st.sb("sums", [P, width])
        loaded = [st.sem(f"loaded{u}") for u in range(n_slots)]
        landed, turned_x, copied, panel_done, sums_out, turned, added = (
            st.sem(k) for k in ("landed", "turned_x", "copied", "panel_done", "sums_out", "turned", "added"))
        slot = [ring[:, u * cols:(u + 1) * cols] for u in range(n_slots)]
        jobs = [(g, t, h) for g in range(2) for t in range(NT) for h in range(2)]
        mods = mod.rearrange("p (t g n) v -> p t g n v", g=4, n=3)
        bias = v("b_mod").rearrange("p (t g n) -> p t g n", g=4, n=3)
        with st.block() as block:
            @block.sync
            def _(sp):
                spectrum.sync(sp)
                for g, src in enumerate((I["x"], I["ctx"])):
                    sp.dma_start(rows[:, g], src.rearrange("(t p) d -> p t d", p=P)).then_inc(landed, 16)
                for u in range(n_slots):
                    sp.dma_start(slot[u], I["w_mod"][u]).then_inc(loaded[u], 16)
                for u in range(n_slots):
                    sp.wait_ge(panel_done, u + 1)
                    sp.dma_start(slot[u], I["w_mod"][n_slots + u]).then_inc(loaded[u], 16)

            @block.tensor
            def _(pe):
                def tile(t):
                    if t:
                        pe.wait_ge(sums_out, t)
                    for j in range(per_tile):
                        q = t * per_tile + j
                        w = slot[q % n_slots].rearrange("p (k g n) -> p k g n", k=2, g=4)
                        pe.wait_ge(loaded[q % n_slots], q // n_slots * 16 + 16)
                        for k in range(2):
                            for g in range(4):
                                mm = pe.matmul(ps[6][32 * g:32 * g + 32, 0:width], cond[:, 2 * j + k], w[:, k, g],
                                               start=j == 0 and k == 0, stop=j == per_tile - 1 and k == 1)
                        mm.then_inc(panel_done, 1)
                    pe.wait_ge(sums_out, t + 1)
                    if t:
                        pe.wait_ge(added, t)
                    for n in range(3):
                        mm = pe.transpose(ps[7][:, n * P:(n + 1) * P], sums[:, n * P:(n + 1) * P], c["ident"])
                    mm.then_inc(turned, 1)

                spectrum.pe_layer(pe, 0)
                pe.wait_ge(landed, 32)
                for n, (g, t, h) in enumerate(jobs):
                    if n >= 4:
                        pe.wait_ge(copied, n - 3)
                    for k in range(4):
                        f = (4 * h + k) * P
                        mm = pe.transpose(ps[2 + n % 4][:, k * P:(k + 1) * P], rows[:, g, t, f:f + P], c["ident"])
                    mm.then_inc(turned_x, 1)
                spectrum.pe_layer(pe, 1)
                tile(0)
                spectrum.pe_filter(pe)
                tile(1)
                spectrum.pe_sizes(pe)
                tile(2)
                spectrum.pe_transform(pe)
                tile(3)

            @block.scalar
            def _(sc):
                def tile(t):
                    sc.wait_ge(panel_done, (t + 1) * per_tile)
                    if t:
                        sc.wait_ge(turned, t)
                    sc.activation(sums, ps[6][:, 0:width], ACT.Copy).then_inc(sums_out, 1)

                spectrum.act_sine(sc, 0)
                spectrum.act_sine(sc, 1)
                tile(0)
                spectrum.act_size(sc)
                for t in range(1, tiles):
                    tile(t)

            @block.vector
            def _(ve):
                def tile(t):
                    ve.wait_ge(turned, t + 1)
                    part = ps[7][:, 0:width].rearrange("p (n g v) -> p g n v", n=3, g=4)
                    ve.tensor_tensor(mods[:, t, :, :, 0], part[:, :, :, 0], bias[:, t], ADD)
                    ve.tensor_tensor(mods[:, t, :, :, 1], part[:, :, :, 1], bias[:, t], ADD).then_inc(added, 1)

                spectrum.dve_layer(ve, 0)
                for n, (g, t, h) in enumerate(jobs):
                    ve.wait_ge(turned_x, n + 1)
                    ve.tensor_copy((xT, ctxT)[g][:, 4 * h:4 * h + 4, t * P:(t + 1) * P],
                                   ps[2 + n % 4].rearrange("p (k n) -> p k n", n=P)).then_inc(copied, 1)
                spectrum.dve_layer(ve, 1)
                tile(0)
                spectrum.dve_window(ve)
                tile(1)
                spectrum.dve_invert(ve)
                tile(2)
                spectrum.dve_divide(ve)
                tile(3)
                ve.wait_ge(added, tiles)
                for j in range(2):
                    ve.scalar_tensor_tensor(gain[:, j], mod[:, 8:16, j], 1.0, v("norm1"), ADD, MUL)
                ve.scalar_tensor_tensor(gain[:, 2], mod[:, 32:40, 0], 1.0, v("norm2"), ADD, MUL)


def first_block(nc, c, ps, ring, I, cst, vec, cond, xT, hT, tables):
    v = lambda k: vec[:, V1[k][0]:V1[k][1]]
    h = hT[:, :, 0:T]
    with Stage(nc, "first") as st:
        mod = st.sb("mod", [P, 48, 2])
        gain = st.sb("gain", [P, 3, KD])
        router = st.sb("router", [P, KD * E])
        with Stage(nc, "mixer") as mx:
            spec = mx.sb("spec", [P, 5, 512])
            ctxT = mx.sb("ctxT", [P, KD, T])
            front(nc, c, ps, ring, I, cst, vec, cond, xT, ctxT, hT.rearrange("p k n -> p (k n)")
                  .rearrange("p (g t d) -> p g t d", g=2, t=NT), mod, gain, spec)
            proj = mx.sb("proj", [P, 36, T])
            kv = mx.sb("kv", [P, 2, 2 * T])
            project_in(nc, c, ps, ring, I, xT, ctxT, hT, mod, gain, proj, kv)
            first_branches(nc, c, ps, ring, cst, vec, spec, proj, kv, ctxT)
            project_out(nc, c, ps, ring, I, xT, h, mod, gain, proj, ctxT, router)
        with Stage(nc, "moe") as s2:
            place = s2.sb("place", [P, E, T])
            x_sel = s2.sb("x_sel", [P, KD, 512])
            slot = [ring[:, u * 4 * D:(u + 1) * 4 * D] for u in range(RING_COLS // (4 * D))]
            loaded = [s2.sem(f"loaded{u}") for u in range(len(slot))]
            route(nc, c, ps, cst, router, hT, place, x_sel, slot, loaded, I["w_expert"])
            experts(nc, c, ps, slot, loaded, I["w_expert"], x_sel, place, xT, mod[:, 40:48, 0], cst, I["positions"],
                    tables)
        norm_modulate(nc, c, ps, [(xT, xT, v("final_g"), None)])


def head_sums(pe, c, bank, x):
    return pe.matmul(bank[:, 0:512], c["ones_head"], x.rearrange("p a b -> p (a b)"), start=True, stop=True)


def head_norm(nc, c, ps, ar, x, eps, gain, bias, out):
    with Stage(nc, "head_norm") as st:
        sq = ar.take(2, T)
        root = ar.take(2, T)
        flat = lambda a: a.rearrange("p a b -> p (a b)")
        meaned, centred, squared, summed, rooted, chain = (
            st.sem(n) for n in ("meaned", "centred", "squared", "summed", "rooted", "chain"))
        with st.block() as block:
            @block.tensor
            def _(pe):
                head_sums(pe, c, ps[0], x).then_inc(meaned, 1)
                pe.wait_ge(squared, 1)
                head_sums(pe, c, ps[1], sq).then_inc(summed, 1)

            @block.scalar
            def _(sc):
                sc.wait_ge(centred, 1)
                sc.activation(sq, x, ACT.Square).then_inc(squared, 1)
                sc.wait_ge(summed, 1)
                sc.activation(flat(root), ps[1], ACT.Sqrt, bias=eps, scale=1.0 / HEAD).then_inc(rooted, 1)

            @block.vector
            def _(ve):
                link = Chain(ve, chain)
                ve.wait_ge(meaned, 1)
                ve.scalar_tensor_tensor(flat(x), ps[0], -1.0 / HEAD, flat(x), MUL, ADD).then_inc(centred, 1)
                ve.wait_ge(rooted, 1)
                link(ve.reciprocal(flat(root), flat(root)))
                link(ve.tensor_tensor(x, x, root, MUL))
                for j in range(2):
                    if bias is None:
                        ve.tensor_scalar(out[:, j], x[:, j], gain[:, j:j + 1], None, MUL)
                    else:
                        ve.tensor_scalar(out[:, j], x[:, j], gain[:, j:j + 1], bias[:, j:j + 1], MUL, ADD)


def retention(nc, c, ps, ring, cst, proj, tables, vec, out):
    v = lambda k: vec[:, V2[k][0]:V2[k][1]]
    ar = Arena(ring, MIX_COLS)
    rel = ar.take(2, NT, T)
    lg = ar.take(8)
    decay = ar.take(4, NT, T)
    score = ar.take(4, NT, T)
    v_tok = ar.take(NT, T)
    y = ar.take(2, T)
    perm = ar.take(P)
    load_all(nc, [(rel[:, 0], cst["ahead"]), (rel[:, 1], cst["behind"]), (perm, cst["swap_half"])])
    rotate(nc, c, ps, proj[:, 14:18], 4, P, perm, tables[:, 0, 0], tables[:, 0, 1])
    turn_tokens(nc, c, ps, lambda j: proj[:, 18 + j % 2, (j // 2) * P:(j // 2 + 1) * P], 4,
                lambda g: v_tok.rearrange("p t (k n) -> p (t k) n", n=P))
    with Stage(nc, "retention") as st:
        rated, signed, spread, decayed, scored, weighted, mixed = (
            st.sem(n) for n in ("rated", "signed", "spread", "decayed", "scored", "weighted", "mixed"))
        with st.block() as block:
            @block.scalar
            def _(sc):
                sc.activation(lg, v("log_rate"), ACT.Exp).then_inc(rated, 1)
                for h in range(4):
                    sc.wait_ge(spread, 2 * h + 2)
                    sc.activation(decay[:, h], decay[:, h], ACT.Exp).then_inc(decayed, 1)

            @block.tensor
            def _(pe):
                for h in range(4):
                    b = slice(h % 2 * HEAD, h % 2 * HEAD + HEAD)
                    for t in range(NT):
                        mm = pe.matmul(ps[h][:, t * T:(t + 1) * T], proj[b, 16 + h // 2, t * P:(t + 1) * P],
                                       proj[b, 14 + h // 2], start=True, stop=True)
                    mm.then_inc(scored, 1)
                for h in range(4):
                    b = slice(h % 2 * HEAD, h % 2 * HEAD + HEAD)
                    pe.wait_ge(weighted, h + 1)
                    for t in range(NT):
                        mm = pe.matmul(ps[4 + h // 2][b, 0:T], v_tok[:, t, h * HEAD:(h + 1) * HEAD], score[:, h, t],
                                       start=t == 0, stop=t == NT - 1)
                    mm.then_inc(mixed, 1)

            @block.vector
            def _(ve):
                ve.wait_ge(rated, 1)
                ve.tensor_scalar(lg, lg, -1.0, None, MUL).then_inc(signed, 1)
                ve.wait_ge(signed, 1)
                for h in range(4):
                    ve.tensor_scalar(decay[:, h], rel[:, 0], lg[:, h:h + 1], None, MUL).then_inc(spread, 1)
                    ve.wait_ge(spread, 2 * h + 1)
                    ve.scalar_tensor_tensor(decay[:, h], rel[:, 1], lg[:, 4 + h:5 + h], decay[:, h], MUL, ADD)\
                        .then_inc(spread, 1)
                for h in range(4):
                    ve.wait_ge(decayed, h + 1)
                    ve.wait_ge(scored, h + 1)
                    ve.scalar_tensor_tensor(score[:, h], ps[h].rearrange("p (a b) -> p a b", b=T), HEAD ** -0.5,
                                            decay[:, h], MUL, MUL).then_inc(weighted, 1)
                for j in range(2):
                    ve.wait_ge(mixed, 2 * j + 2)
                    ve.tensor_copy(y[:, j], ps[4 + j][:, 0:T])
    head_norm(nc, c, ps, ar, y, c["eps"][:, 1:2], v("gn_g"), None, y)
    with Stage(nc, "ret_gate") as st:
        opened = st.sem("opened")
        with st.block() as block:
            @block.scalar
            def _(sc):
                sc.activation(proj[:, 20:22], proj[:, 20:22], ACT.Silu).then_inc(opened, 1)

            @block.vector
            def _(ve):
                ve.wait_ge(opened, 1)
                ve.tensor_tensor(out, y, proj[:, 20:22], MUL)


def latent_attention(nc, c, ps, ring, cst, proj, tables, vec, small, out):
    v = lambda k: vec[:, V2[k][0]:V2[k][1]]
    w_uq = small[:, SM2["w_uq"][0]:SM2["w_uq"][1]].rearrange("p (k n) -> p k n", k=3)
    w_ukv = small[:, SM2["w_ukv"][0]:SM2["w_ukv"][1]].rearrange("p (k n) -> p k n", k=2)
    ar = Arena(ring, MIX_COLS)
    sq = ar.take(5, T)
    root = ar.take(2, T)
    q = ar.take(8, T, rows=96)
    k = ar.take(8, T, rows=96)
    v_tok = ar.take(NT, 512)
    perm = ar.take(P)
    perm_k = ar.take(P)
    load_all(nc, [(perm, cst["swap_mla"]), (perm_k, cst["swap_kpe"])])
    rotate(nc, c, ps, proj[0:32, 22:23], 1, 32, perm_k[0:32, 0:32], tables[0:32, 2, 0], tables[0:32, 2, 1])
    with Stage(nc, "latent_norm") as st:
        squared, summed, rooted, inverted, scaled, projected, copied = (
            st.sem(n) for n in ("squared", "summed", "rooted", "inverted", "scaled", "projected", "copied"))
        groups = ((9, 3, "mla_q_g"), (12, 2, "mla_kv_g"))
        with st.block() as block:
            @block.scalar
            def _(sc):
                sc.activation(sq, proj[:, 9:14], ACT.Square).then_inc(squared, 1)
                for g, (_, n, _) in enumerate(groups):
                    sc.wait_ge(summed, g + 1)
                    sc.activation(root[:, g], ps[g][:, 0:T], ACT.Sqrt, bias=c["eps"][:, 0:1], scale=1.0 / (n * P))\
                        .then_inc(rooted, 1)

            @block.tensor
            def _(pe):
                pe.wait_ge(squared, 1)
                for g, (at, n, _) in enumerate(groups):
                    for j in range(n):
                        mm = pe.matmul(ps[g][:, 0:T], c["ones"], sq[:, at - 9 + j], start=j == 0, stop=j == n - 1)
                    mm.then_inc(summed, 1)

            @block.vector
            def _(ve):
                for g, (at, n, gain) in enumerate(groups):
                    ve.wait_ge(rooted, g + 1)
                    ve.reciprocal(root[:, g], root[:, g]).then_inc(inverted, 1)
                    ve.wait_ge(inverted, g + 1)
                    for j in range(n):
                        ve.scalar_tensor_tensor(proj[:, at + j], proj[:, at + j], v(gain)[:, j:j + 1], root[:, g],
                                                MUL, MUL).then_inc(scaled, 1)
        with st.block() as block:
            @block.tensor
            def _(pe):
                for h in range(8):
                    if h >= 4:
                        pe.wait_ge(copied, 2 * (h - 4) + 1)
                    for j in range(3):
                        mm = pe.matmul(ps[h % 4][0:96, 0:T], w_uq[:, j, h * 96:(h + 1) * 96], proj[:, 9 + j],
                                       start=j == 0, stop=j == 2)
                    mm.then_inc(projected, 1)
                    if h >= 4:
                        pe.wait_ge(copied, 2 * (h - 4) + 2)
                    for j in range(2):
                        mm = pe.matmul(ps[4 + h % 4][0:HEAD, 0:T], w_ukv[:, j, h * P:h * P + HEAD], proj[:, 12 + j],
                                       start=j == 0, stop=j == 1)
                    mm = pe.matmul(ps[4 + h % 4][HEAD:96, 0:T], c["ident"][0:32, 0:32], proj[0:32, 22],
                                   start=True, stop=True)
                    mm.then_inc(projected, 1)
                for t in range(NT):
                    pe.wait_ge(copied, 16)
                    for j in range(2):
                        mm = pe.matmul(ps[t][:, :], proj[:, 12 + j, t * P:(t + 1) * P],
                                       w_ukv[:, j].rearrange("p (h n) -> p h n", n=P)[:, :, HEAD:P],
                                       start=j == 0, stop=j == 1)
                    mm.then_inc(projected, 1)

            @block.scalar
            def _(sc):
                for h in range(8):
                    sc.wait_ge(projected, 2 * h + 1)
                    sc.activation(q[:, h], ps[h % 4][0:96, 0:T], ACT.Copy, scale=96 ** -0.5).then_inc(copied, 1)
                    sc.wait_ge(projected, 2 * h + 2)
                    sc.activation(k[:, h], ps[4 + h % 4][0:96, 0:T], ACT.Copy).then_inc(copied, 1)
                for t in range(NT):
                    sc.wait_ge(projected, 17 + t)
                    sc.activation(v_tok[:, t], ps[t], ACT.Copy)
    rotate(nc, c, ps, q, 8, 96, perm[0:96, 0:96], tables[0:96, 1, 0], tables[0:96, 1, 1])
    attention(nc, c, ps, ar, lambda h, t: q[:, h, t * P:(t + 1) * P], lambda h: k[:, h],
              lambda h, j: v_tok[:, j, h * HEAD:(h + 1) * HEAD],
              lambda h: (h % 2 * HEAD, out[h % 2 * HEAD:h % 2 * HEAD + HEAD, h // 2]), 8, T)


def rwkv(nc, c, ps, ring, cst, z, vec, small, out):
    v = lambda k, j=0, n=1: vec[:, V2[k][0] + j:V2[k][0] + j + n]
    rate = float(np.exp(-0.5))
    flat = lambda a: a.rearrange("p a b -> p (a b)")
    with Stage(nc, "rwkv") as rw:
        ar = Arena(ring, MIX_COLS)
        zs = ar.take(9, T)
        sw = ar.take(4, T)
        a = ar.take(4, T)
        gate = rw.sb("gate", [P, 2, T])
        kh, kt, bt, rh = (ar.take(4, T) for _ in range(4))
        v_tok = ar.take(NT, T)
        tot = rw.sb("tot", [P, 4, NT])
        ehalf = rw.sb("ehalf", [P, 4, NT])
        mark = ar.at
        with Stage(nc, "shift") as st:
            near = ar.take(9, T)
            hmu = st.sb("hmu", [P, 9])
            omu = st.sb("omu", [P, 9])
            chain, kept = st.sem("chain"), st.sem("kept")
            with st.block() as block:
                @block.vector
                def _(ve):
                    link = Chain(ve, chain)
                    link(ve.tensor_scalar(hmu, v("mu", 0, 9), 0.5, None, MUL))
                    link(ve.tensor_scalar(omu, v("mu", 0, 9), -1.0, 1.0, MUL, ADD))
                    ve.tensor_copy(near[:, :, 0:1], z[:, :, 1:2])
                    ve.tensor_copy(near[:, :, T - 1:T], z[:, :, T - 2:T - 1])
                    link(ve.tensor_tensor(near[:, :, 1:T - 1], z[:, :, 0:T - 2], z[:, :, 2:T], ADD))
                    for j in range(9):
                        ve.tensor_scalar(zs[:, j], z[:, j], omu[:, j:j + 1], None, MUL).then_inc(kept, 1)
                    for j in range(9):
                        ve.wait_ge(kept, j + 1)
                        ve.scalar_tensor_tensor(zs[:, j], near[:, j], hmu[:, j:j + 1], zs[:, j], MUL, ADD)
        r, k, vv = zs[:, 0:2], zs[:, 2:4], zs[:, 4:6]
        ar.at = mark
        with Stage(nc, "gates") as st:
            kk, sq = ar.take(2, T), ar.take(2, T)
            root = ar.take(2, T)
            cs, cx = ar.take(4, T), ar.take(4, T)
            e1, e2, e3 = ar.take(4, T), ar.take(4, T), ar.take(2, T)
            kmod = ar.take(4, T)
            hb = st.sb("hb", [P, 4, NT, 2])
            oka = st.sb("oka", [P, 2])
            up, lifted, opened, keyed, squared, summed, rooted, chain, decays, halves, exped, turned = (
                st.sem(n) for n in ("up", "lifted", "opened", "keyed", "squared", "summed", "rooted", "chain",
                                    "decays", "halves", "exped", "turned"))
            w = lambda n: small[:, SM2[n][0]:SM2[n][1]]
            with st.block() as block:
                @block.scalar
                def _(sc):
                    sc.activation(zs[:, 7], zs[:, 7], ACT.Tanh)
                    sc.activation(zs[:, 6], zs[:, 6], ACT.Sigmoid).then_inc(up, 1)
                    sc.wait_ge(lifted, 1)
                    for d in range(2):
                        for j in range(2):
                            sc.activation(sw[:, 2 * d + j], ps[d][:, j * T:(j + 1) * T], ACT.Sigmoid,
                                          bias=v("w0", 2 * d + j))
                            m = sc.activation(a[:, 2 * d + j], ps[2 + d][:, j * T:(j + 1) * T], ACT.Sigmoid,
                                              bias=v("a0", 2 * d + j))
                    sc.activation(flat(gate), ps[4], ACT.Copy).then_inc(opened, 1)
                    sc.wait_ge(keyed, 1)
                    sc.activation(sq, kk, ACT.Square).then_inc(squared, 1)
                    sc.wait_ge(summed, 1)
                    sc.activation(flat(root), ps[5], ACT.Sqrt).then_inc(rooted, 1)
                    sc.wait_ge(halves, 1)
                    for u in range(4):
                        for n in range(NT):
                            col = slice(n * P, (n + 1) * P)
                            plus, minus = hb[:, u, n, 0:1], hb[:, u, n, 1:2]
                            sc.activation(e1[:, u, col], cx[:, u, col], ACT.Exp, bias=plus, scale=-rate)
                            sc.activation(e2[:, u, col], cs[:, u, col], ACT.Exp, bias=minus, scale=rate)
                            if u < 2:
                                sc.activation(e3[:, u, col], cs[:, u, col], ACT.Exp, bias=plus, scale=-rate)
                    sc.activation(ehalf, hb[:, :, :, 1], ACT.Exp).then_inc(exped, 1)

                @block.tensor
                def _(pe):
                    pe.wait_ge(up, 1)
                    for d in range(2):
                        rows = slice(d * HEAD, (d + 1) * HEAD)
                        for j in range(2):
                            pe.matmul(ps[d][:, j * T:(j + 1) * T], w("w_up")[rows, j * P:(j + 1) * P], zs[rows, 7],
                                      start=True, stop=True)
                            pe.matmul(ps[2 + d][:, j * T:(j + 1) * T], w("a_up")[rows, j * P:(j + 1) * P],
                                      zs[rows, 8], start=True, stop=True)
                    for j in range(2):
                        mm = pe.matmul(ps[4][:, j * T:(j + 1) * T], w("g_up")[:, j * P:(j + 1) * P], zs[:, 6],
                                       start=True, stop=True)
                    mm.then_inc(lifted, 1)
                    for n in range(NT):
                        for j in range(2):
                            mm = pe.transpose(ps[6][:, (2 * n + j) * P:(2 * n + j + 1) * P],
                                              vv[:, j, n * P:(n + 1) * P], c["ident"])
                    mm.then_inc(turned, 1)
                    pe.wait_ge(squared, 1)
                    head_sums(pe, c, ps[5], sq).then_inc(summed, 1)

                @block.vector
                def _(ve):
                    link = Chain(ve, chain)
                    for j in range(2):
                        link(ve.tensor_scalar(kk[:, j], k[:, j], v("k_k", j), None, MUL))
                    ve.sem_inc(keyed, 1)
                    link(ve.tensor_scalar(oka, v("k_a", 0, 2), -1.0, 1.0, MUL, ADD))
                    ve.wait_ge(turned, 1)
                    ve.tensor_copy(v_tok, ps[6].rearrange("p (a b) -> p a b", b=T))
                    ve.wait_ge(opened, 1)
                    for u in range(4):
                        for n in range(NT):
                            col = slice(n * P, (n + 1) * P)
                            m = ve.tensor_tensor_scan(cs[:, u, col], sw[:, u, col], c["zeros"][:, 0:P], 0.0,
                                                      ADD, ADD)
                            link(m)
                            link(ve.tensor_copy(tot[:, u, n:n + 1], cs[:, u, (n + 1) * P - 1:(n + 1) * P]))
                    link(ve.tensor_tensor(cx, cs, sw, SUB))
                    link(ve.tensor_scalar(hb[:, :, :, 0], tot, rate / 2, None, MUL))
                    link(ve.tensor_scalar(hb[:, :, :, 1], tot, -rate / 2, None, MUL))
                    ve.sem_inc(halves, 1)
                    ve.wait_ge(rooted, 1)
                    link(ve.tensor_scalar(root, root, 1e-12, None, MAX))
                    link(ve.reciprocal(flat(root), flat(root)))
                    link(ve.tensor_tensor(kk, kk, root, MUL))
                    for d in range(2):
                        for j in range(2):
                            u = 2 * d + j
                            link(ve.tensor_scalar(kmod[:, u], a[:, u], v("k_a", j), oka[:, j:j + 1], MUL, ADD))
                        link(ve.tensor_tensor(kmod[:, 2 * d:2 * d + 2], kmod[:, 2 * d:2 * d + 2], k, MUL))
                        link(ve.tensor_tensor(a[:, 2 * d:2 * d + 2], a[:, 2 * d:2 * d + 2], kk, MUL))
                    ve.wait_ge(exped, 1)
                    for d in range(2):
                        u = slice(2 * d, 2 * d + 2)
                        key, tilde, read = ((e1[:, u], e2[:, u], e3), (e2[:, u], e1[:, u], e2[:, u]))[d]
                        ve.tensor_tensor(kh[:, u], key, kk, MUL)
                        ve.tensor_tensor(kt[:, u], tilde, kmod[:, u], MUL)
                        ve.tensor_tensor(bt[:, u], tilde, a[:, u], MUL)
                        ve.tensor_tensor(rh[:, u], read, r, MUL)
        ar.at = mark
        tok = ar.take(2, 2, 2 * P)
        abT, akT, bkT, bbT = (ar.take(4, 4, P) for _ in range(4))
        turn_tokens(nc, c, ps, lambda j: (kt, bt)[j // 4][:, j % 4, (j % 4 // 2) * P:(j % 4 // 2 + 1) * P], 8,
                    lambda g: tok[:, g].rearrange("p d (k n) -> p (d k) n", n=P))
        with Stage(nc, "products") as st:
            tri = st.sb("tri", [P, 4, P])
            landed, made, masked = st.sem("landed"), st.sem("made"), st.sem("masked")
            kinds = ((bt, kh, abT), (kt, kh, akT), (kt, rh, bkT), (bt, rh, bbT))
            with st.block() as block:
                @block.sync
                def _(sp):
                    sp.dma_start(tri, cst["tri"]).then_inc(landed, 16)

                @block.tensor
                def _(pe):
                    for g in range(4):
                        d, n = g // 2, g % 2
                        col = slice(n * P, (n + 1) * P)
                        for i, (src, dst, _) in enumerate(kinds):
                            for half in range(2):
                                rows = slice(half * HEAD, (half + 1) * HEAD)
                                if g:
                                    pe.wait_ge(masked, 8 * (g - 1) + 2 * i + half + 1)
                                for pair in range(2):
                                    mm = pe.matmul(ps[2 * i + half][:, pair * P:(pair + 1) * P],
                                                   src[rows, 2 * d + pair, col], dst[rows, 2 * d + pair, col],
                                                   start=True, stop=True)
                                mm.then_inc(made, 1)

                @block.vector
                def _(ve):
                    ve.wait_ge(landed, 16)
                    for g in range(4):
                        for i, (_, _, res) in enumerate(kinds):
                            mask = tri[:, g // 2 + (2 if i >= 2 else 0)].unsqueeze(1).broadcast_to([P, 2, P])
                            for half in range(2):
                                ve.wait_ge(made, 8 * g + 2 * i + half + 1)
                                ve.tensor_tensor(res[:, g, 2 * half:2 * half + 2],
                                                 ps[2 * i + half][:, 0:2 * P].rearrange("p (a b) -> p a b", b=P),
                                                 mask, MUL).then_inc(masked, 1)
        x = rw.sb("x", [P, 4, 4, P])
        xt = ar.take(4, 4, P)
        with Stage(nc, "inverse") as st:
            levels = st.sb("levels", [P, 2, 8, P])
            off = ring[:, 9 * T:17 * T].rearrange("p (a b c) -> p a b c", a=4, b=4)
            t1 = ar.take(4, 4, P)
            landed, begun, offs, t1_made, t1_copied, made, updated = (
                st.sem(n) for n in ("landed", "begun", "offs", "t1_made", "t1_copied", "made", "updated"))
            mask = lambda g, k: levels[:, g // 2, k].unsqueeze(1).broadcast_to([P, 4, P])
            with st.block() as block:
                @block.sync
                def _(sp):
                    sp.dma_start(levels[:, 0], cst["level_fwd"]).then_inc(landed, 16)
                    sp.dma_start(levels[:, 1], cst["level_bwd"]).then_inc(landed, 16)

                @block.vector
                def _(ve):
                    ve.wait_ge(landed, 32)
                    for g in range(4):
                        ve.tensor_tensor(xt[:, g], abT[:, g], mask(g, 0), MUL).then_inc(begun, 1)
                    for g in range(4):
                        ve.wait_ge(begun, g + 1)
                        ve.tensor_tensor(xt[:, g], c["ident"].unsqueeze(1).broadcast_to([P, 4, P]), xt[:, g], SUB)
            turn_tokens(nc, c, ps, lambda j: xt[:, j // 4, j % 4], 16, lambda g: x[:, g])
            bank = lambda b, j: ps[b][:, j * P:(j + 1) * P]
            quad = lambda b: ps[b].rearrange("p (a b) -> p a b", b=P)
            with st.block() as block:
                @block.tensor
                def _(pe):
                    def first(i, g):
                        pe.wait_ge(offs, i * 4 + (g - 3))
                        pe.wait_ge(t1_copied, i * 4 + (g - 3))
                        for j in range(4):
                            mm = pe.matmul(bank(g % 2, j), off[:, g, j], x[:, g, j], start=True, stop=True)
                        mm.then_inc(t1_made, 1)

                    def second(i, g):
                        pe.wait_ge(t1_copied, i * 4 + (g - 1))
                        pe.wait_ge(updated, i * 4 + (g - 1))
                        for j in range(4):
                            pe.matmul(bank(2 + g % 2, j), xt[:, g, j], t1[:, g, j], start=True, stop=True)
                        for j in range(4):
                            mm = pe.matmul(bank(4 + g % 2, j), t1[:, g, j], xt[:, g, j], start=True, stop=True)
                        mm.then_inc(made, 1)

                    with pe.Fori(1, 7) as i:
                        first(i, 0)
                        for g in range(1, 4):
                            first(i, g)
                            second(i, g - 1)
                        second(i, 3)

                @block.scalar
                def _(sc):
                    sc.sem_inc(t1_copied, 2)
                    with sc.Fori(1, 7) as i:
                        for g in range(4):
                            sc.wait_ge(t1_made, i * 4 + (g - 3))
                            sc.activation(t1[:, g], quad(g % 2), ACT.Copy).then_inc(t1_copied, 1)

                @block.vector
                def _(ve):
                    for g in range(4):
                        ve.tensor_tensor(off[:, g], abT[:, g], mask(g, 1), MUL).then_inc(offs, 1)
                    ve.sem_inc(updated, 4)
                    with ve.Fori(1, 7) as i:
                        for g in range(4):
                            ve.wait_ge(made, i * 4 + (g - 3))
                            ve.tensor_tensor(x[:, g], x[:, g], quad(2 + g % 2), SUB)
                            ve.tensor_tensor(xt[:, g], xt[:, g], quad(4 + g % 2), SUB).then_inc(updated, 1)
                            ve.tensor_tensor(off[:, g], abT[:, g], mask(g, i + 1), MUL).then_inc(offs, 1)
        y = rw.sb("y", [P, 2, T])
        with Stage(nc, "chunks") as st:
            rhs = ar.take(4, 4, HEAD)
            neg_p = ar.take(4, 4, HEAD)
            state = st.sb("state", [P, 2, 2, HEAD])
            told, copied, solved, negated, carried, scaled, read = (
                st.sem(n) for n in ("told", "copied", "solved", "negated", "carried", "scaled", "read"))
            head = lambda half, pair: slice((2 * pair + half) * HEAD, (2 * pair + half + 1) * HEAD)
            order = [(0, 0), (1, 1), (0, 1), (1, 0)]
            with st.block() as block:
                @block.tensor
                def _(pe):
                    for s, (d, n) in enumerate(order):
                        g = 2 * d + n
                        col = slice(n * P, (n + 1) * P)
                        if s >= 2:
                            pe.wait_ge(scaled, 2 * d + 2)
                        for half in range(2):
                            rows = slice(half * HEAD, (half + 1) * HEAD)
                            for pair in range(2):
                                o = ps[half][:, pair * HEAD:(pair + 1) * HEAD]
                                if s and pair == 0:
                                    pe.wait_ge(copied, 2 * (s - 1) + half + 1)
                                mm = pe.matmul(o, akT[:, g, 2 * half + pair], v_tok[:, n, head(half, pair)],
                                               start=True, stop=s < 2)
                                if s >= 2:
                                    mm = pe.matmul(o, kh[rows, 2 * d + pair, col], state[rows, d, pair],
                                                   start=False, stop=True)
                            mm.then_inc(told, 1)
                        pe.wait_ge(copied, 2 * s + 2)
                        if s:
                            pe.wait_ge(negated, s)
                        for j in range(4):
                            mm = pe.matmul(ps[2][:, j * HEAD:(j + 1) * HEAD], xt[:, g, j], rhs[:, g, j],
                                           start=True, stop=True)
                        mm.then_inc(solved, 1)
                        if s < 2:
                            pe.wait_ge(negated, s + 1)
                            for half in range(2):
                                rows = slice(half * HEAD, (half + 1) * HEAD)
                                for pair in range(2):
                                    ch = slice(pair * P + half * HEAD, pair * P + half * HEAD + HEAD)
                                    o = ps[3 + d][rows, pair * HEAD:(pair + 1) * HEAD]
                                    pe.matmul(o, tok[:, 0, d, ch], v_tok[:, n, head(half, pair)],
                                              start=True, stop=False)
                                    mm = pe.matmul(o, tok[:, 1, d, ch], neg_p[:, g, 2 * half + pair],
                                                   start=False, stop=True)
                            mm.then_inc(carried, 1)
                    pe.wait_ge(negated, 4)
                    for n in range(NT):
                        col = slice(n * P, (n + 1) * P)
                        for half in range(2):
                            rows = slice(half * HEAD, (half + 1) * HEAD)
                            for pair in range(2):
                                o = ps[5 + n][rows, pair * P:(pair + 1) * P]
                                for d in range(2):
                                    g, j = 2 * d + n, 2 * half + pair
                                    pe.matmul(o, v_tok[:, n, head(half, pair)], bkT[:, g, j],
                                              start=d == 0, stop=False)
                                    pe.matmul(o, neg_p[:, g, j], bbT[:, g, j], start=False, stop=False)
                                d = 1 - n
                                mm = pe.matmul(o, state[rows, d, pair], rh[rows, 2 * d + pair, col],
                                               start=False, stop=True)
                        mm.then_inc(read, 1)

                @block.scalar
                def _(sc):
                    for s, (d, n) in enumerate(order):
                        for half in range(2):
                            sc.wait_ge(told, 2 * s + half + 1)
                            sc.activation(rhs[:, 2 * d + n, 2 * half:2 * half + 2],
                                          ps[half][:, 0:P].rearrange("p (a b) -> p a b", b=HEAD),
                                          ACT.Copy).then_inc(copied, 1)

                @block.vector
                def _(ve):
                    for s, (d, n) in enumerate(order):
                        ve.wait_ge(solved, s + 1)
                        ve.tensor_scalar(neg_p[:, 2 * d + n], ps[2][:, 0:T].rearrange("p (a b) -> p a b", b=HEAD),
                                         -1.0, None, MUL).then_inc(negated, 1)
                        if s < 2:
                            ve.wait_ge(carried, s + 1)
                            for pair in range(2):
                                u = 2 * d + pair
                                ve.tensor_scalar(state[:, d, pair], ps[3 + d][:, pair * HEAD:(pair + 1) * HEAD],
                                                 ehalf[:, u, 0:1], ehalf[:, u, 1:2], MUL, MUL).then_inc(scaled, 1)
                    for n in range(NT):
                        ve.wait_ge(read, n + 1)
                        ve.tensor_copy(y[:, :, n * P:(n + 1) * P],
                                       ps[5 + n][:, 0:2 * P].rearrange("p (a b) -> p a b", b=P))
        ar.at = mark
        head_norm(nc, c, ps, ar, y, c["eps"][:, 2:3], v("ln_g", 0, 2), v("ln_b", 0, 2), y)
        with Stage(nc, "bonus") as st:
            prod = ar.take(2, T)
            multiplied, summed, chain = st.sem("multiplied"), st.sem("summed"), st.sem("chain")
            with st.block() as block:
                @block.tensor
                def _(pe):
                    pe.wait_ge(multiplied, 1)
                    head_sums(pe, c, ps[0], prod).then_inc(summed, 1)

                @block.vector
                def _(ve):
                    link = Chain(ve, chain)
                    for j in range(2):
                        link(ve.scalar_tensor_tensor(prod[:, j], r[:, j], v("r_k", j), k[:, j], MUL, MUL))
                    ve.sem_inc(multiplied, 1)
                    ve.wait_ge(summed, 1)
                    link(ve.tensor_tensor(prod, ps[0].rearrange("p (a b) -> p a b", b=T), vv, MUL))
                    link(ve.tensor_tensor(prod, prod, y, ADD))
                    ve.tensor_tensor(out, prod, gate, MUL)


def second_block(nc, c, ps, ring, I, cst, vec1, cond, xT, hT, tables, dbg=None):
    small = ring[:, MIX_COLS:]
    with nc.Fori(0, 2) as l, Stage(nc, "layer") as ly:
        vec = ly.sb("vec", [P, V2_COLS])
        mod = ly.sb("mod", [P, 72])
        gain = ly.sb("gain", [P, 5, KD])
        proj = ly.sb("proj", [P, 24, T])
        mix = ly.sb("mix", [P, 8, T])
        with Stage(nc, "layer_in") as st:
            layer_in(nc, st, c, ring, ps, xT, hT, cond, vec, small, mod, gain, proj, I["vec2"][l], I["small2"][l],
                     I["w_ada"][l], I["w_ff1"][l], I["w_in_2"][l])
        latent_attention(nc, c, ps, ring, cst, proj, tables, vec, small, mix[:, 2:6])
        retention(nc, c, ps, ring, cst, proj, tables, vec, mix[:, 6:8])
        rwkv(nc, c, ps, ring, cst, proj[:, 0:9], vec, small, mix[:, 0:2])
        if dbg:
            dbg(nc, l, mix=mix)
        with Stage(nc, "layer_out") as st:
            layer_out(nc, st, c, ring, ps, xT, hT, vec, mod, gain, mix, proj[:, 0:KF], I["w_out_2"][l], I["w_ff2"][l])
        if dbg:
            dbg(nc, l, xT=xT)
    norm_modulate(nc, c, ps, [(xT, xT, vec1[:, V1["final_2"][0]:V1["final_2"][1]], None)])


V1, V1_COLS = fields(VEC1)
V2, V2_COLS = fields(VEC2)
SM1, SM1_COLS = fields(SMALL1)
SM2, SM2_COLS = fields(SMALL2)
RING2_COLS = (SLOTS + SIDE) * BLK * P
MIX_COLS = RING2_COLS - SM2_COLS


def store(nc, c, ps, xT, out):
    with Stage(nc, "store") as st:
        rows = st.sb("rows", [P, NT, D])
        turn_tokens(nc, c, ps, lambda j: xT[:, j % KD, (j // KD) * P:(j // KD + 1) * P], NT * KD,
                    lambda g: rows[:, g // 2, (g % 2) * 512:(g % 2 + 1) * 512].rearrange("p (k n) -> p k n", n=P))
        stored = st.sem("stored")
        with st.block() as block:
            @block.sync
            def _(sp):
                sp.dma_start(out.rearrange("(t p) d -> p t d", p=P), rows).then_inc(stored, 16)
                sp.wait_ge(stored, 16)


def program(nc, I, cst, out, dbg=None, first=True):
    with ExitStack() as ctx:
        def sb(name, shape):
            return ctx.enter_context(nc.sbuf_tensor(name, shape, F32))[:]

        ps = [ctx.enter_context(nc.psum_tensor(f"bank{j}", [P, 512], F32))[:] for j in range(8)]
        xT = sb("xT", [P, KD, T])
        tables = sb("tables", [P, 6, T]).rearrange("p (a b) t -> p a b t", a=3)
        vec = sb("vec", [P, V1_COLS])
        cond = sb("cond", [P, KD, 32])
        c = {k: sb(k, [P, P]) for k in ("ident", "ones", "ones_head", "zeros")}
        c["eps"] = sb("eps", [P, 3])
        load_all(nc, [(c[k], cst[k]) for k in ("ident", "ones", "ones_head")] + [(vec, I["vec1"])])
        with nc.Block() as block:
            @block.gpsimd
            def _(pool):
                pool.memset(cond[:, :, 3:32], 0.0)

            @block.scalar
            def _(sc):
                for j, k in enumerate(("c", "c_ctx", "c_2")):
                    sc.activation(cond[:, :, j], vec[:, V1[k][0]:V1[k][1]], ACT.Silu)

            @block.vector
            def _(ve):
                ve.memset(c["zeros"], 0.0)
                for j, e in enumerate((EPS, RET_EPS, RWKV_EPS)):
                    ve.memset(c["eps"][:, j:j + 1], e)
        if first:
            with Stage(nc, "hidden") as st:
                ring = st.sb("ring", [P, RING_COLS])
                first_block(nc, c, ps, ring, I, cst, vec, cond, xT, st.sb("hT", [P, KD, 2 * T]),
                            tables)
        else:
            turn_features(nc, c, ps, [I["x"]], [xT])
        with Stage(nc, "hidden") as st:
            ring = st.sb("ring", [P, RING2_COLS])
            hT = st.sb("hT", [P, KD, T])
            second_block(nc, c, ps, ring, I, cst, vec, cond, xT, hT, tables, dbg)
        store(nc, c, ps, xT, out)


def kernel(**inputs):
    import concourse.bacc as bacc
    from concourse.bass_utils import run_bass_kernel_spmd

    data = host_layout({k: np.asarray(a) for k, a in inputs.items()})
    tables = shape_tables()
    nc = bacc.Bacc("TRN2", target_bir_lowering=False, num_devices=1)
    arrays, ins, consts = {}, {}, {}
    for group, prefix, aps in ((data, "in_", ins), (tables, "table_", consts)):
        for name, a in group.items():
            arrays[prefix + name] = a
            aps[name] = nc.dram_tensor(prefix + name, a.shape, mybir.dt.from_np(a.dtype), kind="ExternalInput").ap()
    out = nc.dram_tensor("out", (T, D), F32, kind="ExternalOutput").ap()
    program(nc, ins, consts, out)
    result = run_bass_kernel_spmd(nc, [arrays], core_ids=[0])
    return result.results[0]["out"].reshape(1, T, D)
```

```python
from contextlib import ExitStack

import numpy as np

import concourse.bass as bass
from concourse import mybir

P = 128
D = 1024
KD = D // P
T = 256
NT = T // P
HEAD = 64
E = 16
CAP = 2 * T // E
FF_E = 2 * D
KE = FF_E // P
D_FF = 2816
KF = D_FF // P
RWKV_COLS = 1152
EPS = 1e-6
RET_EPS = 1e-5
RWKV_EPS = 64e-5
PI = 3.14159265358979
RING_COLS = 24576

F32 = mybir.dt.float32
I32 = mybir.dt.int32
ALU = mybir.AluOpType
ACT = mybir.ActivationFunctionType
AX = mybir.AxisListType
MUL, ADD, SUB, MAX = ALU.mult, ALU.add, ALU.subtract, ALU.max


def shape_tables():
    f = np.float32
    out = {}
    p = np.arange(P)
    ident = np.eye(P)
    out["ident"] = ident
    out["ones"] = np.ones((P, P))
    out["ones_head"] = (p[:, None] // HEAD == p[None, :] // HEAD) * 1.0
    out["swap_pair"] = ident[p ^ 1]
    out["swap_head"] = ident[p ^ HEAD]
    out["swap_half"] = ident[p ^ 32]
    swap_mla = np.zeros((P, P))
    for a in range(32):
        swap_mla[64 + a, 64 + (a ^ 16)] = 1
    out["swap_mla"] = swap_mla
    swap_kpe = np.zeros((P, P))
    swap_kpe[:32, :32] = swap_mla[64:96, 64:96]
    out["swap_kpe"] = swap_kpe
    out["ones_but_first"] = np.ones((P, P)) * (p[:, None] > 0)

    tok = np.arange(T)
    inv = 10000.0 ** (-np.arange(0, 32, 2) / 32)
    ang = np.concatenate([(tok // 64)[:, None] * inv, (tok % 64)[:, None] * inv], 1)
    of_pair = (p % HEAD) // 2
    out["axial_cos"] = np.cos(ang)[:, of_pair].T
    out["axial_sin"] = np.sin(ang)[:, of_pair].T * np.where(p % 2, 1.0, -1.0)[:, None]

    rot = np.zeros((P, 6))
    rot[:, 0] = 10000.0 ** (-2 * (p % 32) / 64)
    rot[:, 1] = np.where(p % 64 < 32, -1, 1)
    pe = p - 64
    rot[64:96, 2] = 10000.0 ** (-2 * (pe[64:96] % 16) / 32)
    rot[64:96, 3] = np.where(pe[64:96] < 16, -1, 1)
    rot[:32, 4] = rot[64:96, 2]
    rot[:32, 5] = rot[64:96, 3]
    out["rot_freq"] = rot

    t = tok / (T - 1)
    bands = np.linspace(1e-4, 15, 16)
    fa = 2 * np.pi / T * tok[:, None] * bands[None, :]
    feats = np.zeros((P, T))
    feats[:33] = np.concatenate([t[:, None], np.cos(fa), -np.sin(fa)], 1).T
    out["hy_feats"] = feats
    deltas = np.abs(np.linspace(np.log(1e-2) / 1.5, np.log(1e-2) / 0.3, 256))
    win = np.exp(-t[:, None] * deltas[None, :])
    out["hy_window"] = win.reshape(2, P, 256).transpose(1, 0, 2)
    n2 = 2 * T
    tau = np.concatenate([tok, (n2 - tok) % n2])
    keep = np.ones(n2)
    keep[T] = 0
    fr = np.arange(T)
    th = 2 * np.pi * ((tau[:, None] * fr[None, :]) % n2) / n2
    alt = np.where(tau % 2, -1.0, 1.0)
    cc = np.cos(th[:, :P]).copy()
    cc[:, 0] = alt
    fd = np.concatenate([np.cos(th), -np.sin(th), cc], 1) * keep[:, None]
    out["dft_filter"] = fd.reshape(4, P, 640).transpose(1, 0, 2)
    th = 2 * np.pi * ((tok[:, None] * fr[None, :]) % n2) / n2
    alt = np.where(tok % 2, -1.0, 1.0)
    im = -np.sin(th)
    im[:, 0] = alt
    out["dft_signal"] = np.concatenate([np.cos(th), im], 1).reshape(2, P, 512).transpose(1, 0, 2)
    gre = 2 * np.cos(th.T) / n2
    gre[0] /= 2
    gim = -2 * np.sin(th.T) / n2
    gim[0] = alt / n2
    out["dft_inverse"] = np.concatenate([gre, gim], 0).reshape(4, P, T).transpose(1, 0, 2)

    w = np.arange(64)
    tw = 2 * np.pi * ((w[:, None] * w[None, :]) % 64) / 64
    bd = lambda m: np.kron(np.eye(2), m)
    out["fn_channel"] = np.concatenate([bd(np.cos(tw)), bd(np.sin(tw))], 1)
    tn = 2 * np.pi * ((tok[:, None] * tok[None, :]) % T) / T
    out["fn_token"] = (np.concatenate([np.cos(tn), -np.sin(tn)], 1) / 128).reshape(2, P, 512).transpose(1, 0, 2)

    s_, t_ = p[:, None], p[None, :]
    lev = []
    for k in range(7):
        m = 1 << k
        lev.append(((s_ // m) % 2 == 0) & (t_ // m == s_ // m + 1))
    lev.append(lev[0] & False)
    out["level_fwd"] = np.stack(lev, 1)
    out["level_bwd"] = np.stack([x.T for x in lev], 1)
    out["tri"] = np.stack([s_ < t_, s_ > t_, s_ <= t_, s_ > t_], 1)
    ds = np.arange(T)[None, :] - np.arange(T)[:, None]
    out["ahead"] = np.maximum(ds, 0).reshape(2, P, T).transpose(1, 0, 2)
    out["behind"] = np.maximum(-ds, 0).reshape(2, P, T).transpose(1, 0, 2)
    out["slots"] = np.broadcast_to(np.arange(1, CAP + 1), (P, CAP))
    for name, parts in PACKS.items():
        out[name] = np.concatenate([out.pop(k).reshape(P, -1) for k in parts], 1)
    return {k: np.ascontiguousarray(v, dtype=f) for k, v in out.items()}


PACKS = dict(
    mixer_consts=dict(tri=(4, P), level_fwd=(8, P), level_bwd=(8, P), ahead=(NT, T), behind=(NT, T),
                      swap_half=(P,), swap_mla=(P,), swap_kpe=(P,)),
    branch_consts=dict(axial_cos=(T,), axial_sin=(T,), swap_pair=(P,), swap_head=(P,), dft_signal=(NT, 512),
                       dft_inverse=(4, T), fn_channel=(2 * P,), fn_token=(NT, 512)))


def pack_cols(name):
    return sum(int(np.prod(shape)) for shape in PACKS[name].values())


def unpack(buffer, name):
    at, out = 0, {}
    for k, shape in PACKS[name].items():
        n = int(np.prod(shape))
        a = buffer[:, at:at + n]
        out[k] = a.rearrange("p (a b) -> p a b", b=shape[1]) if len(shape) == 2 else a
        at += n
    return out



def blocks(w):
    *lead, k, n = w.shape
    w = w.reshape(*lead, k // P, P, n // P, P)
    nl = len(lead)
    w = w.transpose(*range(nl), nl + 1, nl + 2, nl, nl + 3)
    return w.reshape(*lead, P, (n // P) * (k // P) * P)


def panels(w, blk):
    *lead, k, n = w.shape
    b = blocks(w).reshape(*lead, P, -1, blk * P)
    nl = len(lead)
    return np.ascontiguousarray(b.transpose(*range(nl), nl + 1, nl, nl + 2))


def wide_tiles(w, width):
    *lead, k, n = w.shape
    nl = len(lead)
    w = w.reshape(*lead, k // (2 * P), 2, P, n // width, width)
    w = w.transpose(*range(nl), nl + 3, nl, nl + 2, nl + 1, nl + 4)
    return w.reshape(*lead, -1, P, 2 * width)


def column(v):
    v = np.asarray(v).reshape(-1)
    if v.size < P:
        v = np.concatenate([v, v])
    return v.reshape(-1, P).T


def interleave(a, b):
    *lead, k, n = a.shape
    return np.stack([a.reshape(*lead, k, n // P, P), b.reshape(*lead, k, n // P, P)], -2).reshape(*lead, k, 2 * n)


VEC1 = dict(c=8, c_ctx=8, b_mod=48, norm1=8, norm2=8, q_gain=1, k_gain=1, short_w=18, short_b=6,
            f_b1=1, f_b2=1, f_freq=1, hy_bias=4, final_g=8, c_2=8, final_2=8)
VEC2 = dict(b_ada=72, mu=9, w0=4, a0=4, k_k=2, k_a=2, r_k=2, ln_g=2, ln_b=2, mla_q_g=3, mla_kv_g=2,
            gn_g=2, log_rate=8)
SMALL1 = dict(f_w1=64, f_w2=64, f_w3=1024, router=128)
SMALL2 = dict(w_up=256, a_up=256, g_up=256, w_uq=2304, w_ukv=2048)


def fields(widths):
    at, out = 0, {}
    for k, n in widths.items():
        out[k] = (at, at + n)
        at += n
    return out, at


def host_layout(i):
    def pad(a):
        return np.concatenate([a, np.zeros((P - a.shape[0],) + a.shape[1:], a.dtype)], 0)

    rows = lambda a: a.reshape(-1, P, a.shape[-1]).transpose(1, 0, 2).reshape(P, -1)
    o = {}
    o["x"], o["ctx"] = i["x"][0], i["ctx"][0]
    w = i["w_in"][0]
    o["w_kv"] = panels(w[:, 512:768], 16)
    o["w_in"] = panels(np.concatenate([w[:, :512], w[:, 768:]], 1), 16)
    o["w_mod"] = wide_tiles(i["w_mod"][0], 1536)
    wb = i["w_branch"][0]
    o["w_branch"] = panels(wb, 16)
    o["w_out"] = panels(i["w_out"][0], 16)
    up = np.stack([i["w_gate"][0].reshape(E, KD, P, FF_E), i["w_up"][0].reshape(E, KD, P, FF_E)], 3)
    down = i["w_down"][0].reshape(E, 4, 4, P, D).transpose(0, 2, 3, 1, 4)
    o["w_expert"] = np.concatenate([up.reshape(E, KD, P, 4 * D), down.reshape(E, 4, P, 4 * D)], 1)
    o["vec1"] = np.concatenate([
        column(i["c"]), column(i["c_ctx"]), column(i["b_mod"]), column(i["norm1_g"]), column(i["norm2_g"]),
        column(i["q_gain"]), column(i["k_gain"]), column(i["hy_short_w"]), column(i["hy_short_b"]),
        column(i["hy_f_b1"]), column(i["hy_f_b2"]), column(i["hy_f_freq"]), column(i["hy_bias"]),
        column(i["final_g"]), column(i["c_2"]), column(i["final_norm_g_2"])], 1)
    o["small1"] = np.concatenate([pad(i["hy_f_w1"][0]), pad(i["hy_f_w2"][0]), pad(i["hy_f_w3"][0]),
                                  rows(i["w_router"][0])], 1)
    o["positions"] = np.broadcast_to(i["positions_2"].reshape(1, T), (P, T))
    o["w_ada"] = wide_tiles(i["w_ada_2"], 1024)
    for n in "12":
        wi = i[f"w_ff{n}_in_2"]
        o[f"w_ff{n}"] = np.concatenate([panels(interleave(wi[..., :D_FF], wi[..., D_FF:]), 16),
                                        panels(i[f"w_ff{n}_out_2"], 16)], 1)
    wi = i["w_in_2"]
    kpe = RWKV_COLS + 640
    gap = np.zeros(wi.shape[:2] + (P - 32,), wi.dtype)
    o["w_in_2"] = panels(np.concatenate([wi[..., :kpe], wi[..., kpe + 32:], wi[..., kpe:kpe + 32], gap,
                                         np.zeros(wi.shape[:2] + (P,), wi.dtype)], 2), 16)
    o["w_out_2"] = panels(i["w_out_2"], 16)
    o["vec2"] = np.stack([np.concatenate([
        column(i["b_ada_2"][l]), column(i["rwkv_mu_2"][l]), column(i["rwkv_w0_2"][l]), column(i["rwkv_a0_2"][l]),
        column(i["rwkv_k_k_2"][l]), column(i["rwkv_k_a_2"][l]), column(i["rwkv_r_k_2"][l]),
        column(i["rwkv_ln_g_2"][l]), column(i["rwkv_ln_b_2"][l]), column(i["mla_q_norm_g_2"][l]),
        column(i["mla_kv_norm_g_2"][l]), column(i["ret_gn_g_2"][l]),
        np.broadcast_to(i["ret_log_rate_2"][l].reshape(1, 8), (P, 8))], 1) for l in range(2)])
    o["small2"] = np.stack([np.concatenate([
        i["rwkv_w_up_2"][l].reshape(P, 256), i["rwkv_a_up_2"][l].reshape(P, 256), i["rwkv_g_up_2"][l],
        rows(i["mla_w_uq_2"][l]), rows(i["mla_w_ukv_2"][l])], 1) for l in range(2)])
    return {k: np.ascontiguousarray(v) for k, v in o.items()}


class Stage:

    count = 0

    def __init__(self, nc, name):
        Stage.count += 1
        self.nc, self.name = nc, f"{name}_{Stage.count}"

    def __enter__(self):
        self.stack, self.sems = ExitStack(), []
        return self

    def sb(self, name, shape, dt=F32):
        return self.stack.enter_context(self.nc.sbuf_tensor(f"{self.name}_{name}", shape, dt))[:]

    def sem(self, name):
        self.sems.append(self.stack.enter_context(self.nc.semaphore(f"{self.name}_{name}")))
        return self.sems[-1]

    def block(self):
        return self.nc.Block()

    def __exit__(self, kind, value, trace):
        if kind is None and self.sems:
            with self.nc.Block() as block:
                @block.gpsimd
                def _(pool):
                    for s in self.sems:
                        pool.sem_clear(s)
        self.stack.close()


class Arena:

    def __init__(self, ring, cols):
        self.ring, self.at, self.cols = ring, 0, cols

    def take(self, *dims, rows=P):
        n = 1
        for d in dims:
            n *= d
        a = self.ring[0:rows, self.at:self.at + n]
        self.at += n
        assert self.at <= self.cols
        if len(dims) == 1:
            return a
        names = "abcd"[:len(dims)]
        return a.rearrange(f"p ({' '.join(names)}) -> p {' '.join(names)}", **dict(zip(names[1:], dims[1:])))


class Chain:

    def __init__(self, eng, sem):
        self.eng, self.sem, self.n = eng, sem, 0

    def __call__(self, ins):
        self.n += 1
        ins.then_inc(self.sem, 1)
        self.eng.wait_ge(self.sem, self.n)


def norm_gain(nc, c, ps, x, gain, early):
    with Stage(nc, "norm") as st:
        sq = st.sb("sq", [P, KD, T])
        root = st.sb("root", [P, T])
        rstd = st.sb("rstd", [P, T])
        squared, summed, rooted, inverted = (st.sem(n) for n in ("squared", "summed", "rooted", "inverted"))
        with st.block() as block:
            @block.sync
            def _(sp):
                for slot, src, sem in early:
                    sp.dma_start(slot, src).then_inc(sem, 16)

            @block.scalar
            def _(sc):
                for k in range(KD):
                    sc.activation(sq[:, k], x[:, k], ACT.Square).then_inc(squared, 1)
                sc.wait_ge(summed, 1)
                sc.activation(root, ps[0][:, 0:T], ACT.Sqrt, bias=c["eps"][:, 0:1], scale=1.0 / D)\
                    .then_inc(rooted, 1)

            @block.tensor
            def _(pe):
                for k in range(KD):
                    pe.wait_ge(squared, k + 1)
                    mm = pe.matmul(ps[0][:, 0:T], c["ones"], sq[:, k], start=k == 0, stop=k == KD - 1)
                mm.then_inc(summed, 1)

            @block.vector
            def _(ve):
                ve.wait_ge(rooted, 1)
                ve.reciprocal(rstd, root).then_inc(inverted, 1)
                ve.wait_ge(inverted, 1)
                for k in range(KD):
                    ve.scalar_tensor_tensor(x[:, k], x[:, k], gain[:, k:k + 1], rstd, MUL, MUL)


def attention(nc, c, ps, ar, q_of, k_of, v_of, out_of, n_heads, n_keys):
    kt = n_keys // P
    with Stage(nc, "attention") as st:
        prob = ar.take(4, n_keys)
        probT = ar.take(2, kt, T)
        low = st.sb("low", [P, 4])
        tot = st.sb("tot", [P, 4])
        inv = st.sb("inv", [P, 4])
        scored, lowest, exped, inverted, scaled, turned, copied, mixed, stored = (st.sem(n) for n in (
            "scored", "lowest", "exped", "inverted", "scaled", "turned", "copied", "mixed", "stored"))
        units = [(h, t) for h in range(n_heads) for t in range(NT)]
        with st.block() as block:
            @block.tensor
            def _(pe):
                def scores(u):
                    h, t = units[u]
                    if u >= 4:
                        pe.wait_ge(exped, u - 3)
                    pe.matmul(ps[u % 4][:, 0:n_keys], q_of(h, t), k_of(h), start=True, stop=True).then_inc(scored, 1)

                def turn(u):
                    pe.wait_ge(scaled, u + 1)
                    if u >= 2:
                        pe.wait_ge(copied, u - 1)
                    for j in range(kt):
                        mm = pe.transpose(ps[4 + u % 2][:, j * P:(j + 1) * P], prob[:, u % 4, j * P:(j + 1) * P],
                                          c["ident"][:, :])
                    mm.then_inc(turned, 1)

                def mix(h):
                    pe.wait_ge(copied, 2 * h + 2)
                    if h >= 2:
                        pe.wait_ge(stored, h - 1)
                    o = out_of(h)
                    for j in range(kt):
                        mm = pe.matmul(ps[6 + h % 2][o[0]:o[0] + HEAD, 0:T], v_of(h, j), probT[:, h % 2, j],
                                       start=j == 0, stop=j == kt - 1)
                    mm.then_inc(mixed, 1)

                for u in range(len(units) + 3):
                    if u < len(units):
                        scores(u)
                    if 2 <= u < len(units) + 2:
                        turn(u - 2)
                    if u >= 4 and u % 2 == 0:
                        mix(u // 2 - 2)

            @block.vector
            def _(ve):
                def head(u):
                    ve.wait_ge(scored, u + 1)
                    if u >= 4:
                        ve.wait_ge(exped, u - 3)
                    ve.tensor_reduce(low[:, u % 4:u % 4 + 1], ps[u % 4][:, 0:n_keys], AX.X, MAX,
                                     negate=True).then_inc(lowest, 1)

                def tail(u):
                    ve.wait_ge(exped, u + 1)
                    ve.reciprocal(inv[:, u % 4:u % 4 + 1], tot[:, u % 4:u % 4 + 1]).then_inc(inverted, 1)
                    ve.wait_ge(inverted, u + 1)
                    ve.tensor_scalar(prob[:, u % 4], prob[:, u % 4], inv[:, u % 4:u % 4 + 1], None,
                                     MUL).then_inc(scaled, 1)

                for u in range(len(units) + 1):
                    if u < len(units):
                        head(u)
                    if u >= 1:
                        tail(u - 1)

            @block.scalar
            def _(sc):
                def turn_out(u):
                    h, t = units[u]
                    sc.wait_ge(turned, u + 1)
                    if u >= 4:
                        sc.wait_ge(mixed, h - 1)
                    sc.activation(probT[:, h % 2, :, t * P:(t + 1) * P],
                                  ps[4 + u % 2][:, 0:n_keys].rearrange("p (j n) -> p j n", n=P),
                                  ACT.Copy).then_inc(copied, 1)

                def store(h):
                    sc.wait_ge(mixed, h + 1)
                    o = out_of(h)
                    sc.activation(o[1], ps[6 + h % 2][o[0]:o[0] + HEAD, 0:T], ACT.Copy).then_inc(stored, 1)

                for u in range(len(units) + 4):
                    if u < len(units):
                        sc.wait_ge(lowest, u + 1)
                        if u >= 4:
                            sc.wait_ge(turned, u - 3)
                        sc.activation(prob[:, u % 4], ps[u % 4][:, 0:n_keys], ACT.Exp, bias=low[:, u % 4:u % 4 + 1],
                                      accum_out=tot[:, u % 4:u % 4 + 1]).then_inc(exped, 1)
                    if 2 <= u < len(units) + 2:
                        turn_out(u - 2)
                    if u >= 5 and u % 2 == 1:
                        store((u - 5) // 2)


def sine(ve, link, out, x, tmp, quarter):
    magic = 12582912.0
    link(ve.tensor_scalar(tmp, x, 1.0 / (2 * PI), 0.25 if quarter else 0.0, MUL, ADD))
    link(ve.tensor_scalar(tmp, tmp, magic, None, ADD))
    link(ve.tensor_scalar(tmp, tmp, magic, None, SUB))
    link(ve.scalar_tensor_tensor(out, tmp, -6.28125, x, MUL, ADD))
    link(ve.scalar_tensor_tensor(out, tmp, -0.0019350051879882812, out, MUL, ADD))
    link(ve.scalar_tensor_tensor(out, tmp, -3.0199159819567e-07, out, MUL, ADD))
    if quarter:
        link(ve.tensor_scalar(out, out, PI / 2, None, ADD))
    link(ve.tensor_scalar(out, out, 3.1415925, -3.1415925, ALU.min, MAX))


class LongConv:

    def __init__(self, sems, c, ps, bufs, cst, spec, n, z, bias, gate, out):
        self.c, self.ps, self.cst, self.n, self.z, self.bias, self.gate, self.out = c, ps, cst, n, z, bias, gate, out
        self.turned, self.copied, self.transformed, self.products, self.mixed, self.inverse, self.gated = sems
        self.zt, self.f1, self.f2 = bufs
        self.spec = lambda f: spec[:, f, n * T:(n + 1) * T]

    def pe_turn(self, pe):
        for t in range(NT):
            for ch in range(2):
                mm = pe.transpose(self.ps[0][:, (2 * t + ch) * P:(2 * t + ch + 1) * P],
                                  self.z[:, ch, t * P:(t + 1) * P], self.c["ident"])
        mm.then_inc(self.turned, 1)

    def pe_transform(self, pe):
        pe.wait_ge(self.copied, self.n + 1)
        for j, f in enumerate((0, 2, 1, 3)):
            for t in range(NT):
                mm = pe.matmul(self.ps[1 + f][:, 0:T], self.cst["dft_signal"][:, t, f * P:(f + 1) * P],
                               self.zt[:, t], start=t == 0, stop=t == NT - 1)
            if j % 2:
                mm.then_inc(self.transformed, 1)

    def pe_inverse(self, pe):
        pe.wait_ge(self.mixed, self.n + 1)
        for ch in range(2):
            for f in range(4):
                mm = pe.matmul(self.ps[ch][:, 0:T], self.f1[:, f, ch * P:(ch + 1) * P],
                               self.cst["dft_inverse"][:, f], start=f == 0, stop=f == 3)
            mm.then_inc(self.inverse, 1)

    def dve_copy(self, ve):
        ve.wait_ge(self.turned, self.n + 1)
        ve.tensor_copy(self.zt, self.ps[0].rearrange("p (a b) -> p a b", b=T)).then_inc(self.copied, 1)

    def dve_mix(self, ve):
        f1, f2, s, bank = self.f1, self.f2, self.spec, lambda f: self.ps[1 + f][:, 0:T]
        for f in range(2):
            ve.wait_ge(self.transformed, 2 * self.n + f + 1)
            ve.tensor_tensor(f1[:, f], bank(f), s(f), MUL)
            ve.tensor_tensor(f2[:, f], bank(2 + f), s(2 + f), MUL)
            ve.tensor_tensor(f1[:, 2 + f], bank(2 + f), s(4 if f == 0 else 1), MUL)
            ve.tensor_tensor(f2[:, 2 + f], bank(f), s(2 + f), MUL).then_inc(self.products, 1)
        ve.wait_ge(self.products, 2 * self.n + 2)
        ve.tensor_tensor(f1[:, 0:2], f1[:, 0:2], f2[:, 0:2], SUB)
        ve.tensor_tensor(f1[:, 2:4], f1[:, 2:4], f2[:, 2:4], ADD).then_inc(self.mixed, 1)

    def dve_gate(self, ve):
        for ch in range(2):
            ve.wait_ge(self.inverse, 2 * self.n + ch + 1)
            ve.scalar_tensor_tensor(self.out[:, ch], self.z[:, ch], self.bias[:, ch:ch + 1], self.ps[ch][:, 0:T],
                                    MUL, ADD).then_inc(self.gated, 1)
        for ch in range(2):
            ve.wait_ge(self.gated, 4 * self.n + ch + 1)
            ve.tensor_tensor(self.out[:, ch], self.out[:, ch], self.gate[:, ch], MUL).then_inc(self.gated, 1)


def project_in(nc, c, ps, ring, I, xT, ctxT, hT, mod, gain, proj, kv, consts, consts_src):
    with Stage(nc, "project_in") as st:
        h = hT[:, :, 0:T]
        d = Dense(nc, st, c, ring, ps, xT, h)
        d.norms[1] = (ctxT, hT[:, :, T:2 * T], ps[7])
        kv_made, consts_here = st.sem("kv_made"), st.sem("consts_here")
        slots, turns = 6, 3
        none = [0] * SLOTS
        pairs = proj.rearrange("p (q a) t -> p q (a t)", a=2)
        with st.block() as block:
            @block.sync
            def _(sp):
                for u in range(slots):
                    sp.dma_start(d.slots[u], I["w_in"][u]).then_inc(d.loaded[u], 16)
                sp.dma_start(d.slots[slots], I["w_kv"][0]).then_inc(d.loaded[slots], 16)
                sp.dma_start(consts, consts_src).then_inc(consts_here, 16)
                sp.wait_ge(consts_here, 16)
                with sp.Fori(1, turns) as i:
                    for u in range(slots):
                        sp.wait_ge(d.panel_done, i * slots + (u + 1 - slots))
                        sp.dma_start(d.slots[u], I["w_in"][i * slots + u]).then_inc(d.loaded[u], 16)

            @block.tensor
            def _(pe):
                for m in range(2):
                    for k in range(KD):
                        d.pe_sum(pe, m, k)
                with pe.Fori(0, turns) as i:
                    for u in range(slots):
                        d.pe_pair(pe, i, u, i * slots, none, 0)
                pe.wait_ge(d.loaded[slots], 16)
                pe.wait_ge(d.h_ready, 2 * KD)
                w = d.slots[slots].rearrange("p (b n) -> p b n", n=P)
                for j in range(2):
                    for k in range(KD):
                        mm = pe.matmul(ps[3 + j], w[:, j * KD + k], hT[:, k], start=k == 0, stop=k == KD - 1)
                    mm.then_inc(kv_made, 1)

            @block.scalar
            def _(sc):
                for m in range(2):
                    for k in range(KD):
                        d.act_square(sc, m, k)

                def take(q, u, func):
                    sc.wait_ge(d.panel_done, q + u + 1)
                    sc.activation(pairs[:, q + u], ps[u % 3], func).then_inc(d.bank_free, 1)

                d.act_norm(sc, 0, mod[:, 0:8, 0])
                for u in range(slots):
                    take(0, u, ACT.Copy)
                d.act_norm(sc, 1, mod[:, 0:8, 1])
                with sc.Fori(1, turns) as i:
                    for u in range(slots):
                        take(i * slots, u, ACT.Sigmoid)
                for j in range(2):
                    sc.wait_ge(kv_made, j + 1)
                    sc.activation(kv[:, j], ps[3 + j], ACT.Copy)

            @block.vector
            def _(ve):
                ve.sem_inc(d.bank_free, 2)
                d.dve_norm(ve, 0, gain[:, 0])
                d.dve_norm(ve, 1, gain[:, 1])


def project_out(nc, c, ps, I, ring, early, late, xT, h, mod, gain, proj, mix, router):
    with Stage(nc, "project_out") as st:
        d = Dense(nc, st, c, ring, ps, xT, h)
        spare = Arena(ring[:, 8 * BLK * P:], RING_COLS - 8 * BLK * P)
        merged, part = spare.take(KD, T), spare.take(2, 3, T)
        merging, router_here = st.sem("merging"), st.sem("router_here")
        panels = 4
        branch, out = (early + late)[:panels], (early + late)[panels:]
        with st.block() as block:
            @block.sync
            def _(sp):
                for slot, src, sem in late:
                    sp.dma_start(slot, src).then_inc(sem, 16)
                sp.dma_start(router, I["small1"][:, SM1["router"][0]:SM1["router"][1]]).then_inc(router_here, 16)
                sp.wait_ge(router_here, 16)

            @block.tensor
            def _(pe):
                for q in range(panels):
                    w = branch[q][0].rearrange("p (b n) -> p b n", n=P)
                    pe.wait_ge(branch[q][2], 16)
                    if q >= 2:
                        pe.wait_ge(d.bank_free, 2 + q - 1)
                    for j in range(2):
                        for b, (lo, hi) in enumerate(((0, 4), (4, 6), (6, 8))):
                            for k in range(lo, hi):
                                mm = pe.matmul(ps[5 * (q % 2) + b][:, j * T:(j + 1) * T], w[:, j * KD + k],
                                               mix[:, k], start=k == lo, stop=k == hi - 1)
                    mm.then_inc(d.panel_done, 1)
                for q in range(KD):
                    d.pe_add(pe, q, merged, KD, 0, [(slot, sem, 16) for slot, _, sem in out], 0,
                             ready=lambda k: k // 2 + 1)

            @block.scalar
            def _(sc):
                for q in range(KD):
                    d.act_added(sc, q, 0, 0)
                d.act_norm(sc, 0, mod[:, 24:32, 0])

            @block.vector
            def _(ve):
                ve.sem_inc(d.bank_free, 2)
                for q in range(panels):
                    ve.wait_ge(d.panel_done, q + 1)
                    for j in range(2):
                        n = 2 * q + j
                        for b in range(3):
                            m = ve.tensor_tensor(part[:, j, b], ps[5 * (q % 2) + b][:, j * T:(j + 1) * T],
                                                 proj[:, 12 + b * KD + n], MUL)
                        m.then_inc(merging, 1)
                        ve.wait_ge(merging, 2 * n + 1)
                        ve.tensor_tensor(part[:, j, 0], part[:, j, 0], part[:, j, 1], ADD).then_inc(merging, 1)
                        ve.wait_ge(merging, 2 * n + 2)
                        m = ve.tensor_tensor(merged[:, n], part[:, j, 0], part[:, j, 2], ADD)
                    m.then_inc(d.bank_free, 1)
                for q in range(KD):
                    d.dve_add(ve, q, 0, mod[:, 16:24, 0])
                d.dve_norm(ve, 0, gain[:, 2])


def prepare_heads(nc, c, ps, ar, cst, vec, q, kv, k_other, v_tok):
    flat = lambda a: a.rearrange("p a b -> p (a b)")
    k = kv[:, 0]
    q_gain, k_gain = (vec[:, V1[n][0]:V1[n][1]] for n in ("q_gain", "k_gain"))
    xs = [k, flat(q[:, 0:2]), flat(q[:, 2:4])]
    sq, root, turned = ar.take(3, 2 * T), ar.take(3, 2 * T), ar.take(3, 2 * T)
    with Stage(nc, "heads") as st:
        squared, summed, rooted, inverted, scaled, swapped, by_sin, by_cos, rotated, v_turned, other = (
            st.sem(n) for n in ("squared", "summed", "rooted", "inverted", "scaled", "swapped", "by_sin", "by_cos",
                                "rotated", "v_turned", "other"))
        with st.block() as block:
            @block.tensor
            def _(pe):
                for j in range(4):
                    mm = pe.transpose(ps[6][:, j * P:(j + 1) * P], kv[:, 1, j * P:(j + 1) * P], c["ident"])
                mm.then_inc(v_turned, 1)
                for g in range(3):
                    pe.wait_ge(squared, g + 1)
                    pe.matmul(ps[g], c["ones_head"], sq[:, g], start=True, stop=True).then_inc(summed, 1)
                for g, w in enumerate((T, 2 * T, 2 * T)):
                    pe.wait_ge(scaled, g + 1)
                    pe.matmul(ps[3 + g][:, 0:w], cst["swap_pair"], xs[g][:, 0:w], start=True, stop=True)\
                        .then_inc(swapped, 1)
                    if g == 1:
                        pe.wait_ge(rotated, 1)
                        pe.matmul(ps[7], cst["swap_head"], k, start=True, stop=True).then_inc(other, 1)

            @block.scalar
            def _(sc):
                for g in range(3):
                    sc.activation(sq[:, g], xs[g], ACT.Square).then_inc(squared, 1)
                for g in range(3):
                    sc.wait_ge(summed, g + 1)
                    sc.activation(root[:, g], ps[g], ACT.Sqrt, bias=c["eps"][:, 3 if g else 0:4 if g else 1],
                                  scale=1.0 if g else 1.0 / HEAD).then_inc(rooted, 1)
                sc.wait_ge(v_turned, 1)
                sc.activation(v_tok, ps[6].rearrange("p (a b) -> p a b", b=P), ACT.Copy)
                sc.wait_ge(other, 1)
                sc.activation(k_other, ps[7], ACT.Copy)

            @block.vector
            def _(ve):
                for g in range(3):
                    ve.wait_ge(rooted, g + 1)
                    ve.reciprocal(root[:, g], root[:, g]).then_inc(inverted, 1)
                    ve.wait_ge(inverted, g + 1)
                    ve.scalar_tensor_tensor(xs[g], xs[g], q_gain if g else k_gain, root[:, g], MUL, MUL)\
                        .then_inc(scaled, 1)
                for g, w in enumerate((1, 2, 2)):
                    tiles = lambda a: a[:, 0:w * T].rearrange("p (a b) -> p a b", b=T)
                    wide = lambda a: a.unsqueeze(1).broadcast_to([P, w, T])
                    ve.wait_ge(swapped, g + 1)
                    ve.tensor_tensor(tiles(turned[:, g]), tiles(ps[3 + g]), wide(cst["axial_sin"]), MUL)\
                        .then_inc(by_sin, 1)
                    ve.tensor_tensor(tiles(xs[g]), tiles(xs[g]), wide(cst["axial_cos"]), MUL).then_inc(by_cos, 1)
                    ve.wait_ge(by_sin, g + 1)
                    ve.wait_ge(by_cos, g + 1)
                    ve.tensor_tensor(tiles(xs[g]), tiles(xs[g]), tiles(turned[:, g]), ADD).then_inc(rotated, 1)


def hyena_fourier(nc, c, ps, ar, cst, vec, spec, x, fx, hy_out, fn_out, early):
    v = lambda k, j=0, n=1: vec[:, V1[k][0] + j:V1[k][0] + j + n]
    u, z = ar.take(6, T), ar.take(2, T)
    bufs = ar.take(NT, T), ar.take(4, T), ar.take(4, T)
    mid = ar.take(2, NT, 2 * P)
    with Stage(nc, "hyena") as st:
        sems = [st.sem(n) for n in ("turned", "copied", "transformed", "products", "mixed", "inverse", "gated")]
        centre, ahead, short, first, mid_out, second = (
            st.sem(n) for n in ("centre", "ahead", "short", "first", "mid_out", "second"))
        gated = sems[-1]
        conv = [LongConv(sems, c, ps, bufs, cst, spec, 0, u[:, 0:2], v("hy_bias", 0, 2), u[:, 2:4], z),
                LongConv(sems, c, ps, bufs, cst, spec, 1, z, v("hy_bias", 2, 2), u[:, 4:6], hy_out)]
        chan, token = cst["fn_channel"], cst["fn_token"]
        with st.block() as block:
            @block.sync
            def _(sp):
                for slot, src, sem in early:
                    sp.dma_start(slot, src).then_inc(sem, 16)

            @block.tensor
            def _(pe):
                for n, (ch, t) in enumerate((ch, t) for ch in range(2) for t in range(NT)):
                    if n >= 2:
                        pe.wait_ge(mid_out, n - 1)
                    pe.matmul(ps[5 + n % 2][:, 0:2 * P], fx[:, ch, t * P:(t + 1) * P], chan, start=True,
                              stop=True).then_inc(first, 1)
                pe.wait_ge(short, 2)
                conv[0].pe_turn(pe)
                conv[0].pe_transform(pe)
                pe.wait_ge(mid_out, 4)
                for ch in range(2):
                    for n, (t, part) in enumerate((t, part) for t in range(NT) for part in range(2)):
                        mm = pe.matmul(ps[5 + ch][:, 0:T], mid[:, ch, t, part * P:(part + 1) * P],
                                       token[:, t, part * T:(part + 1) * T], start=n == 0, stop=n == 3)
                    mm.then_inc(second, 1)
                conv[0].pe_inverse(pe)
                pe.wait_ge(gated, 4)
                conv[1].pe_turn(pe)
                conv[1].pe_transform(pe)
                conv[1].pe_inverse(pe)

            @block.scalar
            def _(sc):
                for n, (ch, t) in enumerate((ch, t) for ch in range(2) for t in range(NT)):
                    sc.wait_ge(first, n + 1)
                    sc.activation(mid[:, ch, t], ps[5 + n % 2][:, 0:2 * P], ACT.Copy).then_inc(mid_out, 1)
                for ch in range(2):
                    sc.wait_ge(second, ch + 1)
                    sc.activation(fn_out[:, ch], ps[5 + ch][:, 0:T], ACT.Copy)

            @block.vector
            def _(ve):
                def short_conv(n):
                    for j in (2 * n, 2 * n + 1):
                        ve.tensor_scalar(u[:, j], x[:, j], v("short_w", 6 + j), v("short_b", j), MUL, ADD)\
                            .then_inc(centre, 1)
                    for j in (2 * n, 2 * n + 1):
                        ve.wait_ge(centre, j + 1)
                        ve.scalar_tensor_tensor(u[:, j, 1:T], x[:, j, 0:T - 1], v("short_w", j), u[:, j, 1:T],
                                                MUL, ADD).then_inc(ahead, 1)
                    for j in (2 * n, 2 * n + 1):
                        ve.wait_ge(ahead, j + 1)
                        ve.scalar_tensor_tensor(u[:, j, 0:T - 1], x[:, j, 1:T], v("short_w", 12 + j),
                                                u[:, j, 0:T - 1], MUL, ADD).then_inc(short, 1)

                short_conv(0)
                conv[0].dve_copy(ve)
                short_conv(1)
                conv[0].dve_mix(ve)
                short_conv(2)
                ve.wait_ge(short, 4)
                conv[0].dve_gate(ve)
                conv[1].dve_copy(ve)
                conv[1].dve_mix(ve)
                ve.wait_ge(short, 6)
                conv[1].dve_gate(ve)


def first_branches(nc, c, ps, ring, cst, vec, spec, proj, kv, mix, early):
    scratch = lambda: Arena(ring, CONSTS_AT)
    with Stage(nc, "qkv") as st:
        k_other = st.sb("k_other", [P, 2 * T])
        v_tok = st.sb("v_tok", [P, 4, P])
        prepare_heads(nc, c, ps, scratch(), cst, vec, proj[:, 0:4], kv, k_other, v_tok)

        def q_of(h, t):
            b = h % 2 * HEAD
            return proj[b:b + HEAD, h // 2, t * P:(t + 1) * P]

        def k_of(h):
            b = h % 2 * HEAD
            return kv[b:b + HEAD, 0] if h // 4 == h % 2 else k_other[b:b + HEAD, :]

        attention(nc, c, ps, scratch(), q_of, k_of, lambda h, j: v_tok[:, j, h // 4 * HEAD:(h // 4 + 1) * HEAD],
                  lambda h: (h % 2 * HEAD, mix[h % 2 * HEAD:h % 2 * HEAD + HEAD, h // 2]), 8, 2 * T)
    behind = CONSTS_AT + pack_cols("branch_consts")
    hyena_fourier(nc, c, ps, Arena(ring[:, behind:], RING_COLS - behind), cst, vec, spec, proj[:, 4:10],
                  proj[:, 10:12], mix[:, 4:6], mix[:, 6:8], early)


def route(nc, c, ps, cst, router, hT, place_of, x_sel, slot, slot_loaded, src):
    with Stage(nc, "route") as st:
        e1 = st.sb("e1", [P, NT, E])
        top = st.sb("top", [P, NT])
        tot = st.sb("tot", [P, NT])
        aff = st.sb("aff", [P, NT, E])
        affT = st.sb("affT", [E, T])
        left = st.sb("left", [E, T])
        best = st.sb("best", [E, 8])
        mask = st.sb("mask", [E, T])
        place = st.sb("place", [E, T])
        zero = st.sb("zero", [E, T])
        placeT = st.sb("placeT", [P, NT, E])
        slots = st.sb("slots", [P, CAP])
        h_tok = st.sb("h_tok", [P, NT, D])
        sel = st.sb("sel", [P, NT, E, CAP])
        w_tok = st.sb("w_tok", [P, NT, E, 4, CAP])
        logits, highest, exped, shared, turned, chain, placed, placed_t, loaded = (
            st.sem(n) for n in ("logits", "highest", "exped", "shared", "turned", "chain", "placed", "placed_t",
                                "loaded"))
        h_turned, h_out, chosen, weighted, spread, gathered, w_turned = (
            st.sem(n) for n in ("h_turned", "h_out", "chosen", "weighted", "spread", "gathered", "w_turned"))
        x_out = [st.sem("x_out_act"), st.sem("x_out_dve")]
        p_out = [st.sem("p_out_act"), st.sem("p_out_dve")]
        gather_bank = lambda k: ps[(7, 0, 1, 2)[k % 4]]
        quads = lambda bank: bank.rearrange("p (k n) -> p k n", n=P)
        with st.block() as block:
            @block.sync
            def _(sp):
                sp.dma_start(slots, cst["slots"]).then_inc(loaded, 16)
                for u, panel in enumerate(slot):
                    sp.dma_start(panel, src[0, u]).then_inc(slot_loaded[u], 16)

            @block.tensor
            def _(pe):
                for t in range(NT):
                    for k in range(KD):
                        mm = pe.matmul(ps[0][:, t * E:(t + 1) * E], hT[:, k, t * P:(t + 1) * P],
                                       router[:, k * E:(k + 1) * E], start=k == 0, stop=k == KD - 1)
                mm.then_inc(logits, 1)
                for g in range(4):
                    for k in range(4):
                        mm = pe.transpose(ps[3 + g][:, k * P:(k + 1) * P],
                                          hT[:, g % 2 * 4 + k, g // 2 * P:(g // 2 + 1) * P], c["ident"])
                    mm.then_inc(h_turned, 1)
                pe.wait_ge(shared, 1)
                for t in range(NT):
                    mm = pe.transpose(ps[1][0:E, t * P:(t + 1) * P], aff[:, t], c["ident"])
                mm.then_inc(turned, 1)
                pe.wait_ge(placed, 1)
                for t in range(NT):
                    mm = pe.transpose(ps[2][:, t * E:(t + 1) * E], place[:, t * P:(t + 1) * P],
                                      c["ident"][0:E, 0:E])
                mm.then_inc(placed_t, 1)
                pe.wait_ge(h_out, 4)
                pe.wait_ge(chosen, NT)
                for k in range(KD):
                    if k >= 4:
                        pe.wait_ge(x_out[k % 2], (k - 4) // 2 + 1)
                    for t in range(NT):
                        mm = pe.matmul(gather_bank(k), h_tok[:, t, k * P:(k + 1) * P],
                                       sel[:, t].rearrange("p a b -> p (a b)"), start=t == 0, stop=t == NT - 1)
                    mm.then_inc(gathered, 1)
                pe.wait_ge(spread, NT)
                for g in range(E // 2):
                    if g >= 4:
                        pe.wait_ge(p_out[g % 2], (g - 4) // 2 + 1)
                    for j in range(4):
                        mm = pe.transpose(ps[3 + g % 4][:, j * P:(j + 1) * P],
                                          w_tok[:, j % 2, 2 * g + j // 2].rearrange("p a b -> p (a b)"), c["ident"])
                    mm.then_inc(w_turned, 1)

            @block.scalar
            def _(sc):
                for t in range(NT):
                    sc.wait_ge(highest, NT)
                    sc.activation(e1[:, t], ps[0][:, t * E:(t + 1) * E], ACT.Exp, bias=top[:, t:t + 1],
                                  accum_out=tot[:, t:t + 1]).then_inc(exped, 1)
                for g in range(4):
                    sc.wait_ge(h_turned, g + 1)
                    sc.activation(h_tok[:, g // 2, (g % 2) * 512:(g % 2 + 1) * 512], ps[3 + g], ACT.Copy)\
                        .then_inc(h_out, 1)
                for t in range(NT):
                    sc.wait_ge(weighted, t + 1)
                    sc.activation(w_tok[:, t, :, 1:4], w_tok[:, t, :, 0:1].broadcast_to([P, E, 3, CAP]), ACT.Copy)\
                        .then_inc(spread, 1)
                for k in range(0, KD, 2):
                    sc.wait_ge(gathered, k + 1)
                    sc.activation(x_sel[:, k], gather_bank(k), ACT.Copy).then_inc(x_out[0], 1)
                for g in range(0, E // 2, 2):
                    sc.wait_ge(w_turned, g + 1)
                    sc.activation(place_of[:, 2 * g:2 * g + 2].rearrange("p g (t n) -> p (g t) n", n=P),
                                  quads(ps[3 + g % 4]), ACT.Copy).then_inc(p_out[0], 1)

            @block.vector
            def _(ve):
                link = Chain(ve, chain)
                link(ve.memset(zero, 0.0))
                ve.wait_ge(logits, 1)
                for t in range(NT):
                    ve.tensor_reduce(top[:, t:t + 1], ps[0][:, t * E:(t + 1) * E], AX.X, MAX, negate=True)\
                        .then_inc(highest, 1)
                ve.wait_ge(exped, NT)
                link(ve.reciprocal(tot, tot))
                for t in range(NT):
                    link(ve.tensor_scalar(aff[:, t], e1[:, t], tot[:, t:t + 1], None, MUL))
                ve.sem_inc(shared, 1)
                ve.wait_ge(turned, 1)
                link(ve.tensor_copy(affT, ps[1][0:E, 0:T]))
                link(ve.tensor_copy(left, ps[1][0:E, 0:T]))
                for _ in range(CAP // 8):
                    link(ve.max(best, left))
                    link(ve.match_replace(left, best, left, -1.0))
                link(ve.tensor_tensor(mask, affT, left, ALU.not_equal))
                link(ve.tensor_tensor_scan(place, mask, zero, 0.0, ADD, ADD))
                link(ve.tensor_tensor(place, place, mask, MUL))
                ve.sem_inc(placed, 1)
                ve.wait_ge(placed_t, 1)
                link(ve.tensor_copy(placeT, ps[2][:, 0:NT * E].rearrange("p (a b) -> p a b", b=E)))
                ve.wait_ge(loaded, 16)
                for t in range(NT):
                    at = placeT[:, t].unsqueeze(2).broadcast_to([P, E, CAP])
                    ve.tensor_tensor(sel[:, t], at, slots.unsqueeze(1).broadcast_to([P, E, CAP]), ALU.is_equal)\
                        .then_inc(chosen, 1)
                for t in range(NT):
                    ve.wait_ge(chosen, t + 1)
                    ve.tensor_tensor(w_tok[:, t, :, 0], sel[:, t], aff[:, t].unsqueeze(2).broadcast_to([P, E, CAP]),
                                     MUL).then_inc(weighted, 1)
                for k in range(1, KD, 2):
                    ve.wait_ge(gathered, k + 1)
                    ve.tensor_copy(x_sel[:, k], gather_bank(k)).then_inc(x_out[1], 1)
                for g in range(1, E // 2, 2):
                    ve.wait_ge(w_turned, g + 1)
                    ve.tensor_copy(place_of[:, 2 * g:2 * g + 2].rearrange("p g (t n) -> p (g t) n", n=P),
                                   quads(ps[3 + g % 4])).then_inc(p_out[1], 1)


class Rotary:

    def __init__(self, st, cst, positions, tables):
        self.cst, self.positions, self.tables = cst, positions, tables
        self.pos_i = st.sb("pos_i", [P, T], I32)
        self.pos = st.sb("pos", [P, T])
        self.freq = st.sb("freq", [P, 6])
        self.ang = st.sb("ang", [P, 3, 2, T])
        self.tmp = st.sb("tmp", [P, T])
        self.landed, self.chain, self.angles, self.sines = (
            st.sem(n) for n in ("landed", "chain", "angles", "sines"))

    def sync(self, sp):
        sp.dma_start(self.pos_i, self.positions).then_inc(self.landed, 16)
        sp.dma_start(self.freq, self.cst["rot_freq"]).then_inc(self.landed, 16)

    def vector(self, ve):
        link = Chain(ve, self.chain)
        ve.wait_ge(self.landed, 32)
        link(ve.tensor_copy(self.pos, self.pos_i))
        for j in range(3):
            link(ve.tensor_scalar(self.ang[:, j, 0], self.pos, self.freq[:, 2 * j:2 * j + 1], None, MUL))
            sine(ve, link, self.ang[:, j, 1], self.ang[:, j, 0], self.tmp, False)
            sine(ve, link, self.tables[:, j, 0], self.ang[:, j, 0], self.tmp, True)
        ve.sem_inc(self.angles, 1)
        ve.wait_ge(self.sines, 1)
        for j in range(3):
            ve.tensor_scalar(self.tables[:, j, 1], self.ang[:, j, 0], self.freq[:, 2 * j + 1:2 * j + 2], None, MUL)

    def scalar(self, sc):
        sc.wait_ge(self.angles, 1)
        for j in range(3):
            sc.activation(self.ang[:, j, 0], self.ang[:, j, 1], ACT.Sin)
            m = sc.activation(self.tables[:, j, 0], self.tables[:, j, 0], ACT.Sin)
        m.then_inc(self.sines, 1)


def experts(nc, c, ps, slot, loaded, src, x_sel, place, xT, gate, cst, positions, tables):
    up_panels, down_panels = KD, 4
    slots, n = len(slot), KD + 4
    with Stage(nc, "experts") as st:
        x_cur = st.sb("x_cur", [P, KD, CAP])
        silu = st.sb("silu", [P, 512])
        hid = st.sb("hid", [P, 512])
        hidT = st.sb("hidT", [P, 4, 4, CAP])
        y = st.sb("y", [P, D])
        rotary = Rotary(st, cst, positions, tables)
        x_ready, panel_done, silu_done, hid_done, turned, turned_out, y_low, y_high, placed, added = (
            st.sem(k) for k in ("x_ready", "panel_done", "silu_done", "hid_done", "turned", "turned_out", "y_low",
                                "y_high", "placed", "added"))
        xs = x_sel.rearrange("p k (e s) -> p k e s", s=CAP)
        quarter = [slice(g * CAP, (g + 1) * CAP) for g in range(4)]
        with st.block() as block:
            @block.sync
            def _(sp):
                rotary.sync(sp)
                for u in range(slots, n):
                    sp.wait_ge(panel_done, u + 1 - slots)
                    sp.dma_start(slot[u % slots], src[0, u]).then_inc(loaded[u % slots], 16)
                with sp.Fori(1, E) as e:
                    for u in range(n):
                        sp.wait_ge(panel_done, e * n + (u + 1 - slots))
                        sp.dma_start(slot[u % slots], src[e, u]).then_inc(loaded[u % slots], 16)

            @block.tensor
            def _(pe):
                with pe.Fori(0, E) as e:
                    pe.wait_ge(x_ready, e + 1)
                    for u in range(up_panels):
                        w = slot[u % slots].rearrange("p (b g n) -> p b g n", b=2, g=4)
                        pe.wait_ge(loaded[u % slots], e * 32 + (u // slots + 1) * 16)
                        for b in range(2):
                            for g in range(4):
                                mm = pe.matmul(ps[b][quarter[g], :], x_cur[:, u], w[:, b, g], start=u == 0,
                                               stop=u == up_panels - 1)
                        mm.then_inc(panel_done, 1)
                    pe.wait_ge(hid_done, e + 1)
                    for s in range(4):
                        mm = pe.transpose(ps[4][:, s * P:(s + 1) * P], hid[:, s * P:(s + 1) * P], c["ident"])
                    mm.then_inc(turned, 1)
                    pe.wait_ge(turned_out, e + 1)
                    for s in range(down_panels):
                        u = up_panels + s
                        w = slot[u % slots].rearrange("p (g b n) -> p g b n", g=4, b=2)
                        pe.wait_ge(loaded[u % slots], e * 32 + (u // slots + 1) * 16)
                        for b in range(2):
                            for g in range(4):
                                mm = pe.matmul(ps[2 + b][quarter[g], :], hidT[:, s, g], w[:, g, b], start=s == 0,
                                               stop=s == down_panels - 1)
                        mm.then_inc(panel_done, 1)
                    pe.wait_ge(y_low, e + 1)
                    pe.wait_ge(y_high, e + 1)
                    for half in range(2):
                        pe.wait_ge(added, e * 2 + (half + 1))
                        for j in range(4):
                            k = 4 * half + j
                            mm = pe.matmul(ps[5 + j // 2][:, (j % 2) * T:(j % 2 + 1) * T], y[:, k * P:(k + 1) * P],
                                           place[:, e], start=True, stop=True)
                        mm.then_inc(placed, 1)

            @block.scalar
            def _(sc):
                def tokens(e):
                    sc.activation(x_cur, xs[:, :, e], ACT.Copy).then_inc(x_ready, 1)

                def middle(e, more):
                    sc.wait_ge(panel_done, e * n + up_panels)
                    sc.activation(silu, ps[0], ACT.Silu).then_inc(silu_done, 1)
                    if more:
                        tokens(e + 1)
                    sc.wait_ge(turned, e + 1)
                    sc.activation(hidT.rearrange("p s g c -> p (s g c)"), ps[4], ACT.Copy).then_inc(turned_out, 1)
                    sc.wait_ge(panel_done, e * n + n)
                    sc.activation(y[:, 0:512], ps[2], ACT.Copy).then_inc(y_low, 1)

                tokens(0)
                rotary.scalar(sc)
                with sc.Fori(0, E - 1) as e:
                    middle(e, True)
                middle(E - 1, False)

            @block.vector
            def _(ve):
                ve.sem_inc(added, 1)
                rotary.vector(ve)
                with ve.Fori(0, E) as e:
                    ve.wait_ge(silu_done, e + 1)
                    ve.tensor_tensor(hid, ps[1], silu, MUL).then_inc(hid_done, 1)
                    ve.wait_ge(panel_done, e * n + n)
                    ve.tensor_copy(y[:, 512:D], ps[3]).then_inc(y_high, 1)
                    for half in range(2):
                        ve.wait_ge(placed, e * 2 + (half + 1))
                        for j in range(4):
                            k = 4 * half + j
                            m = ve.scalar_tensor_tensor(xT[:, k], ps[5 + j // 2][:, (j % 2) * T:(j % 2 + 1) * T],
                                                        gate[:, k:k + 1], xT[:, k], MUL, ADD)
                        m.then_inc(added, 1)


BLK = 16
SLOTS = 11
SIDE = 4


class Dense:

    def __init__(self, nc, st, c, ring, ps, xT, hT):
        self.c, self.ps, self.xT, self.hT = c, ps, xT, hT
        self.slots = [ring[:, u * BLK * P:(u + 1) * BLK * P] for u in range(SLOTS)]
        self.loaded = [st.sem(f"loaded{u}") for u in range(SLOTS)]
        self.panel_done, self.bank_free, self.silu_done = (st.sem(n) for n in ("panel_done", "bank_free", "silu_done"))
        self.chunk_done, self.x_updated, self.squared = (st.sem(n) for n in ("chunk_done", "x_updated", "squared"))
        self.summed, self.rooted, self.inverted = (st.sem(n) for n in ("summed", "rooted", "inverted"))
        self.scaled, self.h_ready = st.sem("scaled"), st.sem("h_ready")
        self.sq = st.sb("sq", [P, 4, T])
        self.root = st.sb("root", [P, T])
        self.rstd = st.sb("rstd", [P, T])
        self.silu = st.sb("silu", [P, 3, T])
        self.norms = {}

    def norm(self, m):
        return self.norms.get(m, (self.xT, self.hT, self.ps[6]))

    def act_square(self, sc, m, k):
        if 8 * m + k >= 4:
            sc.wait_ge(self.summed, 8 * m + k - 3)
        sc.activation(self.sq[:, k % 4], self.norm(m)[0][:, k], ACT.Square).then_inc(self.squared, 1)

    def pe_sum(self, pe, m, k):
        pe.wait_ge(self.squared, 8 * m + k + 1)
        if m and k == 0 and m not in self.norms:
            pe.wait_ge(self.rooted, m)
        pe.matmul(self.norm(m)[2][:, 0:T], self.c["ones"], self.sq[:, k % 4], start=k == 0, stop=k == KD - 1)\
            .then_inc(self.summed, 1)

    def act_root(self, sc, m):
        sc.wait_ge(self.summed, 8 * m + 8)
        _, _, bank = self.norm(m)
        if m:
            sc.wait_ge(self.inverted, m)
        sc.activation(self.root, bank[:, 0:T], ACT.Sqrt, bias=self.c["eps"][:, 0:1], scale=1.0 / D)\
            .then_inc(self.rooted, 1)

    def act_shift(self, sc, m, shift):
        _, out, _ = self.norm(m)
        for k in range(KD):
            sc.wait_ge(self.scaled, 8 * m + k + 1)
            sc.activation(out[:, k], out[:, k], ACT.Identity, bias=shift[:, k:k + 1])\
                .then_inc(self.h_ready, 1)

    def act_norm(self, sc, m, shift):
        self.act_root(sc, m)
        self.act_shift(sc, m, shift)

    def dve_invert(self, ve, m):
        ve.wait_ge(self.rooted, m + 1)
        ve.reciprocal(self.rstd, self.root).then_inc(self.inverted, 1)

    def dve_scale(self, ve, m, gain):
        ve.wait_ge(self.inverted, m + 1)
        x, out, _ = self.norm(m)
        for k in range(KD):
            ve.scalar_tensor_tensor(out[:, k], x[:, k], gain[:, k:k + 1], self.rstd, MUL, MUL)\
                .then_inc(self.scaled, 1)

    def dve_norm(self, ve, m, gain):
        self.dve_invert(ve, m)
        self.dve_scale(ve, m, gain)

    def pe_pair(self, pe, i, u, q, loads, m):
        w = self.slots[u].rearrange("p (b n) -> p b n", n=P)
        pe.wait_ge(self.loaded[u], i * 16 + 16 * (loads[u] + 1))
        pe.wait_ge(self.bank_free, q + u + 1)
        for j in range(2):
            for k in range(KD):
                if u == 0 and j == 0:
                    pe.wait_ge(self.h_ready, 8 * m + k + 1)
                mm = pe.matmul(self.ps[u % 3][:, j * T:(j + 1) * T], w[:, j * KD + k], self.hT[:, k],
                               start=k == 0, stop=k == KD - 1)
        mm.then_inc(self.panel_done, 1)

    def act_gate(self, sc, u, q):
        sc.wait_ge(self.panel_done, q + u + 1)
        sc.activation(self.silu[:, u % 3], self.ps[u % 3][:, 0:T], ACT.Silu).then_inc(self.silu_done, 1)

    def dve_gate(self, ve, u, q, hid):
        ve.wait_ge(self.silu_done, q + u + 1)
        ve.tensor_tensor(hid[:, q + u], self.ps[u % 3][:, T:2 * T], self.silu[:, u % 3], MUL)\
            .then_inc(self.bank_free, 1)

    def panels(self, first, n, loads):
        return [(self.slots[u], self.loaded[u], 16 * (loads[u] + 1)) for u in range(first, first + n)]

    def pe_add(self, pe, q, x, nk, n, panels, m=None, ready=None):
        if n + q >= 2:
            pe.wait_ge(self.x_updated, n + q - 1)
        for k in range(nk):
            b = q * nk + k
            panel, loaded, count = panels[b // BLK]
            if ready and q == 0:
                pe.wait_ge(self.bank_free, ready(k) + 2)
            if b % BLK == 0:
                pe.wait_ge(loaded, count)
            w = panel[:, b % BLK * P:(b % BLK + 1) * P]
            mm = pe.matmul(self.ps[3 + q % 2][:, 0:T], w, x[:, k], start=k == 0, stop=k == nk - 1)
        mm.then_inc(self.chunk_done, 1)
        if m is not None and q:
            self.pe_sum(pe, m, q - 1)
        if m is not None and q == KD - 1:
            self.pe_sum(pe, m, q)

    def dve_add(self, ve, q, n, gain):
        ve.wait_ge(self.chunk_done, n + q + 1)
        ve.scalar_tensor_tensor(self.xT[:, q], self.ps[3 + q % 2][:, 0:T], gain[:, q:q + 1], self.xT[:, q],
                                MUL, ADD).then_inc(self.x_updated, 1)

    def act_added(self, sc, q, n, m):
        sc.wait_ge(self.x_updated, n + q + 1)
        self.act_square(sc, m, q)


def chunks_of(panel, nk):
    return -(-(panel + 1) * BLK // nk)


def layer_in(nc, st, c, l, ring, early_loaded, ps, xT, hT, cond, vec, small, mod, gain, proj, consts, vec_src, small_src, consts_src, w_ada, w_ff, w_in):
    d = Dense(nc, st, c, ring, ps, xT, hT)
    side = ring[:, SLOTS * BLK * P:]
    side_loaded = [st.sem(f"side_loaded{u}") for u in range(SIDE)]
    side_done, rows_out, turned, added, gained, vec_here, small_here = (
        st.sem(n) for n in ("side_done", "rows_out", "turned", "added", "gained", "vec_here", "small_here"))
    acc_step, sums_made = st.sem("acc_step"), st.sem("sums_made")
    rows = st.sb("rows", [P, 3, 2 * P])
    acc = consts[:, 0:3 * D].rearrange("p (t n) -> p t n", t=3)
    side_slots = [side[:, u * BLK * P:(u + 1) * BLK * P] for u in range(SIDE)]
    hid = proj[:, 0:KF]
    head, rest = 8, 28
    beside = [(0, 1), (2,), (3,), (4, 5), (6,), (7,), (8, 9), (10,), (11,), (), ()]
    sum_behind = {3: 0, 6: 1, 9: 2}
    turn_behind = {4: 0, 7: 1, 10: 2}
    bias = vec[:, V2["b_ada"][0]:V2["b_ada"][1]].rearrange("p (t g n) -> p t g n", g=4, n=2)
    mods = mod.rearrange("p (t g n) -> p t g n", g=4, n=2)
    before = [0] * 7 + [1] * 4
    with st.block() as block:
        @block.sync
        def _(sp):
            sp.dma_start(vec, vec_src).then_inc(vec_here, 16)
            for a in range(SIDE, head):
                sp.dma_start(d.slots[a + 3], w_ada[a]).then_inc(d.loaded[a + 3], 16)
            for p in range(3 * SLOTS):
                u = p % SLOTS
                if p >= SLOTS:
                    sp.wait_ge(d.panel_done, p - SLOTS + 1)
                elif p >= 7:
                    sp.wait_ge(side_done, p - 2)
                sp.dma_start(d.slots[u], w_ff[p]).then_inc(d.loaded[u], 16)
                for n in (*beside[u], *((24, 25, 26, 27) if p == 2 * SLOTS - 1 else ())) if p < 2 * SLOTS else ():
                    n += p // SLOTS * 12 if n < 24 else 0
                    sp.wait_ge(side_done, n + 1 if n < SIDE else head + n - SIDE + 1)
                    sp.dma_start(side_slots[n % SIDE], w_ada[head + n]).then_inc(side_loaded[n % SIDE], 16)
            for j in range(12):
                if j < 6:
                    sp.wait_ge(d.chunk_done, chunks_of(j, KF))
                else:
                    sp.wait_ge(d.panel_done, KF + j - 5)
                sp.dma_start(d.slots[j % 6], w_in[j]).then_inc(d.loaded[j % 6], 16)
                if j == 5:
                    sp.wait_ge(sums_made, rest // 4)
                    sp.dma_start(small, small_src).then_inc(small_here, 16)
                    sp.dma_start(consts, consts_src).then_inc(small_here, 16)
            sp.wait_ge(small_here, 32)

        @block.tensor
        def _(pe):
            def tile_panel(w, j, n):
                if j == 0:
                    pe.wait_ge(rows_out, n + 1)
                w = w.rearrange("p (k g n) -> p k g n", k=2, g=4)
                for k in range(2):
                    for g in range(4):
                        mm = pe.matmul(ps[5][32 * g:32 * g + 32, 0:2 * P], cond[:, 2 * j + k], w[:, k, g],
                                       start=j == 0 and k == 0, stop=j == 3 and k == 1)
                mm.then_inc(side_done, 1)

            def tile_sum(t, n):
                pe.wait_ge(rows_out, n + 1)
                pe.wait_ge(side_done, n * 4 + 4)
                for g in range(4):
                    mm = pe.matmul(ps[5][32 * g:32 * g + 32, 0:2 * P], c["ones"][:, 0:32],
                                   acc[:, t, g * 2 * P:(g + 1) * 2 * P], start=True, stop=True)
                mm.then_inc(sums_made, 1)

            def turn(t, n):
                pe.wait_ge(rows_out, n + 2)
                pe.wait_ge(added, n + 1)
                for j in range(2):
                    mm = pe.transpose(ps[7][:, j * P:(j + 1) * P], rows[:, t, j * P:(j + 1) * P], c["ident"])
                mm.then_inc(turned, 1)

            for k in range(KD):
                d.pe_sum(pe, 0, k)
            for t in range(2):
                for j in range(4):
                    a = 4 * t + j
                    if a < SIDE:
                        pe.wait_ge(early_loaded[a], l * 16 + 16)
                        tile_panel(side_slots[a], j, t)
                    else:
                        pe.wait_ge(d.loaded[a + 3], 16)
                        tile_panel(d.slots[a + 3], j, t)
                turn(t, t)
            with pe.Fori(0, 2) as i:
                for u in range(SLOTS):
                    d.pe_pair(pe, i, u, i * SLOTS, before, 0)
                    if u in sum_behind:
                        tile_sum((2 + sum_behind[u]) % 3, i * 3 + (2 + sum_behind[u]))
                    if u in turn_behind:
                        turn((2 + turn_behind[u]) % 3, i * 3 + (2 + turn_behind[u]))
            loads = [b + 2 for b in before]
            for q in range(KD):
                d.pe_add(pe, q, hid, KF, 0, d.panels(0, SLOTS, loads), 1, ready=lambda k: k + 1)
                if q == 1:
                    tile_sum(2, 8)
                if q == 2:
                    turn(2, 8)
            loads = [n + 1 for n in loads]
            with pe.Fori(0, 2) as i:
                for u in range(6):
                    d.pe_pair(pe, i, u, i * 6 + KF, loads, 1)

        @block.scalar
        def _(sc):
            sc.sem_inc(rows_out, 1)

            def tile_rows(t, n, sums, count):
                sc.wait_ge(sums, count)
                sc.wait_ge(added, n + 1)
                sc.activation(rows[:, t], ps[5][:, 0:2 * P], ACT.Copy).then_inc(rows_out, 1)

            for k in range(KD):
                d.act_square(sc, 0, k)
            d.act_root(sc, 0)
            for t in range(2):
                tile_rows(t, t, side_done, t * 4 + 4)
            d.act_shift(sc, 0, mod[:, 0:8])
            with sc.Fori(0, 2) as i:
                for u in range(SLOTS):
                    d.act_gate(sc, u, i * SLOTS)
                    if u in sum_behind:
                        tile_rows((2 + sum_behind[u]) % 3, i * 3 + (2 + sum_behind[u]), sums_made,
                                  i * 3 + (1 + sum_behind[u]))
            for q in range(KD):
                d.act_added(sc, q, 0, 1)
                if q == 1:
                    tile_rows(2, 8, sums_made, 7)
            d.act_norm(sc, 1, mod[:, 24:32])
            pairs = proj.rearrange("p (q a) t -> p q (a t)", a=2)
            with sc.Fori(0, 2) as i:
                for u in range(6):
                    sc.wait_ge(d.panel_done, i * 6 + (KF + u + 1))
                    sc.activation(pairs[:, i * 6 + u], ps[u % 3], ACT.Copy).then_inc(d.bank_free, 1)

        @block.vector
        def _(ve):
            ve.sem_inc(d.bank_free, 2)
            ve.sem_inc(added, 1)

            def tile_add(n):
                ve.wait_ge(turned, n + 1)
                sums = ps[7][:, 0:2 * P].rearrange("p (n g v) -> p g n v", n=2, g=4)
                ve.tensor_tensor(mods[:, n], sums[:, :, :, 2], bias[:, n], ADD).then_inc(added, 1)

            def side_panel(t, n, s, loads):
                j = n % 4
                w = side_slots[n % SIDE].rearrange("p (k n) -> p k n", k=2)
                ve.wait_ge(side_loaded[n % SIDE], loads)
                ve.wait_ge(side_done, s + head)
                if j == 0:
                    ve.tensor_scalar(acc[:, t], w[:, 0], cond[:, 0, 2:3], None, MUL).then_inc(acc_step, 1)
                else:
                    ve.scalar_tensor_tensor(acc[:, t], w[:, 0], cond[:, 2 * j, 2:3], acc[:, t], MUL, ADD)\
                        .then_inc(acc_step, 1)
                ve.wait_ge(acc_step, s + 1)
                ve.scalar_tensor_tensor(acc[:, t], w[:, 1], cond[:, 2 * j + 1, 2:3], acc[:, t], MUL, ADD)\
                    .then_inc(side_done, 1)

            d.dve_invert(ve, 0)
            ve.wait_ge(vec_here, 16)
            for t in range(2):
                tile_add(t)
            ve.wait_ge(added, 3)
            ve.tensor_scalar(gain[:, 0], mod[:, 8:16], 1.0, None, ADD).then_inc(gained, 1)
            ve.wait_ge(gained, 1)
            d.dve_scale(ve, 0, gain[:, 0])
            with ve.Fori(0, 2) as i:
                for u in range(SLOTS):
                    d.dve_gate(ve, u, i * SLOTS, hid)
                    for n in beside[u]:
                        side_panel((2 + n // 4) % 3, n, i * 12 + n, i * 48 + 16 * (n // SIDE + 1))
                    if u in turn_behind:
                        tile_add(i * 3 + (2 + turn_behind[u]))
            for n in range(24, rest):
                side_panel(2, n, n, 16 * (n // SIDE + 1))
            ve.tensor_scalar(gain[:, 3], mod[:, 16:24], 0.5, None, MUL).then_inc(gained, 1)
            ve.wait_ge(gained, 2)
            for q in range(KD):
                d.dve_add(ve, q, 0, gain[:, 3])
                if q == 2:
                    tile_add(8)
            ve.wait_ge(added, 10)
            for j in (1, 2):
                ve.tensor_scalar(gain[:, j], mod[:, 24 * j + 8:24 * j + 16], 1.0, None, ADD)
            ve.tensor_scalar(gain[:, 4], mod[:, 64:72], 0.5, None, MUL).then_inc(gained, 1)
            ve.wait_ge(gained, 3)
            d.dve_norm(ve, 1, gain[:, 1])


def layer_out(nc, st, c, ring, ps, xT, hT, mod, gain, mix, hid, out_slots, out_loaded, w_ff, early):
    d = Dense(nc, st, c, ring, ps, xT, hT)
    none = [0] * SLOTS
    with st.block() as block:
        @block.sync
        def _(sp):
            for u in range(SLOTS):
                sp.dma_start(d.slots[u], w_ff[u]).then_inc(d.loaded[u], 16)
            sp.wait_ge(d.chunk_done, KD)
            for slot, src, sem in early:
                sp.dma_start(slot, src).then_inc(sem, 16)
            with sp.Fori(1, 3) as i:
                for u in range(SLOTS):
                    sp.wait_ge(d.panel_done, i * SLOTS + (u + 1 - SLOTS))
                    sp.dma_start(d.slots[u], w_ff[i * SLOTS + u]).then_inc(d.loaded[u], 16)

        @block.tensor
        def _(pe):
            for q in range(KD):
                d.pe_add(pe, q, mix, KD, 0, [(slot, sem, 16) for slot, sem in zip(out_slots, out_loaded)], 0)
            with pe.Fori(0, 2) as i:
                for u in range(SLOTS):
                    d.pe_pair(pe, i, u, i * SLOTS, none, 0)
            for q in range(KD):
                d.pe_add(pe, q, hid, KF, KD, d.panels(0, SLOTS, [2] * SLOTS), ready=lambda k: k + 1)

        @block.scalar
        def _(sc):
            for q in range(KD):
                d.act_added(sc, q, 0, 0)
            d.act_norm(sc, 0, mod[:, 48:56])
            with sc.Fori(0, 2) as i:
                for u in range(SLOTS):
                    d.act_gate(sc, u, i * SLOTS)

        @block.vector
        def _(ve):
            ve.sem_inc(d.bank_free, 2)
            for q in range(KD):
                d.dve_add(ve, q, 0, mod[:, 40:48])
            d.dve_norm(ve, 0, gain[:, 2])
            with ve.Fori(0, 2) as i:
                for u in range(SLOTS):
                    d.dve_gate(ve, u, i * SLOTS, hid)
            for q in range(KD):
                d.dve_add(ve, q, KD, gain[:, 4])


class Spectrum:

    def __init__(self, st, c, ps, cst, src, vec, spec):
        self.c, self.ps, self.cst, self.src, self.vec, self.spec = c, ps, cst, src, vec, spec
        self.small = st.sb("small", [P, SM1["router"][0]])
        self.feats = st.sb("feats", [P, T])
        self.window = st.sb("window", [P, NT, T])
        self.dft = st.sb("dft", [P, 4, 640])
        self.masked = st.sb("masked", [P, P])
        self.h1 = st.sb("h1", [HEAD, T])
        self.ang = st.sb("ang", [HEAD, T])
        self.tmp = st.sb("tmp", [HEAD, T])
        self.filt = st.sb("filt", [P, NT, 2, 512])
        self.size = st.sb("size", [P, NT, 2, 512])
        self.norm = st.sb("norm", [P, 512])
        self.first_here, self.later_here, self.layer, self.angled, self.sined = (
            st.sem(n) for n in ("first_here", "later_here", "layer", "angled", "sined"))
        self.filtered, self.windowed, self.sized, self.summed = (
            st.sem(n) for n in ("filtered", "windowed", "sized", "summed"))
        self.normed, self.transformed, self.chain = (st.sem(n) for n in ("normed", "transformed", "spec_chain"))

    def weights(self, name):
        return self.small[:, SM1[name][0]:SM1[name][1]]

    def sync_first(self, sp):
        sp.dma_start(self.small, self.src).then_inc(self.first_here, 16)
        sp.dma_start(self.feats, self.cst["hy_feats"]).then_inc(self.first_here, 16)

    def sync_later(self, sp):
        for dst, name in ((self.window, "hy_window"), (self.masked, "ones_but_first"), (self.dft, "dft_filter")):
            sp.dma_start(dst, self.cst[name]).then_inc(self.later_here, 16)

    def pe_layer(self, pe, n):
        if n == 0:
            pe.wait_ge(self.first_here, 32)
            w, x = self.weights("f_w1")[0:33, :], self.feats[0:33, :]
        else:
            pe.wait_ge(self.sined, 1)
            w, x = self.weights("f_w2")[0:HEAD, :], self.h1
        pe.matmul(self.ps[n][0:HEAD, 0:T], w, x, start=True, stop=True).then_inc(self.layer, 1)

    def pe_filter(self, pe):
        pe.wait_ge(self.sined, 2)
        for t in range(NT):
            for j in range(2):
                pe.matmul(self.ps[2 + 2 * t + j], self.h1[:, t * P:(t + 1) * P],
                          self.weights("f_w3")[0:HEAD, j * 512:(j + 1) * 512], start=True, stop=True)\
                    .then_inc(self.filtered, 1)

    def pe_sizes(self, pe):
        pe.wait_ge(self.sized, 1)
        pe.wait_ge(self.later_here, 48)
        for j in range(4):
            mm = pe.matmul(self.ps[0], self.masked if j == 2 else self.c["ones"], self.size[:, j % 2, j // 2],
                           start=j == 0, stop=j == 3)
        mm.then_inc(self.summed, 1)

    def pe_transform(self, pe):
        for f in range(5):
            for j in range(4):
                mm = pe.matmul(self.ps[1 + f], self.dft[:, j, f * P:(f + 1) * P], self.filt[:, j % 2, j // 2],
                               start=j == 0, stop=j == 3)
            mm.then_inc(self.transformed, 1)

    def act_sine(self, sc, n):
        sc.wait_ge(self.angled, n + 1)
        sc.activation(self.h1, self.ang, ACT.Sin).then_inc(self.sined, 1)

    def act_size(self, sc):
        sc.wait_ge(self.windowed, 4)
        sc.activation(self.size, self.filt, ACT.Abs).then_inc(self.sized, 1)

    def dve_layer(self, ve, n):
        v = lambda k: self.vec[0:HEAD, V1[k][0]:V1[k][0] + 1]
        link = Chain(ve, self.chain)
        link.n = 8 * n
        ve.wait_ge(self.layer, n + 1)
        if n:
            ve.wait_ge(self.sined, n)
        link(ve.tensor_scalar(self.ang, self.ps[n][0:HEAD, 0:T], v(("f_b1", "f_b2")[n]), v("f_freq"), ADD, MUL))
        sine(ve, link, self.ang, self.ang, self.tmp, False)
        ve.sem_inc(self.angled, 1)

    def dve_window(self, ve):
        ve.wait_ge(self.later_here, 48)
        for t in range(NT):
            for j in range(2):
                ve.wait_ge(self.filtered, 2 * t + j + 1)
                ve.tensor_tensor(self.filt[:, t, j].rearrange("p (o c) -> p o c", o=2),
                                 self.ps[2 + 2 * t + j].rearrange("p (o c) -> p o c", o=2),
                                 self.window[:, t].unsqueeze(1).broadcast_to([P, 2, T]), MUL)\
                    .then_inc(self.windowed, 1)

    def dve_invert(self, ve):
        ve.wait_ge(self.summed, 1)
        ve.reciprocal(self.norm, self.ps[0]).then_inc(self.normed, 1)

    def dve_divide(self, ve):
        ve.wait_ge(self.normed, 1)
        for f in range(5):
            ve.wait_ge(self.transformed, f + 1)
            ve.tensor_tensor(self.spec[:, f], self.ps[1 + f], self.norm, MUL)


def front(nc, c, ps, ring, I, cst, vec, cond, xT, ctxT, rows, mod, gain, spec):
    v = lambda k: vec[:, V1[k][0]:V1[k][1]]
    n_slots, per_tile, width, tiles = 8, KD // 2, 3 * P, 4
    cols = 8 * width
    with Stage(nc, "front") as st:
        spectrum = Spectrum(st, c, ps, cst, I["small1"][:, 0:SM1["router"][0]], vec, spec)
        sums = st.sb("sums", [P, width])
        loaded = [st.sem(f"loaded{u}") for u in range(n_slots)]
        base_here, conditions, cleared = st.sem("base_here"), st.sem("conditions"), st.sem("cleared")
        landed, turned_x, copied, panel_done, sums_out, turned, added = (
            st.sem(k) for k in ("landed", "turned_x", "copied", "panel_done", "sums_out", "turned", "added"))
        slot = [ring[:, u * cols:(u + 1) * cols] for u in range(n_slots)]
        jobs = [(g, t, h) for g in range(2) for t in range(NT) for h in range(2)]
        mods = mod.rearrange("p (t g n) v -> p t g n v", g=4, n=3)
        bias = v("b_mod").rearrange("p (t g n) -> p t g n", g=4, n=3)
        with st.block() as block:
            @block.sync
            def _(sp):
                for k in ("ident", "ones", "ones_head"):
                    sp.dma_start(c[k], cst[k]).then_inc(base_here, 16)
                sp.dma_start(vec, I["vec1"]).then_inc(base_here, 16)
                spectrum.sync_first(sp)
                for g, src in enumerate((I["x"], I["ctx"])):
                    sp.dma_start(rows[:, g], src.rearrange("(t p) d -> p t d", p=P)).then_inc(landed, 16)
                spectrum.sync_later(sp)
                for u in range(n_slots):
                    sp.dma_start(slot[u], I["w_mod"][u]).then_inc(loaded[u], 16)
                for u in range(n_slots):
                    sp.wait_ge(panel_done, u + 1)
                    sp.dma_start(slot[u], I["w_mod"][n_slots + u]).then_inc(loaded[u], 16)

            @block.tensor
            def _(pe):
                def tile(t):
                    if t:
                        pe.wait_ge(sums_out, t)
                    for j in range(per_tile):
                        q = t * per_tile + j
                        w = slot[q % n_slots].rearrange("p (k g n) -> p k g n", k=2, g=4)
                        pe.wait_ge(loaded[q % n_slots], q // n_slots * 16 + 16)
                        for k in range(2):
                            for g in range(4):
                                mm = pe.matmul(ps[6][32 * g:32 * g + 32, 0:width], cond[:, 2 * j + k], w[:, k, g],
                                               start=j == 0 and k == 0, stop=j == per_tile - 1 and k == 1)
                        mm.then_inc(panel_done, 1)
                    pe.wait_ge(sums_out, t + 1)
                    if t:
                        pe.wait_ge(added, t)
                    for n in range(3):
                        mm = pe.transpose(ps[7][:, n * P:(n + 1) * P], sums[:, n * P:(n + 1) * P], c["ident"])
                    mm.then_inc(turned, 1)

                pe.wait_ge(base_here, 64)
                spectrum.pe_layer(pe, 0)
                pe.wait_ge(landed, 32)
                for n, (g, t, h) in enumerate(jobs):
                    if n >= 4:
                        pe.wait_ge(copied, n - 3)
                    for k in range(4):
                        f = (4 * h + k) * P
                        mm = pe.transpose(ps[2 + n % 4][:, k * P:(k + 1) * P], rows[:, g, t, f:f + P], c["ident"])
                    mm.then_inc(turned_x, 1)
                spectrum.pe_layer(pe, 1)
                pe.wait_ge(conditions, 1)
                pe.wait_ge(cleared, 1)
                spectrum.pe_filter(pe)
                tile(0)
                spectrum.pe_sizes(pe)
                spectrum.pe_transform(pe)
                for t in range(1, tiles):
                    tile(t)

            @block.gpsimd
            def _(pool):
                pool.memset(cond[:, :, 3:32], 0.0).then_inc(cleared, 1)

            @block.scalar
            def _(sc):
                def tile(t):
                    sc.wait_ge(panel_done, (t + 1) * per_tile)
                    if t:
                        sc.wait_ge(turned, t)
                    sc.activation(sums, ps[6][:, 0:width], ACT.Copy).then_inc(sums_out, 1)

                sc.wait_ge(base_here, 64)
                for j, k in enumerate(("c", "c_ctx", "c_2")):
                    m = sc.activation(cond[:, :, j], v(k), ACT.Silu)
                m.then_inc(conditions, 1)
                spectrum.act_sine(sc, 0)
                spectrum.act_sine(sc, 1)
                spectrum.act_size(sc)
                for t in range(tiles):
                    tile(t)

            @block.vector
            def _(ve):
                def tile(t):
                    ve.wait_ge(turned, t + 1)
                    part = ps[7][:, 0:width].rearrange("p (n g v) -> p g n v", n=3, g=4)
                    ve.tensor_tensor(mods[:, t, :, :, 0], part[:, :, :, 0], bias[:, t], ADD)
                    ve.tensor_tensor(mods[:, t, :, :, 1], part[:, :, :, 1], bias[:, t], ADD).then_inc(added, 1)

                ve.memset(c["zeros"], 0.0)
                for j, e in enumerate((EPS, RET_EPS, RWKV_EPS, HEAD * EPS)):
                    ve.memset(c["eps"][:, j:j + 1], e)
                ve.wait_ge(base_here, 64)
                spectrum.dve_layer(ve, 0)
                for n, (g, t, h) in enumerate(jobs):
                    ve.wait_ge(turned_x, n + 1)
                    ve.tensor_copy((xT, ctxT)[g][:, 4 * h:4 * h + 4, t * P:(t + 1) * P],
                                   ps[2 + n % 4].rearrange("p (k n) -> p k n", n=P)).then_inc(copied, 1)
                spectrum.dve_layer(ve, 1)
                spectrum.dve_window(ve)
                tile(0)
                spectrum.dve_invert(ve)
                spectrum.dve_divide(ve)
                for t in range(1, tiles):
                    tile(t)
                ve.wait_ge(added, tiles)
                for j in range(2):
                    ve.scalar_tensor_tensor(gain[:, j], mod[:, 8:16, j], 1.0, v("norm1"), ADD, MUL)
                ve.scalar_tensor_tensor(gain[:, 2], mod[:, 32:40, 0], 1.0, v("norm2"), ADD, MUL)


def first_block(nc, c, ps, ring, I, cst, vec, cond, xT, hT, tables):
    v = lambda k: vec[:, V1[k][0]:V1[k][1]]
    h = hT[:, :, 0:T]
    with Stage(nc, "first") as st:
        mod = st.sb("mod", [P, 48, 2])
        gain = st.sb("gain", [P, 3, KD])
        router = st.sb("router", [P, KD * E])
        with Stage(nc, "mixer") as mx:
            spec = mx.sb("spec", [P, 5, 512])
            ctxT = mx.sb("ctxT", [P, KD, T])
            front(nc, c, ps, ring, I, cst, vec, cond, xT, ctxT, hT.rearrange("p k n -> p (k n)")
                  .rearrange("p (g t d) -> p g t d", g=2, t=NT), mod, gain, spec)
            proj = mx.sb("proj", [P, 36, T])
            kv = mx.sb("kv", [P, 2, 2 * T])
            consts = ring[:, CONSTS_AT:CONSTS_AT + pack_cols("branch_consts")]
            project_in(nc, c, ps, ring, I, xT, ctxT, hT, mod, gain, proj, kv, consts, cst["branch_consts"])
            panels = [(ring[:, u * BLK * P:(u + 1) * BLK * P], I[("w_branch", "w_out")[u // 4]][u % 4],
                       mx.sem(f"loaded{u}")) for u in range(8)]
            first_branches(nc, c, ps, ring, unpack(consts, "branch_consts"), vec, spec, proj, kv, ctxT, panels[:7])
            project_out(nc, c, ps, I, ring, panels[:7], panels[7:], xT, h, mod, gain, proj, ctxT, router)
        with Stage(nc, "moe") as s2:
            place = s2.sb("place", [P, E, T])
            x_sel = s2.sb("x_sel", [P, KD, 512])
            slot = [ring[:, u * 4 * D:(u + 1) * 4 * D] for u in range(RING_COLS // (4 * D))]
            loaded = [s2.sem(f"loaded{u}") for u in range(len(slot))]
            route(nc, c, ps, cst, router, hT, place, x_sel, slot, loaded, I["w_expert"])
            experts(nc, c, ps, slot, loaded, I["w_expert"], x_sel, place, xT, mod[:, 40:48, 0], cst, I["positions"],
                    tables)


def head_sums(pe, c, bank, x):
    return pe.matmul(bank[:, 0:512], c["ones_head"], x.rearrange("p a b -> p (a b)"), start=True, stop=True)


def mixer_inputs(nc, c, ps, cst, tables, vec, small, proj, b):
    v = lambda k, j=0, n=1: vec[:, V2[k][0] + j:V2[k][0] + j + n]
    w = lambda n: small[:, SM2[n][0]:SM2[n][1]]
    w_uq = w("w_uq").rearrange("p (k n) -> p k n", k=3)
    w_ukv = w("w_ukv").rearrange("p (k n) -> p k n", k=2)
    rate = float(np.exp(-0.5))
    flat = lambda a: a.rearrange("p a b -> p (a b)")
    z, kpe = proj[:, 0:9], proj[0:32, 22]
    zs, cs, cx = b["zs"], b["cs"], b["cx"]
    r, k, vv = zs[:, 0:2], zs[:, 2:4], zs[:, 4:6]
    groups = ((9, 3, "mla_q_g"), (12, 2, "mla_kv_g"))
    with Stage(nc, "mixer_inputs") as st:
        hmu, omu, oka = st.sb("hmu", [P, 9]), st.sb("omu", [P, 9]), st.sb("oka", [P, 2])
        hb = st.sb("hb", [P, 4, NT, 2])
        l_squared, l_summed, l_rooted, l_inverted, l_scaled, l_made, l_out, l_swapped, by_sin, by_cos, turned_kpe = (
            st.sem("l_" + n) for n in ("squared", "summed", "rooted", "inverted", "scaled", "made", "out", "swapped",
                                       "by_sin", "by_cos", "turned_kpe"))
        chain, kept, shifted, up, lifted, opened, keyed, squared, gate_made, v_turned, summed, rooted, halves, exped = (
            st.sem(n) for n in ("chain", "kept", "shifted", "up", "lifted", "opened", "keyed", "squared",
                                "gate_made", "v_turned", "summed", "rooted", "halves", "exped"))
        with st.block() as block:
            @block.tensor
            def _(pe):
                def latent_swap(j, bank):
                    pe.matmul(ps[bank][0:96, 0:2 * T], cst["swap_mla"][0:96, 0:96], b["q"][:, 2 * j:2 * j + 2],
                              start=True, stop=True).then_inc(l_swapped, 1)

                def latent_head(h):
                    if h in (4, 5):
                        pe.wait_ge(by_sin, h - 3)
                    if h >= 2:
                        pe.wait_ge(l_out, 2 * (h - 2) + 1)
                    for j in range(3):
                        mm = pe.matmul(ps[h % 2][0:96, 0:T], w_uq[:, j, h * 96:(h + 1) * 96], proj[:, 9 + j],
                                       start=j == 0, stop=j == 2)
                    mm.then_inc(l_made, 1)
                    if h >= 2:
                        pe.wait_ge(l_out, 2 * (h - 2) + 2)
                    if h == 4:
                        pe.wait_ge(rooted, 1)
                    for j in range(2):
                        pe.matmul(ps[2 + h % 2][0:HEAD, 0:T], w_ukv[:, j, h * P:h * P + HEAD], proj[:, 12 + j],
                                  start=j == 0, stop=j == 1)
                    pe.matmul(ps[2 + h % 2][HEAD:96, 0:T], c["ident"][0:32, 0:32], kpe, start=True, stop=True)\
                        .then_inc(l_made, 1)

                pe.matmul(ps[7][0:32, 0:T], cst["swap_kpe"][0:32, 0:32], kpe, start=True, stop=True)\
                    .then_inc(l_swapped, 1)
                pe.wait_ge(l_squared, 1)
                for g, (at, n, _) in enumerate(groups):
                    for j in range(n):
                        mm = pe.matmul(ps[g][:, 0:T], c["ones"], b["l_sq"][:, at - 9 + j], start=j == 0,
                                       stop=j == n - 1)
                    mm.then_inc(l_summed, 1)
                pe.wait_ge(l_scaled, 5)
                pe.wait_ge(turned_kpe, 1)
                for h in range(4):
                    latent_head(h)
                pe.wait_ge(squared, 1)
                pe.wait_ge(l_out, 6)
                head_sums(pe, c, ps[2], b["sq"]).then_inc(summed, 1)
                pe.wait_ge(up, 1)
                for d in range(2):
                    rows = slice(d * HEAD, (d + 1) * HEAD)
                    for j in range(2):
                        pe.matmul(ps[4 + d][:, j * T:(j + 1) * T], w("w_up")[rows, j * P:(j + 1) * P], zs[rows, 7],
                                  start=True, stop=True)
                        mm = pe.matmul(ps[6 + d][:, j * T:(j + 1) * T], w("a_up")[rows, j * P:(j + 1) * P],
                                       zs[rows, 8], start=True, stop=True)
                mm.then_inc(lifted, 1)
                for j in range(2):
                    pe.wait_ge(l_out, 5 + 2 * j)
                    latent_swap(j, j)
                for h in range(4, 8):
                    latent_head(h)
                pe.wait_ge(l_out, 16)
                for j in (2, 3):
                    latent_swap(j, j)
                pe.wait_ge(opened, 1)
                for j in range(2):
                    mm = pe.matmul(ps[4][:, j * T:(j + 1) * T], w("g_up")[:, j * P:(j + 1) * P], zs[:, 6],
                                   start=True, stop=True)
                mm.then_inc(gate_made, 1)
                pe.wait_ge(shifted, 9)
                for n in range(NT):
                    for j in range(2):
                        mm = pe.transpose(ps[5][:, (2 * n + j) * P:(2 * n + j + 1) * P],
                                          vv[:, j, n * P:(n + 1) * P], c["ident"])
                mm.then_inc(v_turned, 1)
                for t in range(NT):
                    pe.wait_ge(l_out, 13 + 2 * t)
                    for j in range(2):
                        mm = pe.matmul(ps[t], proj[:, 12 + j, t * P:(t + 1) * P],
                                       w_ukv[:, j].rearrange("p (h n) -> p h n", n=P)[:, :, HEAD:P],
                                       start=j == 0, stop=j == 1)
                    mm.then_inc(l_made, 1)

            @block.scalar
            def _(sc):
                def latent_out(h):
                    sc.wait_ge(l_made, 2 * h + 1)
                    sc.activation(b["q"][:, h], ps[h % 2][0:96, 0:T], ACT.Copy, scale=96 ** -0.5).then_inc(l_out, 1)
                    sc.wait_ge(l_made, 2 * h + 2)
                    sc.activation(b["k"][:, h], ps[2 + h % 2][0:96, 0:T], ACT.Copy).then_inc(l_out, 1)

                sc.activation(b["l_sq"], proj[:, 9:14], ACT.Square).then_inc(l_squared, 1)
                for g, (_, n, _) in enumerate(groups):
                    sc.wait_ge(l_summed, g + 1)
                    sc.activation(b["l_root"][:, g], ps[g][:, 0:T], ACT.Sqrt, bias=c["eps"][:, 0:1],
                                  scale=1.0 / (n * P)).then_inc(l_rooted, 1)
                latent_out(0)
                latent_out(1)
                sc.wait_ge(shifted, 3)
                sc.activation(zs[:, 7], zs[:, 7], ACT.Tanh)
                sc.activation(zs[:, 6], zs[:, 6], ACT.Sigmoid).then_inc(up, 1)
                latent_out(2)
                latent_out(3)
                sc.wait_ge(keyed, 1)
                sc.activation(b["sq"], b["kk"], ACT.Square).then_inc(squared, 1)
                sc.wait_ge(summed, 1)
                sc.activation(flat(b["root"]), ps[2], ACT.Sqrt).then_inc(rooted, 1)
                sc.wait_ge(lifted, 1)
                for d in range(2):
                    for j in range(2):
                        sc.activation(b["sw"][:, 2 * d + j], ps[4 + d][:, j * T:(j + 1) * T], ACT.Sigmoid,
                                      bias=v("w0", 2 * d + j))
                        m = sc.activation(b["a"][:, 2 * d + j], ps[6 + d][:, j * T:(j + 1) * T], ACT.Sigmoid,
                                          bias=v("a0", 2 * d + j))
                m.then_inc(opened, 1)
                for h in range(4, 8):
                    latent_out(h)
                sc.wait_ge(halves, 1)
                for u in range(4):
                    for n in range(NT):
                        col = slice(n * P, (n + 1) * P)
                        plus, minus = hb[:, u, n, 0:1], hb[:, u, n, 1:2]
                        sc.activation(b["e1"][:, u, col], cx[:, u, col], ACT.Exp, bias=plus, scale=-rate)
                        sc.activation(b["e2"][:, u, col], cs[:, u, col], ACT.Exp, bias=minus, scale=rate)
                        if u < 2:
                            sc.activation(b["e3"][:, u, col], cs[:, u, col], ACT.Exp, bias=plus, scale=-rate)
                sc.activation(b["ehalf"], hb[:, :, :, 1], ACT.Exp).then_inc(exped, 1)
                sc.wait_ge(gate_made, 1)
                sc.activation(flat(b["gate"]), ps[4], ACT.Copy)
                for t in range(NT):
                    sc.wait_ge(l_made, 17 + t)
                    sc.activation(b["l_values"][:, t], ps[t], ACT.Copy).then_inc(l_out, 1)

            @block.vector
            def _(ve):
                def latent_rotate(pairs):
                    wide = lambda x: x.unsqueeze(1).broadcast_to([96, 2, T])
                    for j in pairs:
                        tiles = slice(2 * j, 2 * j + 2)
                        ve.wait_ge(l_swapped, 2 + j)
                        ve.tensor_tensor(b["turned"][:, tiles], ps[j][0:96].rearrange("p (a b) -> p a b", b=T),
                                         wide(tables[0:96, 1, 1]), MUL).then_inc(by_sin, 1)
                        ve.tensor_tensor(b["q"][:, tiles], b["q"][:, tiles], wide(tables[0:96, 1, 0]), MUL)\
                            .then_inc(by_cos, 1)
                    for j in pairs:
                        tiles = slice(2 * j, 2 * j + 2)
                        ve.wait_ge(by_sin, j + 1)
                        ve.wait_ge(by_cos, j + 1)
                        ve.tensor_tensor(b["q"][:, tiles], b["q"][:, tiles], b["turned"][:, tiles], ADD)

                link = Chain(ve, chain)
                near = b["near"]
                link(ve.tensor_scalar(hmu, v("mu", 0, 9), 0.5, None, MUL))
                link(ve.tensor_scalar(omu, v("mu", 0, 9), -1.0, 1.0, MUL, ADD))
                link(ve.tensor_scalar(oka, v("k_a", 0, 2), -1.0, 1.0, MUL, ADD))
                ve.tensor_copy(near[:, :, 0:1], z[:, :, 1:2])
                ve.tensor_copy(near[:, :, T - 1:T], z[:, :, T - 2:T - 1])
                link(ve.tensor_tensor(near[:, :, 1:T - 1], z[:, :, 0:T - 2], z[:, :, 2:T], ADD))
                ve.wait_ge(l_swapped, 1)
                link(ve.tensor_tensor(b["turned"][0:32, 0], ps[7][0:32, 0:T], tables[0:32, 2, 1], MUL))
                link(ve.tensor_tensor(kpe, kpe, tables[0:32, 2, 0], MUL))
                ve.tensor_tensor(kpe, kpe, b["turned"][0:32, 0], ADD).then_inc(turned_kpe, 1)
                for g, (at, n, gain) in enumerate(groups):
                    ve.wait_ge(l_rooted, g + 1)
                    ve.reciprocal(b["l_root"][:, g], b["l_root"][:, g]).then_inc(l_inverted, 1)
                    ve.wait_ge(l_inverted, g + 1)
                    for j in range(n):
                        ve.scalar_tensor_tensor(proj[:, at + j], proj[:, at + j], v(gain, j), b["l_root"][:, g],
                                                MUL, MUL).then_inc(l_scaled, 1)
                order = (6, 7, 8, 2, 3, 0, 1, 4, 5)
                for part in (order[0:3], order[3:9]):
                    for j in part:
                        ve.tensor_scalar(zs[:, j], z[:, j], omu[:, j:j + 1], None, MUL).then_inc(kept, 1)
                    for j in part:
                        ve.wait_ge(kept, order.index(j) + 1)
                        ve.scalar_tensor_tensor(zs[:, j], near[:, j], hmu[:, j:j + 1], zs[:, j], MUL, ADD)\
                            .then_inc(shifted, 1)
                ve.wait_ge(shifted, 9)
                for j in range(2):
                    link(ve.tensor_scalar(b["kk"][:, j], k[:, j], v("k_k", j), None, MUL))
                ve.sem_inc(keyed, 1)
                root, kk, kmod, a = b["root"], b["kk"], b["kmod"], b["a"]
                ve.wait_ge(rooted, 1)
                link(ve.tensor_scalar(root, root, 1e-12, None, MAX))
                link(ve.reciprocal(flat(root), flat(root)))
                link(ve.tensor_tensor(kk, kk, root, MUL))
                latent_rotate((0, 1))
                ve.wait_ge(opened, 1)
                for u in range(4):
                    for n in range(NT):
                        col = slice(n * P, (n + 1) * P)
                        m = ve.tensor_tensor_scan(cs[:, u, col], b["sw"][:, u, col], c["zeros"], 0.0, ADD, ADD)
                link(m)
                link(ve.tensor_copy(b["tot"], cs.rearrange("p u (n t) -> p u n t", n=NT)[:, :, :, P - 1]))
                link(ve.tensor_tensor(cx, cs, b["sw"], SUB))
                link(ve.tensor_scalar(hb[:, :, :, 0], b["tot"], rate / 2, None, MUL))
                link(ve.tensor_scalar(hb[:, :, :, 1], b["tot"], -rate / 2, None, MUL))
                ve.sem_inc(halves, 1)
                for u in range(4):
                    m = ve.tensor_scalar(kmod[:, u], a[:, u], v("k_a", u % 2), oka[:, u % 2:u % 2 + 1], MUL, ADD)
                link(m)
                for d in range(2):
                    u = slice(2 * d, 2 * d + 2)
                    ve.tensor_tensor(kmod[:, u], kmod[:, u], k, MUL)
                    m = ve.tensor_tensor(a[:, u], a[:, u], kk, MUL)
                link(m)
                latent_rotate((2, 3))
                ve.wait_ge(v_turned, 1)
                ve.tensor_copy(b["v_tok"], ps[5].rearrange("p (a b) -> p a b", b=T))
                ve.wait_ge(exped, 1)
                e1, e2, e3 = b["e1"], b["e2"], b["e3"]
                for d in range(2):
                    u = slice(2 * d, 2 * d + 2)
                    key, tilde, read = ((e1[:, u], e2[:, u], e3), (e2[:, u], e1[:, u], e2[:, u]))[d]
                    ve.tensor_tensor(b["kh"][:, u], key, kk, MUL)
                    ve.tensor_tensor(b["kt"][:, u], tilde, kmod[:, u], MUL)
                    ve.tensor_tensor(b["bt"][:, u], tilde, a[:, u], MUL)
                    ve.tensor_tensor(b["rh"][:, u], read, r, MUL)


def chunk_products(nc, c, ps, cst, tables, proj, ret_values, b):
    kinds = (("bt", "kh", "abT"), ("kt", "kh", "akT"), ("kt", "rh", "bkT"), ("bt", "rh", "bbT"))
    x = proj[:, 14:18]
    with Stage(nc, "products") as st:
        made, masked, swapped, by_sin, by_cos, v_turned, turned, copied, first_off = (
            st.sem(n) for n in ("made", "masked", "swapped", "by_sin", "by_cos", "v_turned", "turned", "copied",
                                "first_off"))
        with st.block() as block:
            @block.tensor
            def _(pe):
                for j in range(2):
                    pe.matmul(ps[j], cst["swap_half"], x[:, 2 * j:2 * j + 2], start=True, stop=True)\
                        .then_inc(swapped, 1)
                for j in range(4):
                    mm = pe.transpose(ps[2][:, j * P:(j + 1) * P], proj[:, 18 + j % 2, j // 2 * P:(j // 2 + 1) * P],
                                      c["ident"])
                mm.then_inc(v_turned, 1)
                for g in range(2):
                    for u in range(4):
                        mm = pe.transpose(ps[3 + g][:, u * P:(u + 1) * P],
                                          b[("kt", "bt")[g]][:, u, u // 2 * P:(u // 2 + 1) * P], c["ident"])
                    mm.then_inc(turned, 1)
                for g in range(4):
                    d, n = g // 2, g % 2
                    col = slice(n * P, (n + 1) * P)
                    for i, (src, dst, _) in enumerate(kinds):
                        for half in range(2):
                            rows = slice(half * HEAD, (half + 1) * HEAD)
                            if g:
                                pe.wait_ge(masked, 8 * (g - 1) + 2 * i + half + 1)
                            elif 2 * i + half < 2:
                                pe.wait_ge(by_sin, 2)
                            elif 2 * i + half < 5:
                                pe.wait_ge(copied, 3)
                            for pair in range(2):
                                mm = pe.matmul(ps[2 * i + half][:, pair * P:(pair + 1) * P],
                                               b[src][rows, 2 * d + pair, col], b[dst][rows, 2 * d + pair, col],
                                               start=True, stop=True)
                            mm.then_inc(made, 1)

            @block.scalar
            def _(sc):
                sc.wait_ge(v_turned, 1)
                sc.activation(ret_values.rearrange("p t (k n) -> p (t k) n", n=P),
                              ps[2].rearrange("p (a b) -> p a b", b=P), ACT.Copy).then_inc(copied, 1)
                for g in range(2):
                    sc.wait_ge(turned, g + 1)
                    sc.activation(b["tok"][:, g], ps[3 + g].rearrange("p (a b) -> p a b", b=2 * P), ACT.Copy)\
                        .then_inc(copied, 1)

            @block.vector
            def _(ve):
                wide = lambda a: a.unsqueeze(1).broadcast_to([P, 2, T])
                sin, cos = tables[:, 0, 1], tables[:, 0, 0]
                for j in range(2):
                    ve.wait_ge(swapped, j + 1)
                    ve.tensor_tensor(b["swapped"][:, 2 * j:2 * j + 2], ps[j].rearrange("p (a b) -> p a b", b=T),
                                     wide(sin), MUL).then_inc(by_sin, 1)
                ve.tensor_tensor(x, x, cos.unsqueeze(1).broadcast_to([P, 4, T]), MUL).then_inc(by_cos, 1)
                ve.wait_ge(by_sin, 2)
                ve.wait_ge(by_cos, 1)
                ve.tensor_tensor(x, x, b["swapped"], ADD)
                for g in range(4):
                    for i, (_, _, res) in enumerate(kinds):
                        mask = cst["tri"][:, g // 2 + (2 if i >= 2 else 0)].unsqueeze(1).broadcast_to([P, 2, P])
                        for half in range(2):
                            ve.wait_ge(made, 8 * g + 2 * i + half + 1)
                            ve.tensor_tensor(b[res][:, g, 2 * half:2 * half + 2],
                                             ps[2 * i + half][:, 0:2 * P].rearrange("p (a b) -> p a b", b=P),
                                             mask, MUL).then_inc(masked, 1)

            @block.gpsimd
            def _(pool):
                for g in range(4):
                    first = cst[("level_fwd", "level_bwd")[g // 2]][:, 0]
                    pool.wait_ge(masked, 8 * g + 2)
                    pool.tensor_tensor(b["xt"][:, g], b["abT"][:, g], first.unsqueeze(1).broadcast_to([P, 4, P]),
                                       MUL).then_inc(first_off, 1)
                    pool.wait_ge(first_off, g + 1)
                    pool.tensor_tensor(b["xt"][:, g], c["ident"].unsqueeze(1).broadcast_to([P, 4, P]),
                                       b["xt"][:, g], SUB)


def invert(nc, c, ps, cst, b, x):
    abT, xt, t1, off = b["abT"], b["xt"], b["t1"], b["off"]
    with Stage(nc, "inverse") as st:
        levels = (cst["level_fwd"], cst["level_bwd"])
        x_turned, x_made, offs, t1_made, t1_copied, made, updated = (
            st.sem(n) for n in ("x_turned", "x_made", "offs", "t1_made", "t1_copied", "made", "updated"))
        mask = lambda g, k: levels[g // 2][:, k].unsqueeze(1).broadcast_to([P, 4, P])
        bank = lambda i, j: ps[i][:, j * P:(j + 1) * P]
        quad = lambda i: ps[i].rearrange("p (a b) -> p a b", b=P)
        last = 6
        with st.block() as block:
            @block.tensor
            def _(pe):
                def first(i, g):
                    pe.wait_ge(offs, i * 4 + (g - 3))
                    pe.wait_ge(t1_copied, i * 4 + (g - 3))
                    for j in range(4):
                        mm = pe.matmul(bank(g % 2, j), off[:, g, j], x[:, g, j], start=True, stop=True)
                    mm.then_inc(t1_made, 1)

                def second(i, g, both):
                    pe.wait_ge(t1_copied, i * 4 + (g - 1))
                    pe.wait_ge(updated, i * 4 + (g - 1))
                    if both:
                        for j in range(4):
                            pe.matmul(bank(2 + g % 2, j), xt[:, g, j], t1[:, g, j], start=True, stop=True)
                    for j in range(4):
                        mm = pe.matmul(bank(4 + g % 2, j), t1[:, g, j], xt[:, g, j], start=True, stop=True)
                    mm.then_inc(made, 1)

                def level(i, both):
                    first(i, 0)
                    for g in range(1, 4):
                        first(i, g)
                        second(i, g - 1, both)
                    second(i, 3, both)

                for g in range(4):
                    if g >= 2:
                        pe.wait_ge(x_made, g - 1)
                    for j in range(4):
                        mm = pe.transpose(bank(6 + g % 2, j), xt[:, g, j], c["ident"])
                    mm.then_inc(x_turned, 1)
                pe.wait_ge(x_made, 4)
                with pe.Fori(1, last) as i:
                    level(i, True)
                level(last, False)

            @block.scalar
            def _(sc):
                for g in range(4):
                    sc.wait_ge(x_turned, g + 1)
                    sc.activation(x[:, g], quad(6 + g % 2), ACT.Copy).then_inc(x_made, 1)
                sc.sem_inc(t1_copied, 2)
                with sc.Fori(1, last + 1) as i:
                    for g in range(4):
                        sc.wait_ge(t1_made, i * 4 + (g - 3))
                        sc.activation(t1[:, g], quad(g % 2), ACT.Copy).then_inc(t1_copied, 1)

            @block.vector
            def _(ve):
                for g in range(4):
                    ve.tensor_tensor(off[:, g], abT[:, g], mask(g, 1), MUL).then_inc(offs, 1)
                ve.sem_inc(updated, 4)
                with ve.Fori(1, last) as i:
                    for g in range(4):
                        ve.wait_ge(made, i * 4 + (g - 3))
                        ve.tensor_tensor(x[:, g], x[:, g], quad(2 + g % 2), SUB)
                        ve.tensor_tensor(xt[:, g], xt[:, g], quad(4 + g % 2), SUB).then_inc(updated, 1)
                        ve.tensor_tensor(off[:, g], abT[:, g], mask(g, i + 1), MUL).then_inc(offs, 1)
                for g in range(4):
                    ve.wait_ge(made, last * 4 + g - 3)
                    ve.tensor_tensor(xt[:, g], xt[:, g], quad(4 + g % 2), SUB).then_inc(updated, 1)


def read_out(nc, c, ps, cst, vec, proj, ret_values, b, y, ret_y):
    v = lambda k: vec[:, V2[k][0]:V2[k][1]]
    xt, v_tok, tok, kh, rh = b["xt"], b["v_tok"], b["tok"], b["kh"], b["rh"]
    rhs, neg_p, ehalf = b["rhs"], b["neg_p"], b["ehalf"]
    decay, score, lg = b["decay"], b["score"], b["lg"]
    with Stage(nc, "read_out") as st:
        state = st.sb("state", [P, 2, 2, HEAD])
        told, copied, solved, negated, carried, scaled, read = (
            st.sem(n) for n in ("told", "copied", "solved", "negated", "carried", "scaled", "read"))
        rated, signed, spread, decayed, scored, weighted, mixed, ret_out = (
            st.sem(n) for n in ("rated", "signed", "spread", "decayed", "scored", "weighted", "mixed", "ret_out"))
        head = lambda half, pair: slice((2 * pair + half) * HEAD, (2 * pair + half + 1) * HEAD)
        rows_of = lambda half: slice(half * HEAD, (half + 1) * HEAD)
        order = [(0, 0), (1, 1), (0, 1), (1, 0)]
        with st.block() as block:
            @block.tensor
            def _(pe):
                def ret_score(h):
                    rows = rows_of(h % 2)
                    if h:
                        pe.wait_ge(weighted, h)
                    for t in range(NT):
                        mm = pe.matmul(ps[7][:, t * T:(t + 1) * T], proj[rows, 16 + h // 2, t * P:(t + 1) * P],
                                       proj[rows, 14 + h // 2], start=True, stop=True)
                    mm.then_inc(scored, 1)

                def ret_mix(h):
                    pe.wait_ge(weighted, h + 1)
                    for t in range(NT):
                        mm = pe.matmul(ps[3 + h // 2][rows_of(h % 2), T:2 * T], ret_values[:, t, h * HEAD:(h + 1) * HEAD],
                                       score[:, h, t], start=t == 0, stop=t == NT - 1)
                    mm.then_inc(mixed, 1)

                for s, (d, n) in enumerate(order):
                    g = 2 * d + n
                    col = slice(n * P, (n + 1) * P)
                    if s >= 2:
                        pe.wait_ge(scaled, 2 * d + 2)
                    for half in range(2):
                        for pair in range(2):
                            o = ps[half][:, pair * HEAD:(pair + 1) * HEAD]
                            if s and pair == 0:
                                pe.wait_ge(copied, 2 * (s - 1) + half + 1)
                            mm = pe.matmul(o, b["akT"][:, g, 2 * half + pair], v_tok[:, n, head(half, pair)],
                                           start=True, stop=s < 2)
                            if s >= 2:
                                mm = pe.matmul(o, kh[rows_of(half), 2 * d + pair, col],
                                               state[rows_of(half), d, pair], start=False, stop=True)
                        mm.then_inc(told, 1)
                    ret_score(s)
                    pe.wait_ge(copied, 2 * s + 2)
                    if s:
                        pe.wait_ge(negated, s)
                    for j in range(4):
                        mm = pe.matmul(ps[2][:, j * HEAD:(j + 1) * HEAD], xt[:, g, j], rhs[:, g, j],
                                       start=True, stop=True)
                    mm.then_inc(solved, 1)
                    if s < 2:
                        pe.wait_ge(negated, s + 1)
                        for half in range(2):
                            for pair in range(2):
                                ch = slice(pair * P + half * HEAD, pair * P + half * HEAD + HEAD)
                                o = ps[3 + d][rows_of(half), pair * HEAD:(pair + 1) * HEAD]
                                pe.matmul(o, tok[:, 0, d, ch], v_tok[:, n, head(half, pair)], start=True, stop=False)
                                mm = pe.matmul(o, tok[:, 1, d, ch], neg_p[:, g, 2 * half + pair],
                                               start=False, stop=True)
                        mm.then_inc(carried, 1)
                for h in range(4):
                    pe.wait_ge(scaled, 4)
                    ret_mix(h)
                pe.wait_ge(negated, 4)
                for n in range(NT):
                    col = slice(n * P, (n + 1) * P)
                    for half in range(2):
                        for pair in range(2):
                            o = ps[5 + n][rows_of(half), pair * P:(pair + 1) * P]
                            for d in range(2):
                                g, j = 2 * d + n, 2 * half + pair
                                pe.matmul(o, v_tok[:, n, head(half, pair)], b["bkT"][:, g, j],
                                          start=d == 0, stop=False)
                                pe.matmul(o, neg_p[:, g, j], b["bbT"][:, g, j], start=False, stop=False)
                            d = 1 - n
                            mm = pe.matmul(o, state[rows_of(half), d, pair], rh[rows_of(half), 2 * d + pair, col],
                                           start=False, stop=True)
                    mm.then_inc(read, 1)

            @block.scalar
            def _(sc):
                sc.activation(lg, v("log_rate"), ACT.Exp).then_inc(rated, 1)
                for s, (d, n) in enumerate(order):
                    for half in range(2):
                        sc.wait_ge(told, 2 * s + half + 1)
                        sc.activation(rhs[:, 2 * d + n, 2 * half:2 * half + 2],
                                      ps[half][:, 0:P].rearrange("p (a b) -> p a b", b=HEAD),
                                      ACT.Copy).then_inc(copied, 1)
                    sc.wait_ge(spread, 2 * s + 2)
                    sc.activation(decay[:, s], decay[:, s], ACT.Exp).then_inc(decayed, 1)
                for j in range(2):
                    sc.wait_ge(mixed, 2 * j + 2)
                    sc.activation(ret_y[:, j], ps[3 + j][:, T:2 * T], ACT.Copy)

            @block.vector
            def _(ve):
                ve.wait_ge(rated, 1)
                ve.tensor_scalar(lg, lg, -1.0, None, MUL).then_inc(signed, 1)
                ve.wait_ge(signed, 1)

                def ret_spread(h):
                    ve.tensor_scalar(decay[:, h], cst["ahead"], lg[:, h:h + 1], None, MUL).then_inc(spread, 1)
                    ve.wait_ge(spread, 2 * h + 1)
                    ve.scalar_tensor_tensor(decay[:, h], cst["behind"], lg[:, 4 + h:5 + h], decay[:, h], MUL, ADD)\
                        .then_inc(spread, 1)

                ret_spread(0)
                for s, (d, n) in enumerate(order):
                    ve.wait_ge(solved, s + 1)
                    ve.tensor_scalar(neg_p[:, 2 * d + n], ps[2][:, 0:T].rearrange("p (a b) -> p a b", b=HEAD),
                                     -1.0, None, MUL).then_inc(negated, 1)
                    if s < 3:
                        ret_spread(s + 1)
                    if s < 2:
                        ve.wait_ge(carried, s + 1)
                        for pair in range(2):
                            u = 2 * d + pair
                            ve.tensor_scalar(state[:, d, pair], ps[3 + d][:, pair * HEAD:(pair + 1) * HEAD],
                                             ehalf[:, u, 0:1], ehalf[:, u, 1:2], MUL, MUL).then_inc(scaled, 1)
                    ve.wait_ge(decayed, s + 1)
                    ve.wait_ge(scored, s + 1)
                    ve.scalar_tensor_tensor(score[:, s], ps[7].rearrange("p (a b) -> p a b", b=T), HEAD ** -0.5,
                                            decay[:, s], MUL, MUL).then_inc(weighted, 1)
                for n in range(NT):
                    ve.wait_ge(read, n + 1)
                    ve.tensor_copy(y[:, :, n * P:(n + 1) * P],
                                   ps[5 + n][:, 0:2 * P].rearrange("p (a b) -> p a b", b=P))


def finish(nc, c, ps, vec, proj, b, y, ret_y, rwkv_out, ret_out, slots, loaded, w_out):
    v = lambda k, j=0, n=1: vec[:, V2[k][0] + j:V2[k][0] + j + n]
    flat = lambda a: a.rearrange("p a b -> p (a b)")
    r, k, vv = (b["zs"][:, 2 * j:2 * j + 2] for j in range(3))
    prod, sq, root = b["prod"], b["n_sq"], b["n_root"]
    xs, gates = (y, ret_y), proj[:, 20:22]
    with Stage(nc, "finish") as st:
        meaned, centred, squared, summed, rooted, multiplied, bonus_summed, opened, chain = (
            st.sem(n) for n in ("meaned", "centred", "squared", "summed", "rooted", "multiplied", "bonus_summed",
                                "opened", "chain"))
        with st.block() as block:
            @block.sync
            def _(sp):
                for j, (slot, sem) in enumerate(zip(slots, loaded)):
                    sp.dma_start(slot, w_out[j]).then_inc(sem, 16)

            @block.tensor
            def _(pe):
                for m in range(2):
                    head_sums(pe, c, ps[m], xs[m]).then_inc(meaned, 1)
                pe.wait_ge(multiplied, 2)
                head_sums(pe, c, ps[4], prod).then_inc(bonus_summed, 1)
                for m in range(2):
                    pe.wait_ge(squared, m + 1)
                    head_sums(pe, c, ps[2 + m], sq[:, m]).then_inc(summed, 1)

            @block.scalar
            def _(sc):
                sc.activation(gates, gates, ACT.Silu).then_inc(opened, 1)
                for m in range(2):
                    sc.wait_ge(centred, m + 1)
                    sc.activation(sq[:, m], xs[m], ACT.Square).then_inc(squared, 1)
                for m in range(2):
                    sc.wait_ge(summed, m + 1)
                    sc.activation(flat(root[:, m]), ps[2 + m], ACT.Sqrt, bias=c["eps"][:, 2 - m:3 - m],
                                  scale=1.0 / HEAD).then_inc(rooted, 1)

            @block.vector
            def _(ve):
                link = Chain(ve, chain)
                for m in range(2):
                    ve.wait_ge(meaned, m + 1)
                    ve.scalar_tensor_tensor(flat(xs[m]), ps[m], -1.0 / HEAD, flat(xs[m]), MUL, ADD)\
                        .then_inc(centred, 1)
                for j in range(2):
                    ve.scalar_tensor_tensor(prod[:, j], r[:, j], v("r_k", j), k[:, j], MUL, MUL)\
                        .then_inc(multiplied, 1)
                ve.wait_ge(bonus_summed, 1)
                link(ve.tensor_tensor(prod, ps[4].rearrange("p (a b) -> p a b", b=T), vv, MUL))
                for m in range(2):
                    ve.wait_ge(rooted, m + 1)
                    link(ve.reciprocal(flat(root[:, m]), flat(root[:, m])))
                    link(ve.tensor_tensor(xs[m], xs[m], root[:, m], MUL))
                    for j in range(2):
                        if m:
                            last = ve.tensor_scalar(ret_y[:, j], ret_y[:, j], v("gn_g", j), None, MUL)
                        else:
                            last = ve.tensor_scalar(y[:, j], y[:, j], v("ln_g", j), v("ln_b", j), MUL, ADD)
                    link(last)
                    if m:
                        ve.wait_ge(opened, 1)
                        ve.tensor_tensor(ret_out, ret_y, gates, MUL)
                    else:
                        link(ve.tensor_tensor(prod, prod, y, ADD))
                        ve.tensor_tensor(rwkv_out, prod, b["gate"], MUL)


def mixers(nc, c, ps, ring, cst, proj, tables, vec, small, mix, slots, loaded, w_out):
    with Stage(nc, "mixers") as st:
        ar = Arena(ring, MIX_COLS)
        b = {n: ar.take(k, T) for n, k in dict(zs=9, sw=4, a=4, kh=4, kt=4, bt=4, rh=4, v_tok=2).items()}
        b["gate"] = st.sb("gate", [P, 2, T])
        b["tot"], b["ehalf"] = st.sb("tot", [P, 4, NT]), st.sb("ehalf", [P, 4, NT])
        mark = ar.at
        b.update({n: ar.take(k, T) for n, k in dict(kk=2, sq=2, root=2, cs=4, cx=4, kmod=4).items()})
        near_at = ar.at
        b.update({n: ar.take(k, T) for n, k in dict(e1=4, e2=4, e3=2).items()})
        b["near"] = ring[:, near_at:near_at + 9 * T].rearrange("p (a b) -> p a b", b=T)
        b["q"], b["k"] = ar.take(8, T, rows=96), ar.take(8, T, rows=96)
        b["l_values"] = ar.take(NT, 512)
        b["turned"] = ar.take(8, T, rows=96)
        b["l_sq"], b["l_root"] = ar.take(5, T), ar.take(2, T)
        mixer_inputs(nc, c, ps, cst, tables, vec, small, proj, b)
        ar.at = mark
        attention(nc, c, ps, ar, lambda h, t: b["q"][:, h, t * P:(t + 1) * P], lambda h: b["k"][:, h],
                  lambda h, j: b["l_values"][:, j, h * HEAD:(h + 1) * HEAD],
                  lambda h: (h % 2 * HEAD, mix[h % 2 * HEAD:h % 2 * HEAD + HEAD, 2 + h // 2]), 8, T)
        ar.at = mark
        b["tok"] = ar.take(2, 2, 2 * P)
        b.update({n: ar.take(4, 4, P) for n in ("abT", "akT", "bkT", "bbT", "xt", "t1")})
        b["swapped"] = b["t1"].rearrange("p a b c -> p (a b c)").rearrange("p (a b) -> p a b", b=T)[:, 0:4]
        ret_values = ar.take(NT, T)
        chunk_products(nc, c, ps, cst, tables, proj, ret_values, b)
        b["off"] = ring[:, 9 * T:17 * T].rearrange("p (a b c) -> p a b c", a=4, b=4)
        invert(nc, c, ps, cst, b, st.sb("x", [P, 4, 4, P]))
        b["rhs"], b["neg_p"] = ar.take(4, 4, HEAD), ar.take(4, 4, HEAD)
        b["decay"] = b["abT"].rearrange("p a b c -> p a (b c)").rearrange("p a (t n) -> p a t n", t=NT)
        b["score"] = b["t1"].rearrange("p a b c -> p a (b c)").rearrange("p a (t n) -> p a t n", t=NT)
        b["lg"] = st.sb("lg", [P, 8])
        y, ret_y = b["zs"][:, 6:8], st.sb("ret_y", [P, 2, T])
        read_out(nc, c, ps, cst, vec, proj, ret_values, b, y, ret_y)
        ar.at = 4 * BLK * P
        b.update(dict(prod=ar.take(2, T), n_sq=ar.take(2, 2 * T).rearrange("p m (a b) -> p m a b", a=2),
                      n_root=ar.take(2, 2 * T).rearrange("p m (a b) -> p m a b", a=2)))
        finish(nc, c, ps, vec, proj, b, y, ret_y, mix[:, 0:2], mix[:, 6:8], slots, loaded, w_out)


def second_block(nc, c, ps, ring, I, cst, vec1, cond, xT, hT, tables):
    side = [ring[:, at:at + BLK * P] for at in range(SLOTS * BLK * P, RING2_COLS, BLK * P)]
    with Stage(nc, "between") as bt:
        early_loaded = [bt.sem(f"early_loaded{u}") for u in range(SIDE)]
        early = lambda l: [(side[u], I["w_ada"][l, u], early_loaded[u]) for u in range(SIDE)]
        norm_gain(nc, c, ps, xT, vec1[:, V1["final_g"][0]:V1["final_g"][1]], early(0))
        layers(nc, c, ps, ring, side, early_loaded, early, I, cst, cond, xT, hT, tables)
        with bt.block() as block:
            @block.sync
            def _(sp):
                for sem in early_loaded:
                    sp.wait_ge(sem, 48)


def layers(nc, c, ps, ring, side, early_loaded, early, I, cst, cond, xT, hT, tables):
    small = ring[:, MIX_COLS:]
    with nc.Fori(0, 2) as l, Stage(nc, "layer") as ly:
        vec = ly.sb("vec", [P, V2_COLS])
        mod = ly.sb("mod", [P, 72])
        gain = ly.sb("gain", [P, 5, KD])
        proj = ly.sb("proj", [P, 24, T])
        mix = ly.sb("mix", [P, 8, T])
        consts = ly.sb("consts", [P, pack_cols("mixer_consts")])
        out_panels = side, [ly.sem(f"out_loaded{u}") for u in range(SIDE)]
        with Stage(nc, "layer_in") as st:
            layer_in(nc, st, c, l, ring, early_loaded, ps, xT, hT, cond, vec, small, mod, gain, proj, consts, I["vec2"][l],
                     I["small2"][l], cst["mixer_consts"], I["w_ada"][l], I["w_ff1"][l], I["w_in_2"][l])
        mixers(nc, c, ps, ring, unpack(consts, "mixer_consts"), proj, tables, vec, small, mix, *out_panels, I["w_out_2"][l])
        with Stage(nc, "layer_out") as st:
            layer_out(nc, st, c, ring, ps, xT, hT, mod, gain, mix, proj[:, 0:KF], *out_panels, I["w_ff2"][l],
                      early(1 - l))


V1, V1_COLS = fields(VEC1)
V2, V2_COLS = fields(VEC2)
SM1, SM1_COLS = fields(SMALL1)
SM2, SM2_COLS = fields(SMALL2)
CONSTS_AT = 7 * BLK * P
RING2_COLS = (SLOTS + SIDE) * BLK * P
MIX_COLS = RING2_COLS - SM2_COLS


def norm_and_store(nc, c, ps, x, gain, out):
    with Stage(nc, "store") as st:
        sq, root, rstd = st.sb("sq", [P, KD, T]), st.sb("root", [P, T]), st.sb("rstd", [P, T])
        rows = st.sb("rows", [P, NT, 2, 512])
        squared, summed, rooted, inverted, scaled, turned, by_act, by_dve, stored = (
            st.sem(n) for n in ("squared", "summed", "rooted", "inverted", "scaled", "turned", "by_act", "by_dve",
                                "stored"))
        outs = out.rearrange("(t p) (h d) -> p t h d", p=P, h=2)
        bank = lambda t, h: ps[1 + 2 * h + t]
        with st.block() as block:
            @block.scalar
            def _(sc):
                for k in range(KD):
                    sc.activation(sq[:, k], x[:, k], ACT.Square).then_inc(squared, 1)
                sc.wait_ge(summed, 1)
                sc.activation(root, ps[0][:, 0:T], ACT.Sqrt, bias=c["eps"][:, 0:1], scale=1.0 / D)\
                    .then_inc(rooted, 1)
                for n, (h, t) in enumerate(((0, 0), (0, 1), (1, 0))):
                    sc.wait_ge(turned, n + 1)
                    sc.activation(rows[:, t, h], bank(t, h), ACT.Copy).then_inc(by_act, 1)

            @block.tensor
            def _(pe):
                for k in range(KD):
                    pe.wait_ge(squared, k + 1)
                    mm = pe.matmul(ps[0][:, 0:T], c["ones"], sq[:, k], start=k == 0, stop=k == KD - 1)
                mm.then_inc(summed, 1)
                for k in range(KD):
                    pe.wait_ge(scaled, k + 1)
                    for t in range(NT):
                        mm = pe.transpose(bank(t, k // 4)[:, k % 4 * P:(k % 4 + 1) * P], x[:, k, t * P:(t + 1) * P],
                                          c["ident"])
                        if k % 4 == 3:
                            mm.then_inc(turned, 1)

            @block.vector
            def _(ve):
                ve.wait_ge(rooted, 1)
                ve.reciprocal(rstd, root).then_inc(inverted, 1)
                ve.wait_ge(inverted, 1)
                for k in range(KD):
                    ve.scalar_tensor_tensor(x[:, k], x[:, k], gain[:, k:k + 1], rstd, MUL, MUL).then_inc(scaled, 1)
                ve.wait_ge(turned, 4)
                ve.tensor_copy(rows[:, 1, 1], bank(1, 1)).then_inc(by_dve, 1)

            @block.sync
            def _(sp):
                for n, (h, t) in enumerate(((0, 0), (0, 1), (1, 0))):
                    sp.wait_ge(by_act, n + 1)
                    sp.dma_start(outs[:, t, h], rows[:, t, h]).then_inc(stored, 16)
                sp.wait_ge(by_dve, 1)
                sp.dma_start(outs[:, 1, 1], rows[:, 1, 1]).then_inc(stored, 16)
                sp.wait_ge(stored, 64)


def program(nc, I, cst, out):
    with ExitStack() as ctx:
        def sb(name, shape):
            return ctx.enter_context(nc.sbuf_tensor(name, shape, F32))[:]

        ps = [ctx.enter_context(nc.psum_tensor(f"bank{j}", [P, 512], F32))[:] for j in range(8)]
        xT = sb("xT", [P, KD, T])
        tables = sb("tables", [P, 6, T]).rearrange("p (a b) t -> p a b t", a=3)
        vec = sb("vec", [P, V1_COLS])
        cond = sb("cond", [P, KD, 32])
        c = {k: sb(k, [P, P]) for k in ("ident", "ones", "ones_head", "zeros")}
        c["eps"] = sb("eps", [P, 4])
        with Stage(nc, "hidden") as st:
            ring = st.sb("ring", [P, RING_COLS])
            first_block(nc, c, ps, ring, I, cst, vec, cond, xT, st.sb("hT", [P, KD, 2 * T]), tables)
        with Stage(nc, "hidden") as st:
            ring = st.sb("ring", [P, RING2_COLS])
            hT = st.sb("hT", [P, KD, T])
            second_block(nc, c, ps, ring, I, cst, vec, cond, xT, hT, tables)
        norm_and_store(nc, c, ps, xT, vec[:, V1["final_2"][0]:V1["final_2"][1]], out)


def kernel(**inputs):
    import concourse.bacc as bacc
    from concourse.bass_utils import run_bass_kernel_spmd

    data = host_layout({k: np.asarray(a) for k, a in inputs.items()})
    tables = shape_tables()
    nc = bacc.Bacc("TRN2", target_bir_lowering=False, num_devices=1)
    arrays, ins, consts = {}, {}, {}
    for group, prefix, aps in ((data, "in_", ins), (tables, "table_", consts)):
        for name, a in group.items():
            arrays[prefix + name] = a
            aps[name] = nc.dram_tensor(prefix + name, a.shape, mybir.dt.from_np(a.dtype), kind="ExternalInput").ap()
    out = nc.dram_tensor("out", (T, D), F32, kind="ExternalOutput").ap()
    program(nc, ins, consts, out)
    result = run_bass_kernel_spmd(nc, [arrays], core_ids=[0])
    return result.results[0]["out"].reshape(1, T, D)
```
